# Optimizing a Trainium2 kernel written in Bass

```python
import jax, jax.numpy as jnp
from jax import lax
import numpy as np
import math

D_MODEL = 1024
BATCH = 1
SEQ = 256
DEPTH = 2

N_A_LAYERS = DEPTH // 2
N_B_LAYERS = DEPTH - N_A_LAYERS
POOL_WINDOWS = (2, 4, 8, 16)
N_POOL_GROUPS = len(POOL_WINDOWS)
POOL_GROUP = D_MODEL // N_POOL_GROUPS
HEAD_DIM = 128
N_HEADS = D_MODEL // HEAD_DIM
MOBA_BLOCK = 256
MOBA_TOPK = 3
Q_CHUNK = 64
D_FF = ((8 * D_MODEL // 3 + 255) // 256) * 256
ROPE_THETA = 10000.0
EPS = 1e-6
N_SUBLAYERS = 3
N_MOD = 3 * N_SUBLAYERS
MACARON_WEIGHT = 0.5


def rms_norm(x, g):
    xf = x.astype(jnp.float32)
    y = xf * lax.rsqrt(jnp.mean(xf * xf, axis=-1, keepdims=True) + EPS)
    return (y * g.astype(jnp.float32)).astype(x.dtype)

def modulate(h, shift, scale):
    return h * (1.0 + scale[:, None, :]) + shift[:, None, :]

def swiglu(h, w_in, w_out):
    gu = h @ w_in
    g, u = jnp.split(gu, 2, axis=-1)
    return (jax.nn.silu(g) * u) @ w_out

def rope_tables(T):
    pos = jnp.arange(T, dtype=jnp.float32)
    inv = ROPE_THETA ** (-jnp.arange(0, HEAD_DIM, 2, dtype=jnp.float32) / HEAD_DIM)
    ang = pos[:, None] * inv[None, :]
    return jnp.cos(ang), jnp.sin(ang)

def rope(x, cos, sin):
    half = HEAD_DIM // 2
    xf = x.astype(jnp.float32)
    x1, x2 = xf[..., :half], xf[..., half:]
    c = cos[None, :, None, :]
    s = sin[None, :, None, :]
    return jnp.concatenate([x1 * c - x2 * s, x2 * c + x1 * s], axis=-1).astype(x.dtype)

def pool_mixer(h, w_pool, pool_scale):
    B, T, _ = h.shape
    hg = h.astype(jnp.float32).reshape(B, T, N_POOL_GROUPS, POOL_GROUP)
    cs = jnp.cumsum(hg, axis=1)
    t = jnp.arange(T)
    outs = []
    for gi, w in enumerate(POOL_WINDOWS):
        c_g = cs[:, :, gi]
        prev = jnp.pad(c_g, ((0, 0), (w, 0), (0, 0)))[:, :T]
        cnt = jnp.minimum(t + 1, w).astype(jnp.float32)[None, :, None]
        outs.append((c_g - prev) / cnt - hg[:, :, gi])
    pooled = jnp.stack(outs, axis=2).astype(h.dtype)
    y = jnp.einsum('btgc,gcd->btgd', pooled, w_pool).reshape(B, T, D_MODEL)
    return y * pool_scale

def shared_kv(h, c_silu, kv_norm, kv_ada_w, kv_ada_b, w_kv, k_norm, cos, sin):
    B, T, _ = h.shape
    shift, scale = jnp.split(c_silu @ kv_ada_w + kv_ada_b, 2, axis=-1)
    hn = modulate(rms_norm(h, kv_norm), shift, scale)
    k, v = jnp.split(hn @ w_kv, 2, axis=-1)
    k = rope(rms_norm(k.reshape(B, T, N_HEADS, HEAD_DIM), k_norm), cos, sin)
    v = v.reshape(B, T, N_HEADS, HEAD_DIM)
    nb = -(-T // MOBA_BLOCK)
    pad = nb * MOBA_BLOCK - T
    k = jnp.pad(k.transpose(0, 2, 1, 3), ((0, 0), (0, 0), (0, pad), (0, 0)))
    v = jnp.pad(v.transpose(0, 2, 1, 3), ((0, 0), (0, 0), (0, pad), (0, 0)))
    k_blocks = k.reshape(B, N_HEADS, nb, MOBA_BLOCK, HEAD_DIM)
    v_blocks = v.reshape(B, N_HEADS, nb, MOBA_BLOCK, HEAD_DIM)
    k_mean = jnp.mean(k_blocks.astype(jnp.float32), axis=3).astype(k.dtype)
    return k_blocks, v_blocks, k_mean

def moba_attention(q, k_blocks, v_blocks, k_mean):
    B, H, T, _ = q.shape
    nb = k_blocks.shape[2]
    topk = min(MOBA_TOPK, nb)
    n_chunks = T // Q_CHUNK
    bi = jnp.arange(B)[:, None, None, None]
    hi = jnp.arange(H)[None, :, None, None]
    sm_scale = HEAD_DIM ** -0.5

    def chunk(ci):
        q0 = ci * Q_CHUNK
        qc = lax.dynamic_slice_in_dim(q, q0, Q_CHUNK, axis=2)
        n = q0 // MOBA_BLOCK
        gate = jnp.einsum('bhqd,bhnd->bhqn', qc, k_mean).astype(jnp.float32)
        gate = jnp.where(jnp.arange(nb) < n, gate, -jnp.inf)
        _, idx = lax.top_k(gate, topk)
        valid = jnp.arange(topk) < n
        k_sel = k_blocks[bi, hi, idx]
        v_sel = v_blocks[bi, hi, idx]
        s_sel = jnp.einsum('bhqd,bhqkjd->bhqkj', qc, k_sel).astype(jnp.float32) * sm_scale
        s_sel = jnp.where(valid[:, None], s_sel, -jnp.inf).reshape(B, H, Q_CHUNK, topk * MOBA_BLOCK)
        k_own = lax.dynamic_index_in_dim(k_blocks, n, axis=2, keepdims=False)
        v_own = lax.dynamic_index_in_dim(v_blocks, n, axis=2, keepdims=False)
        s_own = jnp.einsum('bhqd,bhkd->bhqk', qc, k_own).astype(jnp.float32) * sm_scale
        qpos = q0 + jnp.arange(Q_CHUNK)
        kpos = n * MOBA_BLOCK + jnp.arange(MOBA_BLOCK)
        s_own = jnp.where(kpos[None, :] <= qpos[:, None], s_own, -jnp.inf)
        p = jax.nn.softmax(jnp.concatenate([s_sel, s_own], axis=-1), axis=-1).astype(v_blocks.dtype)
        p_sel = p[..., :topk * MOBA_BLOCK].reshape(B, H, Q_CHUNK, topk, MOBA_BLOCK)
        p_own = p[..., topk * MOBA_BLOCK:]
        return (jnp.einsum('bhqkj,bhqkjd->bhqd', p_sel, v_sel)
                + jnp.einsum('bhqk,bhkd->bhqd', p_own, v_own))

    outs = lax.map(chunk, jnp.arange(n_chunks))
    return outs.transpose(1, 2, 0, 3, 4).reshape(B, H, T, HEAD_DIM)

def first_inputs(seed: int = 0) -> dict:
    key = jax.random.key(seed)
    ks = jax.random.split(key, 20)
    f32 = jnp.float32
    D = D_MODEL
    nrm = lambda k, shape, s: (jax.random.normal(k, shape, f32) * s)
    return {
        "x": nrm(ks[0], (BATCH, SEQ, D), 1.0),
        "c": nrm(ks[1], (BATCH, D), 1.0),
        "ada_w": nrm(ks[2], (DEPTH, D, N_MOD * D), 0.1 * D ** -0.5),
        "ada_b": nrm(ks[3], (DEPTH, N_MOD * D), 0.05),
        "norm_g": 1.0 + nrm(ks[4], (DEPTH, N_SUBLAYERS, D), 0.05),
        "ffn_w_in": nrm(ks[5], (DEPTH, 2, D, 2 * D_FF), D ** -0.5),
        "ffn_w_out": nrm(ks[6], (DEPTH, 2, D_FF, D), D_FF ** -0.5),
        "pool_w": nrm(ks[7], (N_A_LAYERS, N_POOL_GROUPS, POOL_GROUP, POOL_GROUP), POOL_GROUP ** -0.5),
        "pool_scale": 1.0 + nrm(ks[8], (N_A_LAYERS, D), 0.1),
        "kv_norm": 1.0 + nrm(ks[9], (D,), 0.05),
        "kv_ada_w": nrm(ks[10], (D, 2 * D), 0.1 * D ** -0.5),
        "kv_ada_b": nrm(ks[11], (2 * D,), 0.05),
        "w_kv": nrm(ks[12], (D, 2 * D), D ** -0.5),
        "k_norm": 1.0 + nrm(ks[13], (HEAD_DIM,), 0.05),
        "w_q": nrm(ks[14], (N_B_LAYERS, D, D), D ** -0.5),
        "q_norm": 1.0 + nrm(ks[15], (N_B_LAYERS, HEAD_DIM), 0.05),
        "w_o": nrm(ks[16], (N_B_LAYERS, D, D), D ** -0.5),
    }

def first_block(x, c, ada_w, ada_b, norm_g, ffn_w_in, ffn_w_out, pool_w, pool_scale,
              kv_norm, kv_ada_w, kv_ada_b, w_kv, k_norm, w_q, q_norm, w_o):
    B, T, D = x.shape
    c_silu = jax.nn.silu(c)
    cos, sin = rope_tables(T)
    kv = None
    for layer in range(DEPTH):
        mods = jnp.split(c_silu @ ada_w[layer] + ada_b[layer], N_MOD, axis=-1)
        sh, sc, g = mods[0], mods[1], mods[2]
        h = modulate(rms_norm(x, norm_g[layer, 0]), sh, sc)
        x = x + MACARON_WEIGHT * (1.0 + g)[:, None, :] * swiglu(h, ffn_w_in[layer, 0], ffn_w_out[layer, 0])
        sh, sc, g = mods[3], mods[4], mods[5]
        h = modulate(rms_norm(x, norm_g[layer, 1]), sh, sc)
        if layer < N_A_LAYERS:
            y = pool_mixer(h, pool_w[layer], pool_scale[layer])
        else:
            j = layer - N_A_LAYERS
            k_blocks, v_blocks, k_mean = kv
            q = (h @ w_q[j]).reshape(B, T, N_HEADS, HEAD_DIM)
            q = rope(rms_norm(q, q_norm[j]), cos, sin).transpose(0, 2, 1, 3)
            att = moba_attention(q, k_blocks, v_blocks, k_mean)
            y = att.transpose(0, 2, 1, 3).reshape(B, T, D) @ w_o[j]
        x = x + (1.0 + g)[:, None, :] * y
        sh, sc, g = mods[6], mods[7], mods[8]
        h = modulate(rms_norm(x, norm_g[layer, 2]), sh, sc)
        x = x + MACARON_WEIGHT * (1.0 + g)[:, None, :] * swiglu(h, ffn_w_in[layer, 1], ffn_w_out[layer, 1])
        if layer == N_A_LAYERS - 1:
            kv = shared_kv(x, c_silu, kv_norm, kv_ada_w, kv_ada_b, w_kv, k_norm, cos, sin)
    return x


DEPTH_2 = 1

CHUNK = 64
Q_BLOCK = 128
SSM_WIDTH = 1024
SSM_GROUP = 16
SSM_GROUPS = SSM_WIDTH // SSM_GROUP
SSM_STATE = 64
DT_MIN = 1e-3
DT_MAX = 1e-1
MLA_HEADS = 16
QK_NOPE = 64
QK_ROPE = 32
V_HEAD = 64
Q_LORA = 256
KV_LORA = 256
MLA_WIDTH = MLA_HEADS * V_HEAD
ROPE_BASE = 10000.0
IN_SPLITS = (SSM_WIDTH, SSM_WIDTH, Q_LORA, KV_LORA, QK_ROPE, MLA_WIDTH, D_MODEL, D_MODEL)
IN_WIDTH = sum(IN_SPLITS)


def _rmsnorm(x, g):
    xf = x.astype(jnp.float32)
    y = xf * lax.rsqrt(jnp.mean(xf * xf, axis=-1, keepdims=True) + EPS)
    return (y * g.astype(jnp.float32)).astype(x.dtype)

def _cmul(ar, ai, br, bi):
    return ar * br - ai * bi, ar * bi + ai * br

def _ssm_branch(u, log_dt, a_re, a_im, b_re, b_im, c_re, c_im, d_skip):
    f32 = jnp.float32
    out_dtype = u.dtype
    bsz, seq, _ = u.shape
    n_chunks = seq // CHUNK
    u = u.astype(f32).reshape(bsz, n_chunks, CHUNK, SSM_GROUPS, SSM_GROUP)
    u = jnp.moveaxis(u, 1, 0)
    dt = jnp.exp(log_dt.astype(f32))[:, None]
    lr, li = a_re.astype(f32), a_im.astype(f32)
    mag = jnp.exp(lr * dt)
    abar_re, abar_im = mag * jnp.cos(li * dt), mag * jnp.sin(li * dt)
    den = lr * lr + li * li
    nr, ni = abar_re - 1.0, abar_im
    fr = (nr * lr + ni * li) / den
    fi = (ni * lr - nr * li) / den
    br, bi = b_re.astype(f32), b_im.astype(f32)
    bbar_re, bbar_im = _cmul(fr[..., None], fi[..., None], br, bi)
    cr_w, ci_w = c_re.astype(f32), c_im.astype(f32)
    d = d_skip.astype(f32).reshape(SSM_GROUPS, SSM_GROUP)

    def combine(e1, e2):
        a1r, a1i, b1r, b1i = e1
        a2r, a2i, b2r, b2i = e2
        ar, ai = _cmul(a2r, a2i, a1r, a1i)
        xr, xi = _cmul(a2r, a2i, b1r, b1i)
        return ar, ai, xr + b2r, xi + b2i

    def chunk_step(carry, u_c):
        sr, si = carry
        bur = jnp.einsum('btgp,gnp->btgn', u_c, bbar_re)
        bui = jnp.einsum('btgp,gnp->btgn', u_c, bbar_im)
        ar = jnp.broadcast_to(abar_re, bur.shape)
        ai = jnp.broadcast_to(abar_im, bur.shape)
        pr, pi_, xr, xi = lax.associative_scan(combine, (ar, ai, bur, bui), axis=1)
        cr, ci = _cmul(pr, pi_, sr[:, None], si[:, None])
        xr, xi = xr + cr, xi + ci
        y = (jnp.einsum('btgn,gpn->btgp', xr, cr_w)
             - jnp.einsum('btgn,gpn->btgp', xi, ci_w) + d * u_c)
        return (xr[:, -1], xi[:, -1]), y

    init = (jnp.zeros((bsz, SSM_GROUPS, SSM_STATE), f32),
            jnp.zeros((bsz, SSM_GROUPS, SSM_STATE), f32))
    _, ys = lax.scan(chunk_step, init, u)
    return jnp.moveaxis(ys, 0, 1).reshape(bsz, seq, SSM_WIDTH).astype(out_dtype)

def _rope(t, cos, sin):
    half = t.shape[-1] // 2
    t1, t2 = t[..., :half], t[..., half:]
    return jnp.concatenate([t1 * cos - t2 * sin, t2 * cos + t1 * sin], axis=-1).astype(t.dtype)

def _mla_branch(q_lat, kv_lat, k_rope, positions, g_q_norm, w_q_up, g_kv_norm, w_kv_up):
    bsz, seq, _ = q_lat.shape
    q = (_rmsnorm(q_lat, g_q_norm) @ w_q_up).reshape(bsz, seq, MLA_HEADS, QK_NOPE + QK_ROPE)
    q_nope, q_rope = q[..., :QK_NOPE], q[..., QK_NOPE:]
    kv = (_rmsnorm(kv_lat, g_kv_norm) @ w_kv_up).reshape(bsz, seq, MLA_HEADS, QK_NOPE + V_HEAD)
    k_nope, v = kv[..., :QK_NOPE], kv[..., QK_NOPE:]
    inv_freq = ROPE_BASE ** (-jnp.arange(0, QK_ROPE, 2, dtype=jnp.float32) / QK_ROPE)
    ang = positions.astype(jnp.float32)[..., None] * inv_freq
    cos, sin = jnp.cos(ang), jnp.sin(ang)
    q_rope = _rope(q_rope, cos[:, :, None], sin[:, :, None])
    k_rope = _rope(k_rope, cos, sin)
    n_blk = seq // Q_BLOCK
    key_chunk = jnp.arange(seq) // CHUNK
    scale = (QK_NOPE + QK_ROPE) ** -0.5

    def to_blocks(t):
        return jnp.moveaxis(t.reshape(bsz, n_blk, Q_BLOCK, *t.shape[2:]), 1, 0)

    def attend(args):
        qn, qr, blk = args
        s = (jnp.einsum('bqhd,bkhd->bhqk', qn, k_nope)
             + jnp.einsum('bqhr,bkr->bhqk', qr, k_rope)).astype(jnp.float32) * scale
        q_chunk = (blk * Q_BLOCK + jnp.arange(Q_BLOCK)) // CHUNK
        mask = key_chunk[None, :] <= q_chunk[:, None]
        p = jax.nn.softmax(jnp.where(mask, s, -jnp.inf), axis=-1).astype(v.dtype)
        return jnp.einsum('bhqk,bkhd->bqhd', p, v)

    o = lax.map(attend, (to_blocks(q_nope), to_blocks(q_rope), jnp.arange(n_blk)))
    return jnp.moveaxis(o, 0, 1).reshape(bsz, seq, MLA_WIDTH)

def second_inputs(seed: int = 0) -> dict:
    key = jax.random.key(seed)
    ks = jax.random.split(key, 25)
    f32 = jnp.float32

    def nrm(k, shape, scale):
        return jax.random.normal(k, shape, f32) * scale

    positions = (jax.random.randint(ks[2], (BATCH, 1), 0, 2048, dtype=jnp.int32)
                 + jnp.arange(SEQ, dtype=jnp.int32)[None, :])
    return {
        "x": nrm(ks[0], (BATCH, SEQ, D_MODEL), 1.0),
        "c": nrm(ks[1], (BATCH, D_MODEL), 1.0),
        "positions": positions,
        "w_ada": nrm(ks[3], (DEPTH_2, D_MODEL, 3 * D_MODEL), 0.5 * D_MODEL ** -0.5),
        "b_ada": nrm(ks[4], (DEPTH_2, 3 * D_MODEL), 0.01),
        "g_pre": 1.0 + nrm(ks[5], (DEPTH_2, D_MODEL), 0.01),
        "w_in": nrm(ks[6], (DEPTH_2, D_MODEL, IN_WIDTH), D_MODEL ** -0.5),
        "ssm_log_dt": jax.random.uniform(ks[7], (DEPTH_2, SSM_GROUPS), f32,
                                         math.log(DT_MIN), math.log(DT_MAX)),
        "ssm_a_re": -0.5 + nrm(ks[8], (DEPTH_2, SSM_GROUPS, SSM_STATE), 0.01),
        "ssm_a_im": (jnp.pi * jnp.arange(SSM_STATE, dtype=f32)
                     + nrm(ks[9], (DEPTH_2, SSM_GROUPS, SSM_STATE), 0.01)),
        "ssm_b_re": nrm(ks[10], (DEPTH_2, SSM_GROUPS, SSM_STATE, SSM_GROUP), (2 * SSM_GROUP) ** -0.5),
        "ssm_b_im": nrm(ks[11], (DEPTH_2, SSM_GROUPS, SSM_STATE, SSM_GROUP), (2 * SSM_GROUP) ** -0.5),
        "ssm_c_re": nrm(ks[12], (DEPTH_2, SSM_GROUPS, SSM_GROUP, SSM_STATE), (2 * SSM_STATE) ** -0.5),
        "ssm_c_im": nrm(ks[13], (DEPTH_2, SSM_GROUPS, SSM_GROUP, SSM_STATE), (2 * SSM_STATE) ** -0.5),
        "ssm_d": nrm(ks[14], (DEPTH_2, SSM_WIDTH), 0.5),
        "w_glu": nrm(ks[15], (DEPTH_2, SSM_WIDTH, 2 * SSM_WIDTH), SSM_WIDTH ** -0.5),
        "b_glu": nrm(ks[16], (DEPTH_2, 2 * SSM_WIDTH), 0.01),
        "g_q_norm": 1.0 + nrm(ks[17], (DEPTH_2, Q_LORA), 0.01),
        "w_q_up": nrm(ks[18], (DEPTH_2, Q_LORA, MLA_HEADS * (QK_NOPE + QK_ROPE)), Q_LORA ** -0.5),
        "g_kv_norm": 1.0 + nrm(ks[19], (DEPTH_2, KV_LORA), 0.01),
        "w_kv_up": nrm(ks[20], (DEPTH_2, KV_LORA, MLA_HEADS * (QK_NOPE + V_HEAD)), KV_LORA ** -0.5),
        "w_br_ssm": nrm(ks[21], (DEPTH_2, SSM_WIDTH, D_MODEL), SSM_WIDTH ** -0.5),
        "w_br_mla": nrm(ks[22], (DEPTH_2, MLA_WIDTH, D_MODEL), MLA_WIDTH ** -0.5),
        "w_out": nrm(ks[23], (DEPTH_2, D_MODEL, D_MODEL), D_MODEL ** -0.5),
        "g_post": 1.0 + nrm(ks[24], (DEPTH_2, D_MODEL), 0.01),
    }

def second_block(x, c, positions, w_ada, b_ada, g_pre, w_in, ssm_log_dt, ssm_a_re, ssm_a_im,
              ssm_b_re, ssm_b_im, ssm_c_re, ssm_c_im, ssm_d, w_glu, b_glu, g_q_norm, w_q_up,
              g_kv_norm, w_kv_up, w_br_ssm, w_br_mla, w_out, g_post):
    split_at = np.cumsum(IN_SPLITS)[:-1].tolist()
    for l in range(DEPTH_2):
        mod = c @ w_ada[l] + b_ada[l]
        shift, scale, gate = jnp.split(mod, 3, axis=-1)
        h = _rmsnorm(x, g_pre[l]) * (1.0 + scale[:, None]) + shift[:, None]
        proj = h @ w_in[l]
        u_s, z_s, q_lat, kv_lat, k_rope, z_m, gl_s, gl_m = jnp.split(proj, split_at, axis=-1)
        y_s = _ssm_branch(u_s, ssm_log_dt[l], ssm_a_re[l], ssm_a_im[l], ssm_b_re[l],
                          ssm_b_im[l], ssm_c_re[l], ssm_c_im[l], ssm_d[l])
        glu_a, glu_b = jnp.split(jax.nn.gelu(y_s) @ w_glu[l] + b_glu[l], 2, axis=-1)
        y_s = ((glu_a * jax.nn.sigmoid(glu_b)) * jax.nn.silu(z_s)) @ w_br_ssm[l]
        y_m = _mla_branch(q_lat, kv_lat, k_rope, positions, g_q_norm[l], w_q_up[l],
                          g_kv_norm[l], w_kv_up[l])
        y_m = (y_m * jax.nn.silu(z_m)) @ w_br_mla[l]
        merged = jax.nn.sigmoid(gl_s) * y_s + jax.nn.sigmoid(gl_m) * y_m
        out = merged @ w_out[l]
        x = x + gate[:, None] * _rmsnorm(out, g_post[l])
    return x


def setup_inputs(seed=0):
    out = dict(first_inputs(seed))
    for name, value in second_inputs(seed + 1).items():
        if name != "x":
            out[name + "_2"] = value
    return out


def reference(
    x, c, ada_w, ada_b, norm_g, ffn_w_in, ffn_w_out, pool_w, pool_scale, kv_norm, kv_ada_w,
    kv_ada_b, w_kv, k_norm, w_q, q_norm, w_o, c_2, positions_2, w_ada_2, b_ada_2, g_pre_2,
    w_in_2, ssm_log_dt_2, ssm_a_re_2, ssm_a_im_2, ssm_b_re_2, ssm_b_im_2, ssm_c_re_2,
    ssm_c_im_2, ssm_d_2, w_glu_2, b_glu_2, g_q_norm_2, w_q_up_2, g_kv_norm_2, w_kv_up_2,
    w_br_ssm_2, w_br_mla_2, w_out_2, g_post_2,
):
    x = first_block(
        x, c, ada_w, ada_b, norm_g, ffn_w_in, ffn_w_out, pool_w, pool_scale, kv_norm, kv_ada_w,
        kv_ada_b, w_kv, k_norm, w_q, q_norm, w_o,
    )
    return second_block(
        x, c_2, positions_2, w_ada_2, b_ada_2, g_pre_2, w_in_2, ssm_log_dt_2, ssm_a_re_2,
        ssm_a_im_2, ssm_b_re_2, ssm_b_im_2, ssm_c_re_2, ssm_c_im_2, ssm_d_2, w_glu_2, b_glu_2,
        g_q_norm_2, w_q_up_2, g_kv_norm_2, w_kv_up_2, w_br_ssm_2, w_br_mla_2, w_out_2, g_post_2,
    )


_drawn_inputs = setup_inputs


def setup_inputs(seed=0):
    import zlib

    import numpy as np

    out = dict(_drawn_inputs(seed))
    spreads = {}
    factors = {'kv_norm': 5.585,
     'k_norm': 8.0,
     'q_norm': 8.0,
     'b_ada_2': 5.838,
     'g_pre_2': 8.0,
     'ssm_log_dt_2': 31.88,
     'ssm_a_re_2': 64.0,
     'ssm_a_im_2': 24.328,
     'ssm_b_re_2': 36.48,
     'ssm_b_im_2': 36.208,
     'ssm_c_re_2': 35.024,
     'ssm_c_im_2': 37.456,
     'b_glu_2': 64.0,
     'g_q_norm_2': 8.0,
     'g_kv_norm_2': 8.0,
     'g_post_2': 64.0}
    for name, (base, spread) in spreads.items():
        noise = np.random.default_rng([zlib.crc32(name.encode()), seed]).standard_normal(out[name].shape)
        drawn = base * np.exp(spread * noise) if base else spread * noise
        out[name] = __import__('jax').numpy.asarray(drawn.astype(out[name].dtype))
    for name, factor in factors.items():
        out[name] = (out[name] * factor).astype(out[name].dtype)
    return out
```

```python
from contextlib import ExitStack

import numpy as np

import concourse.bass as bass
from concourse import mybir

F32 = mybir.dt.float32
F32R = mybir.dt.float32r
I32 = mybir.dt.int32
ALU = mybir.AluOpType
ACT = mybir.ActivationFunctionType
AX = mybir.AxisListType.X

P = 128
D = 1024
KT = D // P
T = 256
FFN_TILES = 22
WIDTH = 1024
EPS = 1e-6
HEADS_1, HEAD_DIM = 8, 128
HEADS_2, QK_2, V_2 = 16, 96, 64
TWO_PI = 6.283185307179586

PHASES = [("ffn0", 66), ("pool", 2), ("ffn1", 66), ("kv", 16), ("ffn2", 66), ("q", 8), ("o", 8), ("ffn3", 66),
          ("lat", 4), ("kr", 1), ("u", 8), ("qup", 4), ("kvup", 4), ("zm", 8), ("brm", 8), ("glm", 8),
          ("zs", 8), ("gls", 8), ("glu", 16), ("brs", 8), ("out", 8)]
UNIT, N_UNITS = {}, 0
for _name, _n in PHASES:
    UNIT[_name] = N_UNITS
    N_UNITS += _n
FFN_BASE = [UNIT[f"ffn{f}"] for f in range(4)]

RING, LAND = 6, 3
GW = 512
N_G = 46
G_PRE, G_POOL = 4, 1
G_FIRST = [1, 1, 1, 0]
SEGMENTS = [[(5, "silu")], [(5, "silu")], [(5, "silu")], [(1, "silu"), (3, "c2"), (1, None)]]
G_FFN = [4, 16, 27, 38]
M_LAYER = [0, 88]
M_KV, M_2 = 72, 160
N_MOD = 184

TILES = [("ffn0", 22, "d"), ("pool", 8, "d"), ("ffn1", 22, "d"), ("k", 8, "a"), ("v", 8, "a"), ("ffn2", 22, "d"),
         ("q", 8, "a"), ("att1", 4, "d"), ("o", 8, "d"), ("ffn3", 22, "d"), ("lat", 4, "a"), ("kr", 1, "a"),
         ("u", 8, "a"), ("qup", 8, "a"), ("kvup", 12, "a"), ("att2", 8, "d"), ("zm", 8, "a"), ("brm", 8, "a"),
         ("glm", 8, "a"), ("zs", 8, "a"), ("gls", 8, "a"), ("glu", 16, "x"), ("brs", 8, "d"), ("out", 8, "a")]
TILE, OWNER = {}, []
for _name, _n, _who in TILES:
    TILE[_name] = len(OWNER)
    OWNER += [_who] * _n if _who != "x" else ["d", "a"] * (_n // 2)
TILE_UNITS = {"pool": ("pool", 0, 4), "k": ("kv", 0, 1), "v": ("kv", 8, 1), "qup": ("qup", 0, 2), "kvup": ("kvup", 0, 3),
              "att1": None, "att2": None}
FINISHED, _parts = {}, 0
for _name, _n, _who in TILES:
    if _name.startswith("ffn"):
        continue
    _from = TILE_UNITS.get(_name, (_name, 0, 1))
    for _k in range(_n):
        if _from and _k % _from[2] == _from[2] - 1:
            FINISHED[TILE[_name] + _k] = ("used", UNIT[_from[0]] + _from[1] + _k // _from[2] + 1)
        else:
            _parts += 1
            FINISHED[TILE[_name] + _k] = ("part", _parts)


def freed_count(o):
    return OWNER[o], OWNER[:o + 1].count(OWNER[o])


VEC, NV = {}, 0
for _name, _n in [("c", 8), ("c2", 8), ("logdt", 32), ("lr", 32), ("li", 32), ("bias", N_MOD), ("norm_g", 48),
                  ("pool_scale", 8), ("kv_norm", 8), ("k_norm", 1), ("q_norm", 1), ("g_pre", 8), ("ssm_d", 8),
                  ("b_glu", 16), ("g_q", 2), ("g_kv", 2), ("g_post", 8)]:
    VEC[_name] = NV
    NV += _n
CON, NC_ = {}, 0
for _name, _n in [("ident", 128), ("ones", 128), ("rot1", 128), ("rot2", 96), ("cos1", T), ("sin1", T),
                  ("mask", 2 * T), ("cnt", 64), ("invf", 1), ("eps", 1), ("zero", 1)]:
    CON[_name] = NC_
    NC_ += _n
POOL_W = (2, 4, 8, 16)
PAD = 16
CH = 32
NCH = T // CH


GATES = [(_name, _n) for _name in ("brm", "glm", "zs", "gls") for _n in range(KT)]


def g_unit(base, j):
    return base + (2 * j if j < 2 else 3 * j - 1)


def o_unit(base, j):
    return base + (65 if j == FFN_TILES - 1 else 3 * j + 4)


def build_program(nc, stream, gstream, vecs_d, cons_d, mask2_d, xin, pos_d, ssm_b, ssm_c, out):
    with ExitStack() as ctx:
        def sb(name, shape, dt=F32):
            return ctx.enter_context(nc.sbuf_tensor(name, shape, dt))

        def sem(name):
            return ctx.enter_context(nc.semaphore(name))

        land = sb("land", [P, LAND, WIDTH])
        w_hi = sb("w_hi", [P, RING, WIDTH], F32R)
        w_lo = sb("w_lo", [P, RING, WIDTH], F32R)
        x = sb("x", [P, KT, T])
        x_hi = sb("x_hi", [P, KT, T], F32R)
        x_lo = sb("x_lo", [P, KT, T], F32R)
        a_hi = sb("a_hi", [P, KT, T], F32R)
        a_lo = sb("a_lo", [P, KT, T], F32R)
        h_hi = sb("h_hi", [P, 2, T], F32R)
        h_lo = sb("h_lo", [P, 2, T], F32R)
        vecs = sb("vecs", [P, NV])
        cons = sb("cons", [P, NC_])
        rh = sb("rh", [P, 2 * T])
        base_t = sb("base_t", [P, 2, 32, CH])
        chunk_t = sb("chunk_t", [P, 2, 32, NCH])
        ssm_s = sb("ssm_s", [P, 20, 32])
        coef = sb("coef", [P, 9, 32])
        csil = sb("csil", [P, KT])
        att_s = sb("att_s", [P, 2, 16])
        arena = sb("arena", [P, 20480])

        def region(kb, shape):
            n = int(np.prod(shape))
            v = arena[:, kb * 256:kb * 256 + n]
            names = "abcd"[:len(shape)]
            if len(shape) == 1:
                return v
            kw = {names[i]: shape[i] for i in range(1, len(shape))}
            return v.rearrange(f"p ({' '.join(names)}) -> p {' '.join(names)}", **kw)

        def region_at(col, shape):
            n = int(np.prod(shape))
            v = arena[:, col:col + n]
            names = "abcd"[:len(shape)]
            kw = {names[i]: shape[i] for i in range(1, len(shape))}
            return v.rearrange(f"p ({' '.join(names)}) -> p {' '.join(names)}", **kw)

        rx = region(79, [T])
        g_land = region(0, [2, 8, GW])
        g_acc = region(32, [2, GW])
        silu_b = region(36, [2, T])
        hid = region(38, [2, T])
        kT = region(40, [HEADS_1, T])
        v1 = region(48, [2, D])
        t_buf = region(56, [KT, T])
        qT = region(64, [HEADS_1, T])
        win_h = region(40, [KT, PAD + T])
        win_a = region_at(64 * 256, [KT, PAD + T])
        win_b = region_at(64 * 256 + KT * (PAD + T), [6, PAD + T])
        rope_sq, rope_kn, rope_t = region(56, [2, T]), region(58, [2, T]), region(60, [2, 2, T])
        ws1 = [(region(72, [4, T]), region(76, [2, 384])), (region(32, [4, T]), region(36, [2, 384]))]
        uT = region(0, [KT, T])
        q2 = region(8, [HEADS_2, T])
        k2 = region(24, [HEADS_2, T])
        v2 = region(40, [2, D])
        ym = region(48, [KT, T])
        lat_raw, lat_sq, lat_n = region(64, [4, T]), region(68, [4, T]), region(72, [4, T])
        kr_buf = region(76, [3, T])
        pos_i = region(78, [T])
        rope2 = region(56, [2, T])[0:QK_2]
        ang = region(58, [6, T])
        ws2 = [(region(64, [4, T]), region(68, [2, 384])), (region(72, [4, T]), region(76, [2, 384]))]
        rot_t = [region(8, [2, 2, T]), region(12, [2, 2, T])]
        ssm_m = region(20, [2, 2, T])
        glm_t, sig_t = region(24, [2, T]), region(26, [2, T])
        ssm_v = [region(16, [2, 2, T]), region(28, [2, 2, T])]
        gel = region(56, [KT, T])
        zs_t = region(32, [KT, T])
        b_sb = region(40, [2, KT, P])
        mrg = region(48, [KT, T])
        gs_t = region(64, [KT, T])
        cc = region(72, [2, 32, 32])
        cc_tmp = region(64, [2, 32, 32])
        c_raw = region(32, [2, 32, 32])
        o_raw = region(8, [KT, T])

        acc4 = ctx.enter_context(nc.psum_tensor("acc4", [P, 4, 512], F32))
        tiles = ctx.enter_context(nc.psum_tensor("tiles", [P, 2, 512], F32))
        nrm = ctx.enter_context(nc.psum_tensor("nrm", [P, 512], F32))
        mods = ctx.enter_context(nc.psum_tensor("mods", [P, 512], F32))
        yT = [acc4[:, n // 2, (n % 2) * T:(n % 2 + 1) * T] for n in range(KT)]

        landed = [sem(f"landed{i}") for i in range(LAND)]
        hi_done = sem("hi_done")
        lo_done = sem("lo_done")
        used = sem("used")
        g_landed = [sem(f"g_landed{i}") for i in range(2)]
        g_step = sem("g_step")
        g_done = sem("g_done")
        g_red = sem("g_red")
        vec_in, con_in, x_in, pos_in = sem("vec_in"), sem("con_in"), sem("x_in"), sem("pos_in")
        b_in, c_in, mask_in, out_st = sem("b_in"), sem("c_in"), sem("mask_in"), sem("out_st")
        freed = {"d": sem("freed_d"), "a": sem("freed_a")}
        part_done = sem("part_done")
        x_upd = sem("x_upd")
        sq_done, nrm_done, rt_done = sem("sq_done"), sem("nrm_done"), sem("rt_done")
        t_done, xh_done, xl_done = sem("t_done"), sem("xh_done"), sem("xl_done")
        silu_done, hh_done, h_done = sem("silu_done"), sem("hh_done"), sem("h_done")
        dve_s, act_s, pool_s = sem("dve_s"), sem("act_s"), sem("pool_s")
        csilu_done, ang_done, sin_done, f_done = sem("csilu_done"), sem("ang_done"), sem("sin_done"), sem("f_done")
        hsq_done, hs_done, hrt_done = sem("hsq_done"), sem("hs_done"), sem("hrt_done")
        kn_done, hrot_done, rope_done = sem("kn_done"), sem("hrot_done"), sem("rope_done")
        s_done, sm_done, mx_done, ex_done = sem("s_done"), sem("sm_done"), sem("mx_done"), sem("ex_done")
        pn_done, pt_done, pe_done = sem("pn_done"), sem("pt_done"), sem("pe_done")
        af_done, ah_done, al_done = sem("af_done"), sem("ah_done"), sem("al_done")
        lsq_done, lsum_done, lrt_done = sem("lsq_done"), sem("lsum_done"), sem("lrt_done")
        krot_done, kr_done, kb_done = sem("krot_done"), sem("kr_done"), sem("kb_done")
        qrot_done, qrope_done = sem("qrot_done"), sem("qrope_done")
        base_done = sem("base_done")
        tab_done, tab_free, cc_done = sem("tab_done"), sem("tab_free"), sem("cc_done")
        bu_done, bu_free, zz_done, y_done = sem("bu_done"), sem("bu_free"), sem("zz_done"), sem("y_done")
        yp_done, gel_done, glm_used, gv_done = sem("yp_done"), sem("gel_done"), sem("glm_used"), sem("gv_done")
        fin_done = sem("fin_done")
        done_sem = {"used": used, "part": part_done}

        def wait_tile(eng, o):
            which, n = FINISHED[o]
            eng.wait_ge(done_sem[which], n)

        def wait_freed(eng, o):
            who, n = freed_count(o)
            eng.wait_ge(freed[who], n)

        def vec(name, a=0, n=1):
            return vecs[:, VEC[name] + a:VEC[name] + a + n]

        def con(name, n):
            return cons[:, CON[name]:CON[name] + n]

        ident, ones = con("ident", P), con("ones", P)
        cos1, sin1 = con("cos1", T), con("sin1", T)
        zero = con("zero", 1)

        STAGE = [(M_LAYER[0], 8 + M_LAYER[0], ("norm_g", 0)), (24, 32, ("norm_g", 8)), (48, 56, ("norm_g", 16)),
                 (M_KV, M_KV + 8, ("kv_norm", 0)), (88, 96, ("norm_g", 24)), (112, 120, ("norm_g", 32)),
                 (136, 144, ("norm_g", 40)), (M_2, M_2 + 8, ("g_pre", 0))]
        SPLITS = {0: 1, 1: 2, 2: 3, 3: 4, 4: 5, 5: 6, 6: 7, 7: 8}

        def wait_bank(eng, o):
            if o >= 2:
                who, n = freed_count(o - 2)
                eng.wait_ge(freed[who], n)

        def load_unit(sp, u, slot, i=0):
            if u >= LAND:
                sp.wait_ge(lo_done, i * 12 + (u - LAND + 1))
            sp.dma_start(land[:, slot], stream[i * 12 + u]).then_inc(landed[slot], 16)

        def split_hi(act, u, i=0):
            act.wait_ge(landed[u % LAND], i * (16 * 12 // LAND) + 16 * (u // LAND + 1))
            if u >= RING:
                act.wait_ge(used, i * 12 + (u - RING + 1))
            nc.scalar.copy(w_hi[:, u % RING], land[:, u % LAND]).then_inc(hi_done, 1)

        def split_lo(dve, u, i=0):
            dve.wait_ge(hi_done, i * 12 + (u + 1))
            nc.vector.tensor_tensor(w_lo[:, u % RING], land[:, u % LAND], w_hi[:, u % RING].bitcast(F32),
                                    ALU.subtract).then_inc(lo_done, 1)

        def products(pe, outs, pairs, start=True, stop=True, **kw):
            last = None
            for n, (lh, ll, rh, rl) in enumerate(pairs):
                first, end = start and n == 0, stop and n == len(pairs) - 1
                nc.tensor.matmul(outs, lh, rh, start=first, stop=False, **kw)
                nc.tensor.matmul(outs, lh, rl, start=False, stop=False, **kw)
                last = nc.tensor.matmul(outs, ll, rh, start=False, stop=end, **kw)
            return last

        def w_tile(u, a, n):
            return w_hi[:, u % RING, a:a + n], w_lo[:, u % RING, a:a + n]

        block = ctx.enter_context(nc.Block())

        @block.sync
        def _(sp):
            def g_load(b, i=0):
                if b >= 2:
                    sp.wait_ge(g_done, i * 2 + (b - 1))
                sp.dma_start(g_land[:, b % 2], gstream[i * 2 + b]).then_inc(g_landed[b % 2], 16)

            def units(name, n):
                for u in range(UNIT[name], UNIT[name] + n):
                    load_unit(sp, u, u % LAND)

            sp.dma_start(vecs[:], vecs_d).then_inc(vec_in, 16)
            g_load(0)
            g_load(1)
            sp.dma_start(cons[:], cons_d).then_inc(con_in, 16)
            sp.dma_start(x[:], xin).then_inc(x_in, 16)
            for k in range(LAND):
                load_unit(sp, k, k)
            g_load(2)
            g_load(3)
            for f in range(4):
                base, b = FFN_BASE[f], G_FFN[f]
                if G_FIRST[f]:
                    g_load(b)
                    b += 1
                for u in range(base, base + 5):
                    if not (f == 0 and u < LAND):
                        load_unit(sp, u, u % LAND)
                u = base + 5
                for reps, vector in SEGMENTS[f]:
                    with sp.Fori(0, reps) as i:
                        for m in range(4):
                            if vector and m % 2 == 0:
                                g_load(b + m // 2, i)
                            for s in range(3):
                                load_unit(sp, u + 3 * m + s, (u + 3 * m + s) % LAND, i)
                    u += 12 * reps
                    b += 2 * reps if vector else 0
                load_unit(sp, u, u % LAND)
                if f == 0:
                    g_load(G_PRE + 11)
                    units("pool", 2)
                elif f == 1:
                    units("kv", 16)
                elif f == 2:
                    units("q", 8)
                    units("o", 8)
            wait_freed(sp, TILE["att1"] + 3)
            sp.dma_start(con("mask", 2 * T), mask2_d).then_inc(mask_in, 16)
            sp.dma_start(pos_i[64:96].bitcast(I32), pos_d).then_inc(pos_in, 16)
            for name, n in PHASES[8:14]:
                units(name, n)
            wait_tile(sp, TILE["att2"] + 7)
            sp.dma_start(b_sb, ssm_b).then_inc(b_in, 16)
            sp.dma_start(c_raw, ssm_c).then_inc(c_in, 16)
            for name, n in PHASES[14:]:
                units(name, n)
            for k in range(KT):
                sp.wait_ge(fin_done, k + 1)
                sp.dma_start(out[:, k], x[:, k]).then_inc(out_st, 16)
            sp.wait_ge(out_st, 16 * KT)

        @block.tensor
        def _(pe):
            def reduce_block(b, i=0):
                pe.wait_ge(g_done, i * 2 + (b + 1))
                for q in range(4):
                    m = nc.tensor.matmul(mods[:, bass.ds(i * 8 + (4 * b + q), 1)],
                                         g_acc[:, b % 2, q * P:(q + 1) * P], ones[:, 0:1], start=True, stop=True)
                m.then_inc(g_red, 1)

            def sum_squares(n):
                if n:
                    pe.wait_ge(rt_done, n)
                for k in range(KT):
                    pe.wait_ge(sq_done, KT * n + k + 1)
                    m = nc.tensor.matmul(nrm[:, 0:T], ones, t_buf[:, k], start=(k == 0), stop=(k == KT - 1))
                m.then_inc(nrm_done, 1)

            def column_unit(u, o, hi, lo, split_base=None, half=None, n_out=P):
                wait_bank(pe, o)
                pe.wait_ge(lo_done, u + 1)
                if split_base is not None:
                    pe.wait_ge(xl_done, split_base + KT)
                dst = tiles[0:n_out, o % 2, 0:T]
                m = products(pe, dst, [(*w_tile(u, k * n_out, n_out), hi[:, k], lo[:, k]) for k in range(KT)])
                m.then_inc(used, 1)

            def gate_unit(base, j, u, i, first=None):
                pe.wait_ge(lo_done, i * 12 + (u + 1))
                for k in range(KT):
                    if first is not None:
                        pe.wait_ge(xl_done, KT * (first - 1) + k + 1)
                    m = products(pe, tiles[:, j % 2, 0:T], [(*w_tile(u, k * P, P), x_hi[:, k], x_lo[:, k])],
                                 start=(k == 0), stop=(k == KT - 1))
                m.then_inc(used, 1)

            def up_unit(j, u, i):
                pe.wait_ge(lo_done, i * 12 + (u + 1))
                m = products(pe, tiles[:, j % 2, T:2 * T],
                             [(*w_tile(u, k * P, P), x_hi[:, k], x_lo[:, k]) for k in range(KT)])
                m.then_inc(used, 1)

            def out_unit(f, j, u, i, per):
                pe.wait_ge(lo_done, i * 12 + (u + 1))
                pe.wait_ge(h_done, i * per + (FFN_TILES * f + j + 1))
                for n in range(KT):
                    m = products(pe, yT[n], [(*w_tile(u, n * P, P), h_hi[:, j % 2], h_lo[:, j % 2])],
                                 start=(j == 0 and per == 0 and n % 2 == 0),
                                 stop=(j == FFN_TILES - 1 and per == 0), skip_group_check=True)
                m.then_inc(used, 1)

            def ffn(f, stage):
                base, o0, b = FFN_BASE[f], TILE[f"ffn{f}"], G_FFN[f]
                nd = OWNER[:o0].count("d")
                for j in range(2):
                    wait_bank(pe, o0 + j)
                    gate_unit(base, j, g_unit(base, j), 0, SPLITS[stage] if j == 0 else None)
                    up_unit(j, g_unit(base, j) + 1, 0)
                out_unit(f, 0, o_unit(base, 0), 0, 0)
                if G_FIRST[f]:
                    reduce_block(b)
                    b += 1
                j0 = 2
                for reps, vector in SEGMENTS[f]:
                    with pe.Fori(0, reps) as i:
                        for m in range(4):
                            j = j0 + m
                            u = g_unit(base, j)
                            pe.wait_ge(freed["d"], i * 4 + (nd + j - 1))
                            gate_unit(base, j, u, i)
                            up_unit(j, u + 1, i)
                            out_unit(f, j - 1, u + 2, i, 4)
                            if vector and m % 2 == 1:
                                reduce_block(b + m // 2, i)
                    j0 += 4 * reps
                    b += 2 * reps if vector else 0
                out_unit(f, FFN_TILES - 1, o_unit(base, FFN_TILES - 1), 0, 0)

            def head_sum(n):
                pe.wait_ge(hsq_done, n + 1)
                nc.tensor.matmul(acc4[:, n % 2], ones, rope_sq, start=True, stop=True).then_inc(hs_done, 1)

            def head_rot(n):
                pe.wait_ge(kn_done, n + 1)
                nc.tensor.matmul(acc4[:, 2 + n % 2], con("rot1", P), rope_kn, start=True, stop=True).then_inc(hrot_done, 1)

            rot2 = cons[0:QK_2, CON["rot2"]:CON["rot2"] + QK_2]

            def attention(n0, groups, o0, qq, kk, vv, parts, vdim, ws, ready):
                def scores(g):
                    ready(g)
                    if n0 + g:
                        pe.wait_ge(sm_done, n0 + g)
                    for h in range(2):
                        for qt in range(2):
                            m = nc.tensor.matmul(acc4[:, h, qt * T:(qt + 1) * T], qq[0:parts, 2 * g + h, qt * P:(qt + 1) * P],
                                                 kk[0:parts, 2 * g + h, :], start=True, stop=True)
                    m.then_inc(s_done, 1)

                scores(0)
                for g in range(groups):
                    n = n0 + g
                    if g + 1 < groups:
                        scores(g + 1)
                    sm, pt = ws[g % 2]
                    pe.wait_ge(pn_done, 4 * (n + 1))
                    if n:
                        pe.wait_ge(pe_done, n)
                    for h in range(2):
                        for qt, kt in ((0, 0), (1, 0), (1, 1)):
                            col = T + 0 if kt else qt * P
                            m = nc.tensor.transpose(acc4[:, 2 + h, col:col + P], sm[:, 2 * h + qt, kt * P:(kt + 1) * P],
                                                    ident)
                    m.then_inc(pt_done, 1)
                    wait_bank(pe, o0 + g)
                    pe.wait_ge(pe_done, n + 1)
                    for h in range(2):
                        head = 2 * g + h
                        if vdim == P:
                            dst = tiles[:, (o0 + g) % 2, h * T:(h + 1) * T]
                        else:
                            dst = tiles[h * vdim:(h + 1) * vdim, (o0 + g) % 2, 0:T]
                        nc.tensor.matmul(dst, vv[:, 0, head * vdim:(head + 1) * vdim], pt[:, h, 0:T],
                                         start=True, stop=False)
                        m = nc.tensor.matmul(dst[:, P:T], vv[:, 1, head * vdim:(head + 1) * vdim], pt[:, h, T:T + P],
                                             start=False, stop=True)
                    m.then_inc(part_done, 1)

            pe.wait_ge(con_in, 16)
            for b in range(G_PRE):
                reduce_block(b)
            sum_squares(0)
            ffn(0, 0)
            sum_squares(1)
            reduce_block(G_PRE + 11)
            for q in range(2):
                u = UNIT["pool"] + q
                pe.wait_ge(lo_done, u + 1)
                for g in range(2):
                    for n in range(2):
                        o = TILE["pool"] + 4 * q + 2 * g + n
                        k0 = 4 * q + 2 * g
                        wait_bank(pe, o)
                        pe.wait_ge(xl_done, KT * (SPLITS[1] - 1) + k0 + 2)
                        m = products(pe, tiles[:, o % 2, 0:T],
                                     [(*w_tile(u, (2 * g + k) * 256 + n * P, P), x_hi[:, k0 + k], x_lo[:, k0 + k])
                                      for k in range(2)])
                        m.then_inc(used if (g, n) == (1, 1) else part_done, 1)
            sum_squares(2)
            ffn(1, 2)
            sum_squares(3)
            for h in range(HEADS_1):
                column_unit(UNIT["kv"] + h, TILE["k"] + h, x_hi, x_lo, KT * (SPLITS[3] - 1) if h == 0 else None)
                if h in (3, 5, 7):
                    head_sum(h // 2 - 1)
                if h in (4, 6):
                    head_rot(h // 2 - 2)
            for h in range(HEADS_1):
                u, o = UNIT["kv"] + 8 + h, TILE["v"] + h
                wait_bank(pe, o)
                pe.wait_ge(lo_done, u + 1)
                for tt in range(2):
                    m = products(pe, tiles[:, o % 2, tt * P:(tt + 1) * P],
                                 [(x_hi[:, k, tt * P:(tt + 1) * P], x_lo[:, k, tt * P:(tt + 1) * P],
                                   *w_tile(u, k * P, P)) for k in range(KT)])
                m.then_inc(used, 1)
                if h == 0:
                    head_rot(2)
                if h == 1:
                    head_sum(3)
                if h == 2:
                    head_rot(3)
            ffn(2, 4)
            sum_squares(4)
            for h in range(HEADS_1):
                column_unit(UNIT["q"] + h, TILE["q"] + h, x_hi, x_lo, KT * (SPLITS[5] - 1) if h == 0 else None)
                if h in (3, 5, 7):
                    head_sum(4 + h // 2 - 1)
                if h in (4, 6):
                    head_rot(4 + h // 2 - 2)
            head_rot(6)
            head_sum(7)
            head_rot(7)
            attention(0, 4, TILE["att1"], qT, kT, v1, P, P, ws1, lambda g: pe.wait_ge(rope_done, 8))
            for n in range(KT):
                if n == 0:
                    wait_freed(pe, TILE["att1"] + 3)
                column_unit(UNIT["o"] + n, TILE["o"] + n, a_hi, a_lo)
            sum_squares(5)
            ffn(3, 6)
            sum_squares(6)
            for n in range(4):
                column_unit(UNIT["lat"] + n, TILE["lat"] + n, x_hi, x_lo, KT * (SPLITS[7] - 1) if n == 0 else None)
            column_unit(UNIT["kr"], TILE["kr"], x_hi, x_lo, n_out=QK_2)
            for n in range(2):
                column_unit(UNIT["u"] + n, TILE["u"] + n, x_hi, x_lo)
            for q in range(2):
                for k in range(2):
                    pe.wait_ge(lsq_done, 2 * q + k + 1)
                    m = nc.tensor.matmul(nrm[:, q * T:(q + 1) * T], ones, lat_sq[:, 2 * q + k], start=(k == 0),
                                         stop=(k == 1))
            m.then_inc(lsum_done, 1)
            wait_freed(pe, TILE["kr"])
            nc.tensor.matmul(acc4[0:QK_2, 2, 0:T], rot2, kr_buf[0:QK_2, 0], start=True, stop=True).then_inc(krot_done, 1)
            for n in range(2, KT):
                column_unit(UNIT["u"] + n, TILE["u"] + n, x_hi, x_lo)
            for n in range(4):
                u = UNIT["qup"] + n
                pe.wait_ge(lo_done, u + 1)
                if n == 0:
                    pe.wait_ge(al_done, 4)
                for pair in range(2):
                    o = TILE["qup"] + 2 * n + pair
                    wait_bank(pe, o)
                    for h in range(2):
                        m = products(pe, tiles[0:QK_2, o % 2, h * T:(h + 1) * T],
                                     [(*w_tile(u, k * 384 + (2 * pair + h) * QK_2, QK_2), a_hi[:, k], a_lo[:, k])
                                      for k in range(2)])
                    m.then_inc(used if pair else part_done, 1)
            for n in range(4):
                u = UNIT["kvup"] + n
                pe.wait_ge(lo_done, u + 1)
                for pair in range(2):
                    o = TILE["kvup"] + 3 * n + pair
                    wait_bank(pe, o)
                    for h in range(2):
                        m = products(pe, tiles[:, o % 2, h * T:(h + 1) * T],
                                     [(*w_tile(u, k * 512 + (2 * pair + h) * P, P), a_hi[:, 2 + k], a_lo[:, 2 + k])
                                      for k in range(2)])
                    m.then_inc(part_done, 1)
                o = TILE["kvup"] + 3 * n + 2
                wait_bank(pe, o)
                for tt in range(2):
                    m = products(pe, tiles[:, o % 2, tt * T:(tt + 1) * T],
                                 [(a_hi[:, 2 + k, tt * P:(tt + 1) * P], a_lo[:, 2 + k, tt * P:(tt + 1) * P],
                                   *(w[:, u % RING, k * 512:(k + 1) * 512].rearrange("p (h c) -> p h c", c=P)[:, :, V_2:P]
                                     for w in (w_hi, w_lo))) for k in range(2)])
                m.then_inc(used, 1)
                for g in (2 * n, 2 * n + 1):
                    wait_freed(pe, TILE["qup"] + g)
                    if g >= 2:
                        pe.wait_ge(qrope_done, g - 1)
                    nc.tensor.matmul(acc4[0:QK_2, g % 2], rot2, q2[0:QK_2, 2 * g:2 * g + 2], start=True,
                                     stop=True).then_inc(qrot_done, 1)
            attention(4, 8, TILE["att2"], q2, k2, v2, QK_2, V_2, ws2, lambda g: (
                pe.wait_ge(qrope_done, 8), pe.wait_ge(kb_done, 1), wait_freed(pe, TILE["kvup"] + 11)))
            for n in range(KT):
                column_unit(UNIT["zm"] + n, TILE["zm"] + n, x_hi, x_lo)

            def ssm_b_step(s):
                if s == 0:
                    pe.wait_ge(b_in, 16)
                if s >= 2:
                    pe.wait_ge(bu_free, s - 1)
                f, jj = s // 2, 2 * (s % 2)
                for j in range(2):
                    r = 32 * (jj + j)
                    for c in range(2):
                        m = nc.tensor.matmul(acc4[:, jj + j, c * T:(c + 1) * T], b_sb[r:r + 32, c, f],
                                             uT[r:r + 32, f], start=True, stop=True)
                m.then_inc(bu_done, 1)

            def ssm_c_step(s):
                f, jj = s // 2, 2 * (s % 2)
                if s == 0:
                    pe.wait_ge(cc_done, 1)
                if s % 2 == 0 and f >= 1:
                    pe.wait_ge(yp_done, f)
                pe.wait_ge(zz_done, s + 1)
                for j in range(2):
                    r = 32 * (jj + j)
                    for c in range(2):
                        m = nc.tensor.matmul(nrm[r:r + 32, (f % 2) * T:(f % 2 + 1) * T], cc[:, c, 4 * f + jj + j],
                                             ssm_v[s % 2][:, c, j], start=(c == 0), stop=(c == 1))
                m.then_inc(y_done, 1)

            ssm_b_step(0)
            for s in range(16):
                for nm, n in GATES[2 * s:2 * s + 2]:
                    if nm == "brm" and n == 0:
                        pe.wait_ge(al_done, 4 + 8)
                    hi, lo = (a_hi, a_lo) if nm == "brm" else (x_hi, x_lo)
                    column_unit(UNIT[nm] + n, TILE[nm] + n, hi, lo)
                if s + 1 < 16:
                    ssm_b_step(s + 1)
                ssm_c_step(s)
            for n in range(16):
                if n == 0:
                    pe.wait_ge(al_done, 12 + 8)
                column_unit(UNIT["glu"] + n, TILE["glu"] + n, a_hi, a_lo)
            for n in range(KT):
                if n == 0:
                    pe.wait_ge(xl_done, KT * SPLITS[7] + KT)
                column_unit(UNIT["brs"] + n, TILE["brs"] + n, x_hi, x_lo)
            for n in range(KT):
                if n == 0:
                    pe.wait_ge(al_done, 20 + 8)
                column_unit(UNIT["out"] + n, TILE["out"] + n, a_hi, a_lo)
            sum_squares(7)

        @block.scalar
        def _(act):
            chain = [0]

            def link(ins):
                chain[0] += 1
                ins.then_inc(act_s, 1)
                act.wait_ge(act_s, chain[0])

            def split(name, a, b):
                for n in range(a, b):
                    split_hi(act, UNIT[name] + n)

            def squares(n, ready):
                for k in range(KT):
                    ready(k)
                    nc.scalar.square(t_buf[:, k], x[:, k]).then_inc(sq_done, 1)
                act.wait_ge(nrm_done, n + 1)
                nc.scalar.activation(rx, nrm[:, 0:T], ACT.Sqrt, bias=con("eps", 1), scale=1.0 / D).then_inc(rt_done, 1)

            def norm_hi(stage):
                n = SPLITS[stage] - 1
                for k in range(KT):
                    act.wait_ge(t_done, KT * n + k + 1)
                    nc.scalar.activation(x_hi[:, k], t_buf[:, k], ACT.Identity,
                                         bias=coef[:, stage, 8 + k:9 + k]).then_inc(xh_done, 1)

            def silu_step(f, j, u, i, per):
                act.wait_ge(used, i * 12 + (u + 1))
                if j >= 2 or per:
                    nd = OWNER[:TILE[f"ffn{f}"]].count("d")
                    if nd + j - 1 > 0:
                        act.wait_ge(freed["d"], i * per + (nd + j - 1))
                nc.scalar.activation(silu_b[:, j % 2], tiles[:, j % 2, 0:T], ACT.Silu).then_inc(silu_done, 1)

            def ffn(f, pre):
                base = FFN_BASE[f]
                for s in range(pre, 4):
                    split_hi(act, base + s)
                split_hi(act, base + 4)
                silu_step(f, 0, base + 1, 0, 0)
                j0 = 2
                for reps, _ in SEGMENTS[f]:
                    with act.Fori(0, reps) as i:
                        for m in range(4):
                            u = g_unit(base, j0 + m)
                            for s in range(3):
                                split_hi(act, u + s, i)
                            silu_step(f, j0 + m - 1, g_unit(base, j0 + m - 1) + 1, i, 4)
                    j0 += 4 * reps
                split_hi(act, o_unit(base, 21))
                silu_step(f, 21, g_unit(base, 21) + 1, 0, 0)

            def head_square(n, src):
                if n:
                    act.wait_ge(hs_done, n)
                nc.scalar.square(rope_sq, src).then_inc(hsq_done, 1)

            def head_root(n):
                act.wait_ge(hs_done, n + 1)
                if n:
                    act.wait_ge(kn_done, n)
                nc.scalar.activation(rh[:], acc4[:, n % 2], ACT.Sqrt, bias=con("eps", 1),
                                     scale=1.0 / HEAD_DIM).then_inc(hrt_done, 1)

            def evacuate(o, src, dst, func=ACT.Copy, **kw):
                wait_tile(act, o)
                nc.scalar.activation(dst, src, func, **kw).then_inc(freed["a"], 1)

            def tile_of(name, n):
                return tiles[:, (TILE[name] + n) % 2, 0:T]

            def exps(n, g, ws, scale):
                sm, pt = ws[g % 2]
                act.wait_ge(mx_done, n + 1)
                for r in range(4):
                    nc.scalar.activation(sm[:, r], sm[:, r], ACT.Exp, bias=att_s[:, g % 2, 4 + r:5 + r], scale=scale,
                                         accum_out=att_s[:, g % 2, 8 + r:9 + r]).then_inc(ex_done, 1)

            def probs_t(n, g, ws, o0):
                sm, pt = ws[g % 2]
                act.wait_ge(pt_done, n + 1)
                if g >= 2:
                    wait_tile(act, o0 + g - 2)
                nc.scalar.copy(pt, acc4[:, 2:4, 0:384]).then_inc(pe_done, 1)

            act.wait_ge(vec_in, 16)
            nc.scalar.activation(csil[:], vec("c", 0, 8), ACT.Silu).then_inc(csilu_done, 1)
            link(nc.scalar.activation(ssm_s[:, 0], vec("logdt", 0, 32), ACT.Exp))
            act.wait_ge(ang_done, 1)
            link(nc.scalar.activation(ssm_s[:, 1], ssm_s[:, 2], ACT.Exp))
            act.wait_ge(ang_done, 2)
            nc.scalar.activation(ssm_s[:, 5:7], ssm_s[:, 3:5], ACT.Sin).then_inc(sin_done, 1)
            act.wait_ge(con_in, 16)
            for k in range(3):
                split_hi(act, k)
            squares(0, lambda k: act.wait_ge(x_in, 16))
            norm_hi(0)
            ffn(0, 3)
            split("pool", 0, 2)
            split_hi(act, UNIT["ffn1"])
            squares(1, lambda k: act.wait_ge(x_upd, k + 1))
            for k in range(KT):
                act.wait_ge(t_done, KT + k + 1)
                nc.scalar.copy(x_hi[:, k], t_buf[:, k]).then_inc(xh_done, 1)
            for s in range(1, 4):
                split_hi(act, UNIT["ffn1"] + s)
            squares(2, lambda k: wait_freed(act, TILE["pool"] + k))
            norm_hi(2)
            ffn(1, 4)
            split("kv", 0, 4)
            squares(3, lambda k: act.wait_ge(x_upd, KT + k + 1))
            norm_hi(3)
            for h in range(HEADS_1):
                split_hi(act, UNIT["kv"] + h + 4)
                evacuate(TILE["k"] + h, tile_of("k", h), kT[:, h])
                if h % 2 == 1:
                    wait_freed(act, TILE["k"] + h)
                    head_square(h // 2, kT[:, h - 1:h + 1])
                if h in (4, 6):
                    head_root(h // 2 - 2)
            for h in range(HEADS_1):
                split_hi(act, UNIT["kv"] + 12 + h)
                wait_tile(act, TILE["v"] + h)
                nc.scalar.copy(v1[:, :, h * P:(h + 1) * P],
                               tile_of("v", h).rearrange("p (t c) -> p t c", t=2)).then_inc(freed["a"], 1)
                if h in (0, 2):
                    head_root(2 + h // 2)
            norm_hi(4)
            ffn(2, 4)
            split("q", 0, 4)
            squares(4, lambda k: act.wait_ge(x_upd, 2 * KT + k + 1))
            norm_hi(5)
            for h in range(HEADS_1):
                split_hi(act, UNIT["q"] + h + 4)
                evacuate(TILE["q"] + h, tile_of("q", h), qT[:, h])
                if h % 2 == 1:
                    wait_freed(act, TILE["q"] + h)
                    head_square(4 + h // 2, qT[:, h - 1:h + 1])
                if h in (4, 6):
                    head_root(4 + h // 2 - 2)
            head_root(6)
            head_root(7)

            def att_hi(g):
                wait_tile(act, TILE["att1"] + g)
                nc.scalar.copy(a_hi[:, 2 * g:2 * g + 2],
                               tiles[:, (TILE["att1"] + g) % 2].rearrange("p (h t) -> p h t", h=2)).then_inc(ah_done, 2)

            exps(0, 0, ws1, HEAD_DIM ** -0.5)
            for g in range(4):
                if g < 3:
                    exps(g + 1, g + 1, ws1, HEAD_DIM ** -0.5)
                probs_t(g, g, ws1, TILE["att1"])
                if g:
                    att_hi(g - 1)
            att_hi(3)
            for n in range(4, 8):
                split_hi(act, UNIT["o"] + n)
            for s in range(4):
                split_hi(act, UNIT["ffn3"] + s)
            squares(5, lambda k: wait_freed(act, TILE["o"] + k))
            norm_hi(6)
            ffn(3, 4)
            split("lat", 0, 4)
            squares(6, lambda k: act.wait_ge(x_upd, 3 * KT + k + 1))
            norm_hi(7)
            next_unit = [UNIT["lat"] + 4]

            def ahead(n=1):
                for _ in range(n):
                    if next_unit[0] < N_UNITS:
                        split_hi(act, next_unit[0])
                        next_unit[0] += 1

            for n in range(4):
                ahead()
                evacuate(TILE["lat"] + n, tile_of("lat", n), lat_raw[:, n])
                wait_freed(act, TILE["lat"] + n)
                nc.scalar.square(lat_sq[:, n], lat_raw[:, n]).then_inc(lsq_done, 1)
            ahead()
            evacuate(TILE["kr"], tile_of("kr", 0)[0:QK_2], kr_buf[0:QK_2, 0])
            act.wait_ge(ang_done, 3)
            nc.scalar.activation(rope2[64:96], ang[64:96, 0:2], ACT.Sin).then_inc(sin_done, 1)
            for n in range(KT):
                ahead()
                evacuate(TILE["u"] + n, tile_of("u", n), uT[:, n])
                if n == 1:
                    act.wait_ge(lsum_done, 1)
                    nc.scalar.activation(rh[:], nrm[:], ACT.Sqrt, bias=con("eps", 1), scale=1.0 / 256).then_inc(lrt_done, 1)
                if n == 3:
                    for k in range(4):
                        act.wait_ge(af_done, k + 1)
                        nc.scalar.copy(a_hi[:, k], lat_n[:, k]).then_inc(ah_done, 1)
            for g in range(8):
                if g % 2 == 0:
                    ahead()
                o = TILE["qup"] + g
                evacuate(o, tiles[0:QK_2, o % 2].rearrange("p (h t) -> p h t", h=2), q2[0:QK_2, 2 * g:2 * g + 2])
            for n in range(4):
                ahead()
                for pair in range(2):
                    o = TILE["kvup"] + 3 * n + pair
                    h = 4 * n + 2 * pair
                    evacuate(o, tiles[0:64, o % 2].rearrange("p (h t) -> p h t", h=2), k2[0:64, h:h + 2])
                o = TILE["kvup"] + 3 * n + 2
                evacuate(o, tiles[:, o % 2].rearrange("p (t c) -> p t c", t=2), v2[:, :, 256 * n:256 * (n + 1)])
            exps(4, 0, ws2, QK_2 ** -0.5)
            for g in range(8):
                if g < 7:
                    exps(5 + g, g + 1, ws2, QK_2 ** -0.5)
                probs_t(4 + g, g, ws2, TILE["att2"])
            for n in range(KT):
                ahead()
                evacuate(TILE["zm"] + n, tile_of("zm", n), t_buf[:, n], ACT.Silu)
                if n >= 1:
                    act.wait_ge(af_done, 4 + n)
                    nc.scalar.copy(a_hi[:, n - 1], ym[:, n - 1]).then_inc(ah_done, 1)
            act.wait_ge(af_done, 4 + KT)
            nc.scalar.copy(a_hi[:, 7], ym[:, 7]).then_inc(ah_done, 1)

            def gelu_tile(f):
                act.wait_ge(yp_done, f + 1)
                nc.scalar.activation(gel[:, f], gel[:, f], ACT.Gelu_apprx_tanh).then_inc(gel_done, 1)

            def gelu_hi(f):
                act.wait_ge(gel_done, f + 1)
                nc.scalar.copy(a_hi[:, f], gel[:, f]).then_inc(ah_done, 1)

            act.wait_ge(al_done, 12)
            for s in range(16):
                for nm, n in GATES[2 * s:2 * s + 2]:
                    ahead()
                    o = TILE[nm] + n
                    if nm == "brm":
                        evacuate(o, tile_of(nm, n), mrg[:, n])
                    elif nm == "glm":
                        if n >= 2:
                            act.wait_ge(glm_used, n - 1)
                        evacuate(o, tile_of(nm, n), glm_t[:, n % 2], ACT.Sigmoid)
                    elif nm == "zs":
                        if n == 0:
                            act.wait_ge(cc_done, 1)
                        evacuate(o, tile_of(nm, n), zs_t[:, n], ACT.Silu)
                    else:
                        evacuate(o, tile_of(nm, n), gs_t[:, n], ACT.Sigmoid)
                for f in {9: (0, 1, 2, 3), 15: (4, 5, 6)}.get(s, ()):
                    gelu_tile(f)
                for f in {9: (0, 1, 2, 3), 15: (4, 5, 6)}.get(s, ()):
                    gelu_hi(f)
            gelu_tile(7)
            gelu_hi(7)
            for n in range(KT):
                ahead(2)
                if n >= 2:
                    act.wait_ge(gv_done, n - 1)
                evacuate(TILE["glu"] + 2 * n + 1, tile_of("glu", 2 * n + 1), sig_t[:, n % 2], ACT.Sigmoid,
                         bias=vec("b_glu", 8 + n))
                if n >= 1:
                    act.wait_ge(gv_done, n)
                    nc.scalar.copy(x_hi[:, n - 1], gel[:, n - 1]).then_inc(xh_done, 1)
            act.wait_ge(gv_done, KT)
            nc.scalar.copy(x_hi[:, 7], gel[:, 7]).then_inc(xh_done, 1)
            for n in range(KT):
                ahead()
                act.wait_ge(af_done, 12 + n + 1)
                nc.scalar.copy(a_hi[:, n], mrg[:, n]).then_inc(ah_done, 1)
            for n in range(KT):
                ahead()
                evacuate(TILE["out"] + n, tile_of("out", n), o_raw[:, n])
                wait_freed(act, TILE["out"] + n)
                nc.scalar.square(t_buf[:, n], o_raw[:, n]).then_inc(sq_done, 1)
            act.wait_ge(nrm_done, 8)
            nc.scalar.activation(rx, nrm[:, 0:T], ACT.Sqrt, bias=con("eps", 1), scale=1.0 / D).then_inc(rt_done, 1)

        @block.vector
        def _(dve):
            chain = [0]
            blocks = [G_PRE]
            V = nc.vector

            def link(ins):
                chain[0] += 1
                ins.then_inc(dve_s, 1)
                dve.wait_ge(dve_s, chain[0])

            def g_part(b, k, vector, i=0):
                cv = csil[:, k:k + 1] if vector == "silu" else vec("c2", k)
                acc, rows = g_acc[:, b % 2], g_land[:, b % 2, k]
                if k == 0:
                    dve.wait_ge(g_landed[b % 2], i * 16 + 16 * (b // 2 + 1))
                    if b >= 2:
                        dve.wait_ge(g_red, i * 2 + (b - 1))
                    V.tensor_scalar(acc, rows, cv, None, ALU.mult).then_inc(g_step, 1)
                else:
                    dve.wait_ge(g_step, i * 14 + (7 * b + k))
                    V.scalar_tensor_tensor(out=acc, in0=rows, scalar=cv, in1=acc, op0=ALU.mult,
                                           op1=ALU.add).then_inc(g_done if k == 7 else g_step, 1)

            def g_block(b):
                for k in range(8):
                    g_part(b, k, "silu")

            def hidden(f, j, i, per):
                base, nd = FFN_BASE[f], OWNER[:TILE[f"ffn{f}"]].count("d")
                J = FFN_TILES * f + j
                dve.wait_ge(silu_done, i * per + (J + 1))
                V.tensor_tensor(hid[:, j % 2], silu_b[:, j % 2], tiles[:, j % 2, T:2 * T],
                                ALU.mult).then_inc(freed["d"], 1)
                dve.wait_ge(freed["d"], i * per + (nd + j + 1))
                if j >= 2 or per:
                    dve.wait_ge(used, i * 12 + (base + 3 * (j - 2) + 4 + 1))
                V.tensor_copy(h_hi[:, j % 2], hid[:, j % 2]).then_inc(hh_done, 1)
                dve.wait_ge(hh_done, i * per + (J + 1))
                V.tensor_tensor(h_lo[:, j % 2], hid[:, j % 2], h_hi[:, j % 2].bitcast(F32),
                                ALU.subtract).then_inc(h_done, 1)

            def gate_coef(stage, col, weight):
                dve.wait_ge(g_red, blocks[0])
                link(V.tensor_tensor(coef[:, stage, 24:32], mods[:, col:col + 8], vec("bias", col, 8), ALU.add))
                if isinstance(weight, float):
                    link(V.tensor_scalar(coef[:, stage, 16:24], coef[:, stage, 24:32], 1.0, weight, ALU.add, ALU.mult))
                else:
                    link(V.scalar_tensor_tensor(out=coef[:, stage, 16:24], in0=coef[:, stage, 24:32], scalar=1.0,
                                                in1=weight, op0=ALU.add, op1=ALU.mult))

            def norm_coef(stage):
                sh, sc, (gname, g0) = STAGE[stage]
                dve.wait_ge(g_red, blocks[0])
                link(V.tensor_tensor(coef[:, stage, 24:32], mods[:, sc:sc + 8], vec("bias", sc, 8), ALU.add))
                link(V.scalar_tensor_tensor(out=coef[:, stage, 0:8], in0=coef[:, stage, 24:32], scalar=1.0,
                                            in1=vec(gname, g0, 8), op0=ALU.add, op1=ALU.mult))
                link(V.tensor_tensor(coef[:, stage, 8:16], mods[:, sh:sh + 8], vec("bias", sh, 8), ALU.add))

            def root(n):
                dve.wait_ge(rt_done, n + 1)
                link(V.reciprocal(rx, rx))

            def norm_t(stage):
                for k in range(KT):
                    V.scalar_tensor_tensor(out=t_buf[:, k], in0=x[:, k], scalar=coef[:, stage, k:k + 1], in1=rx,
                                           op0=ALU.mult, op1=ALU.mult).then_inc(t_done, 1)
                    if k >= 1:
                        norm_lo(stage, k - 1)
                norm_lo(stage, KT - 1)

            def norm_lo(stage, k):
                n = SPLITS[stage] - 1
                dve.wait_ge(xh_done, KT * n + k + 1)
                dve.wait_ge(t_done, KT * n + k + 1)
                V.scalar_tensor_tensor(out=x_lo[:, k], in0=t_buf[:, k], scalar=coef[:, stage, 8 + k:9 + k],
                                       in1=x_hi[:, k].bitcast(F32), op0=ALU.add, op1=ALU.subtract).then_inc(xl_done, 1)

            def update(k, src, stage, signal):
                V.scalar_tensor_tensor(out=x[:, k], in0=src, scalar=coef[:, stage, 16 + k:17 + k], in1=x[:, k],
                                       op0=ALU.mult, op1=ALU.add).then_inc(signal, 1)

            def ffn(f, stage, pre, gate_col, ahead_units):
                base, b = FFN_BASE[f], G_FFN[f]
                for s in range(pre, 5):
                    split_lo(dve, base + s)
                hidden(f, 0, 0, 0)
                if G_FIRST[f]:
                    g_block(b)
                    b += 1
                j0 = 2
                for reps, vector in SEGMENTS[f]:
                    with dve.Fori(0, reps) as i:
                        for m in range(4):
                            j, u = j0 + m, g_unit(base, j0 + m)
                            for s in range(3):
                                split_lo(dve, u + s, i)
                                if vector:
                                    g_part(b + m // 2, 4 * (m % 2) + s, vector, i)
                            hidden(f, j - 1, i, 4)
                            if vector:
                                g_part(b + m // 2, 4 * (m % 2) + 3, vector, i)
                    j0 += 4 * reps
                    b += 2 * reps if vector else 0
                blocks[0] = b
                split_lo(dve, o_unit(base, 21))
                hidden(f, 21, 0, 0)
                for u in ahead_units:
                    split_lo(dve, u)
                gate_coef(stage, gate_col, 0.5)
                dve.wait_ge(used, base + 66)
                for k in range(KT):
                    update(k, yT[k], stage, x_upd)

            def reduce_angle(th, out_s, out_c, tmp, tmp2):
                for out_, quarter in ((out_s, 0.0), (out_c, 0.25)):
                    link(V.tensor_scalar(tmp, th, 1.0 / TWO_PI, quarter, ALU.mult, ALU.add))
                    link(V.tensor_scalar(tmp, tmp, 12582912.0, None, ALU.add))
                    link(V.tensor_scalar(tmp, tmp, -12582912.0, None, ALU.add))
                    link(V.scalar_tensor_tensor(out=tmp2, in0=tmp, scalar=-6.28125, in1=th, op0=ALU.mult, op1=ALU.add))
                    link(V.scalar_tensor_tensor(out=tmp2, in0=tmp, scalar=-0.0019350051879882812, in1=tmp2,
                                                op0=ALU.mult, op1=ALU.add))
                    link(V.scalar_tensor_tensor(out=tmp2, in0=tmp, scalar=-(TWO_PI - 6.28125 - 0.0019350051879882812),
                                                in1=tmp2, op0=ALU.mult, op1=ALU.add))
                    link(V.tensor_scalar(tmp2, tmp2, quarter * TWO_PI, 3.1415925, ALU.add, ALU.min))
                    link(V.tensor_scalar(out_, tmp2, -3.1415925, None, ALU.max))

            dve.wait_ge(act_s, 1)
            S = lambda n: ssm_s[:, n]
            lr, li = vec("lr", 0, 32), vec("li", 0, 32)
            V.tensor_tensor(S(2), lr, S(0), ALU.mult).then_inc(ang_done, 1)
            link(V.tensor_tensor(S(7), li, S(0), ALU.mult))
            reduce_angle(S(7), S(4), S(3), S(8), S(9))
            V.tensor_copy(S(19), S(8)).then_inc(ang_done, 1)
            dve.wait_ge(act_s, 2)
            dve.wait_ge(sin_done, 1)
            link(V.tensor_tensor(S(10), S(1), S(5), ALU.mult))
            link(V.tensor_scalar(S(10), S(10), -1.0, None, ALU.add))
            link(V.tensor_tensor(S(11), S(1), S(6), ALU.mult))
            link(V.tensor_tensor(S(12), lr, lr, ALU.mult))
            link(V.tensor_tensor(S(13), li, li, ALU.mult))
            link(V.tensor_tensor(S(12), S(12), S(13), ALU.add))
            link(V.reciprocal(S(12), S(12)))
            link(V.tensor_tensor(S(13), S(10), lr, ALU.mult))
            link(V.tensor_tensor(S(14), S(11), li, ALU.mult))
            link(V.tensor_tensor(S(13), S(13), S(14), ALU.add))
            link(V.tensor_tensor(S(13), S(13), S(12), ALU.mult))
            link(V.tensor_tensor(S(14), S(11), lr, ALU.mult))
            link(V.tensor_tensor(S(15), S(10), li, ALU.mult))
            link(V.tensor_tensor(S(14), S(14), S(15), ALU.subtract))
            V.tensor_tensor(S(14), S(14), S(12), ALU.mult).then_inc(f_done, 1)
            dve.wait_ge(csilu_done, 1)
            dve.wait_ge(vec_in, 16)
            for b in range(G_PRE):
                g_block(b)
                if b < 3:
                    split_lo(dve, b)
            norm_coef(0)
            root(0)
            norm_t(0)

            def rng(name, a, b):
                return range(UNIT[name] + a, UNIT[name] + b)

            def split(units):
                for u in units:
                    split_lo(dve, u)

            ffn(0, 0, 3, 16, [*rng("pool", 0, 2), UNIT["ffn1"]])

            g_block(G_PRE + 11)
            blocks[0] += 1
            norm_coef(1)
            gate_coef(1, 40, vec("pool_scale", 0, 8))
            dve.wait_ge(base_done, 1)
            link(V.memset(win_h[:, :, 0:PAD], 0.0))
            link(V.memset(win_a[:, :, 0:PAD], 0.0))
            link(V.memset(win_b[:, :, 0:PAD], 0.0))
            root(1)
            for k in range(KT):
                link(V.scalar_tensor_tensor(out=win_h[:, k, PAD:], in0=x[:, k], scalar=coef[:, 1, k:k + 1], in1=rx,
                                            op0=ALU.mult, op1=ALU.mult))
            for k in range(KT):
                link(V.tensor_scalar(win_h[:, k, PAD:], win_h[:, k, PAD:], coef[:, 1, 8 + k:9 + k], None, ALU.add))
            for g, w in enumerate(POOL_W):
                k0 = 2 * g
                src, dst = win_h[:, k0:k0 + 2], win_a[:, k0:k0 + 2]
                for level in range(g + 1):
                    sh = 1 << level
                    link(V.tensor_tensor(dst[:, :, PAD:], src[:, :, PAD:], src[:, :, PAD - sh:PAD + T - sh], ALU.add))
                    src, dst = dst, (win_b[:, k0 - 2:k0] if level % 2 == 0 and g else win_a[:, k0:k0 + 2])
                h2, t2 = win_h[:, k0:k0 + 2], t_buf[:, k0:k0 + 2]
                link(V.scalar_tensor_tensor(out=t2, in0=src[:, :, PAD:], scalar=1.0 / w, in1=h2[:, :, PAD:],
                                            op0=ALU.mult, op1=ALU.subtract))
                cnt = cons[:, CON["cnt"] + 16 * g:CON["cnt"] + 16 * (g + 1)].unsqueeze(1).to_broadcast([P, 2, 16])
                link(V.tensor_tensor(t2[:, :, 0:16], src[:, :, PAD:PAD + 16], cnt, ALU.mult))
                V.tensor_tensor(t2[:, :, 0:16], t2[:, :, 0:16], h2[:, :, PAD:PAD + 16], ALU.subtract).then_inc(t_done, 2)
                dve.wait_ge(t_done, KT + k0 + 2)
                dve.wait_ge(xh_done, KT + k0 + 2)
                V.tensor_tensor(x_lo[:, k0:k0 + 2], t2, x_hi[:, k0:k0 + 2].bitcast(F32), ALU.subtract).then_inc(xl_done, 2)
            for k in range(KT):
                if 1 <= k <= 3:
                    split_lo(dve, UNIT["ffn1"] + k)
                wait_tile(dve, TILE["pool"] + k)
                update(k, tiles[:, k % 2, 0:T], 1, freed["d"])
            norm_coef(2)
            root(2)
            norm_t(2)
            ffn(1, 2, 4, 64, rng("kv", 0, 4))

            def head_norm(n, raw, weight):
                dve.wait_ge(hrt_done, n + 1)
                link(V.reciprocal(rh[:], rh[:]))
                V.scalar_tensor_tensor(out=rope_kn, in0=raw, scalar=weight, in1=rh[:].rearrange("p (h t) -> p h t", h=2),
                                       op0=ALU.mult, op1=ALU.mult).then_inc(kn_done, 1)
                dve.wait_ge(kn_done, n + 1)
                V.tensor_tensor(rope_t[:, 0], rope_kn, cos1.unsqueeze(1).to_broadcast([P, 2, T]), ALU.mult)

            def head_rope(n, raw):
                dve.wait_ge(hrot_done, n + 1)
                link(V.tensor_tensor(rope_t[:, 1], acc4[:, 2 + n % 2].rearrange("p (h t) -> p h t", h=2),
                                     sin1.unsqueeze(1).to_broadcast([P, 2, T]), ALU.mult))
                V.tensor_tensor(raw, rope_t[:, 0], rope_t[:, 1], ALU.add).then_inc(rope_done, 1)

            norm_coef(3)
            root(3)
            norm_t(3)
            for h in range(HEADS_1):
                split_lo(dve, UNIT["kv"] + h + 4)
                if h in (5, 7):
                    head_rope((h - 5) // 2, kT[:, h - 5:h - 3])
                if h in (4, 6):
                    head_norm(h // 2 - 2, kT[:, h - 4:h - 2], vec("k_norm"))
            norm_coef(4)
            for h in range(HEADS_1):
                split_lo(dve, UNIT["kv"] + h + 12)
                if h in (0, 2):
                    head_norm(2 + h // 2, kT[:, 4 + h:6 + h], vec("k_norm"))
                if h in (1, 3):
                    head_rope(2 + h // 2, kT[:, 3 + h:5 + h])
            dve.wait_ge(used, UNIT["ffn2"])
            norm_t(4)
            ffn(2, 4, 4, 104, rng("q", 0, 4))

            def scores_max(n, g, ws):
                sm, pt = ws[g % 2]
                scale = HEAD_DIM ** -0.5 if n < 4 else QK_2 ** -0.5
                dve.wait_ge(s_done, n + 1)
                if g >= 2:
                    dve.wait_ge(pt_done, n - 1)
                V.tensor_tensor(sm.rearrange("p (h q) t -> p h (q t)", h=2), acc4[:, 0:2],
                                con("mask", 2 * T).unsqueeze(1).to_broadcast([P, 2, 2 * T]), ALU.add).then_inc(sm_done, 1)
                dve.wait_ge(sm_done, n + 1)
                link(V.tensor_reduce(att_s[:, g % 2, 0:4], sm, AX, ALU.max))
                V.tensor_scalar(att_s[:, g % 2, 4:8], att_s[:, g % 2, 0:4], -scale, None, ALU.mult).then_inc(mx_done, 1)

            def normalise(n, g, ws):
                sm, pt = ws[g % 2]
                dve.wait_ge(ex_done, 4 * (n + 1))
                link(V.reciprocal(att_s[:, g % 2, 12:16], att_s[:, g % 2, 8:12]))
                for r in range(4):
                    V.tensor_scalar(sm[:, r], sm[:, r], att_s[:, g % 2, 12 + r:13 + r], None, ALU.mult).then_inc(pn_done, 1)

            def att_lo(g):
                dve.wait_ge(ah_done, 2 * g + 2)
                V.tensor_tensor(a_lo[:, 2 * g:2 * g + 2], tiles[:, (TILE["att1"] + g) % 2].rearrange("p (h t) -> p h t", h=2),
                                a_hi[:, 2 * g:2 * g + 2].bitcast(F32), ALU.subtract).then_inc(freed["d"], 1)

            norm_coef(5)
            root(4)
            norm_t(5)
            for h in range(HEADS_1):
                split_lo(dve, UNIT["q"] + h + 4)
                if h in (5, 7):
                    head_rope(4 + (h - 5) // 2, qT[:, h - 5:h - 3])
                if h in (4, 6):
                    head_norm(4 + h // 2 - 2, qT[:, h - 4:h - 2], vec("q_norm"))
            for n in (6, 7):
                head_norm(n, qT[:, 2 * (n - 4):2 * (n - 4) + 2], vec("q_norm"))
                head_rope(n, qT[:, 2 * (n - 4):2 * (n - 4) + 2])
            scores_max(0, 0, ws1)
            for g in range(4):
                if g < 3:
                    scores_max(g + 1, g + 1, ws1)
                normalise(g, g, ws1)
                if g:
                    att_lo(g - 1)
            att_lo(3)
            gate_coef(5, 128, 1.0)
            for k in range(KT):
                split_lo(dve, UNIT["o"] + 4 + k)
                wait_tile(dve, TILE["o"] + k)
                update(k, tiles[:, k % 2, 0:T], 5, freed["d"])
            norm_coef(6)
            root(5)
            norm_t(6)
            ffn(3, 6, 4, 152, rng("lat", 0, 4))

            next_unit = [UNIT["lat"] + 4]

            def ahead(n=1):
                for _ in range(n):
                    if next_unit[0] < N_UNITS:
                        split_lo(dve, next_unit[0])
                        next_unit[0] += 1

            def a_part(k, src, ah, signal):
                dve.wait_ge(ah_done, ah)
                V.tensor_tensor(a_lo[:, k], src, a_hi[:, k].bitcast(F32), ALU.subtract).then_inc(signal, 1)

            norm_coef(7)
            root(6)
            norm_t(7)
            R = slice(64, 96)
            dve.wait_ge(xl_done, KT * SPLITS[7])
            dve.wait_ge(pos_in, 16)
            link(V.tensor_copy(ang[R, 2], pos_i[R].bitcast(I32)))
            link(V.tensor_scalar(ang[R, 3], ang[R, 2], con("invf", 1)[R], None, ALU.mult))
            reduce_angle(ang[R, 3], ang[R, 1], ang[R, 0], ang[R, 4], ang[R, 5])
            V.memset(rope2[0:64, 0], 1.0)
            V.memset(rope2[0:64, 1], 0.0)
            V.tensor_copy(ang[R, 5], ang[R, 4]).then_inc(ang_done, 1)
            ahead(5)
            for n in range(KT):
                ahead()
                if n == 2:
                    dve.wait_ge(lrt_done, 1)
                    link(V.reciprocal(rh[:], rh[:]))
                    for k in range(4):
                        V.scalar_tensor_tensor(out=lat_n[:, k], in0=lat_raw[:, k],
                                               scalar=vec("g_q", k) if k < 2 else vec("g_kv", k - 2),
                                               in1=rh[:, (k // 2) * T:(k // 2 + 1) * T], op0=ALU.mult,
                                               op1=ALU.mult).then_inc(af_done, 1)
                if n == 4:
                    dve.wait_ge(krot_done, 1)
                    dve.wait_ge(sin_done, 2)
                    V.tensor_tensor(kr_buf[R, 1], kr_buf[R, 0], rope2[R, 0], ALU.mult)
                    link(V.tensor_tensor(kr_buf[R, 2], acc4[R, 2, 0:T], rope2[R, 1], ALU.mult))
                    V.tensor_tensor(kr_buf[R, 1], kr_buf[R, 1], kr_buf[R, 2], ALU.add).then_inc(kr_done, 1)
                    dve.wait_ge(af_done, 4)
                    for k in range(4):
                        a_part(k, lat_n[:, k], 8 + k + 1, al_done)
            for n in range(4):
                ahead()

            def q_rope(g):
                pair = q2[0:QK_2, 2 * g:2 * g + 2]
                c2, s2 = (rope2[:, n].unsqueeze(1).to_broadcast([QK_2, 2, T]) for n in range(2))
                if g:
                    dve.wait_ge(qrope_done, g)
                dve.wait_ge(qrot_done, g + 1)
                V.tensor_tensor(rope_t[0:QK_2, 0], pair, c2, ALU.mult)
                link(V.tensor_tensor(rope_t[0:QK_2, 1], acc4[0:QK_2, g % 2].rearrange("p (h t) -> p h t", h=2), s2, ALU.mult))
                V.tensor_tensor(pair, rope_t[0:QK_2, 0], rope_t[0:QK_2, 1], ALU.add).then_inc(qrope_done, 1)

            for n in range(4):
                ahead()
                q_rope(2 * n)
                q_rope(2 * n + 1)

            def att2_out(g):
                wait_tile(dve, TILE["att2"] + g)
                V.tensor_copy(ym[:, g], tiles[:, (TILE["att2"] + g) % 2, 0:T]).then_inc(freed["d"], 1)

            dve.wait_ge(mask_in, 16)
            scores_max(4, 0, ws2)
            for g in range(8):
                if g < 7:
                    scores_max(5 + g, g + 1, ws2)
                normalise(4 + g, g, ws2)
                if g:
                    att2_out(g - 1)
            att2_out(7)
            wait_freed(dve, TILE["att2"] + 7)
            for n in range(KT):
                ahead()
                wait_freed(dve, TILE["zm"] + n)
                V.tensor_tensor(ym[:, n], ym[:, n], t_buf[:, n], ALU.mult).then_inc(af_done, 1)
                if n:
                    dve.wait_ge(af_done, 4 + n)
                    a_part(n - 1, ym[:, n - 1], 12 + n, al_done)
            dve.wait_ge(af_done, 12)
            a_part(7, ym[:, 7], 20, al_done)

            def ssm_step(s):
                f, jj = s // 2, 2 * (s % 2)
                cs, sn = rot_t[s % 2][:, 0], rot_t[s % 2][:, 1]
                v, (m0, m1) = ssm_v[s % 2], (ssm_m[:, 0], ssm_m[:, 1])
                bur, bui = acc4[:, jj:jj + 2, 0:T], acc4[:, jj:jj + 2, T:2 * T]
                dve.wait_ge(tab_done, s + 1)
                dve.wait_ge(bu_done, s + 1)
                if s >= 2:
                    dve.wait_ge(y_done, s - 1)
                V.tensor_tensor(v[:, 0], bur, cs, ALU.mult)
                V.tensor_tensor(m0, bui, sn, ALU.mult)
                V.tensor_tensor(v[:, 1], bui, cs, ALU.mult)
                link(V.tensor_tensor(m1, bur, sn, ALU.mult))
                V.tensor_tensor(v[:, 0], v[:, 0], m0, ALU.add).then_inc(bu_free, 1)
                link(V.tensor_tensor(v[:, 1], v[:, 1], m1, ALU.subtract))
                for c in range(2):
                    for j in range(2):
                        mag = ssm_s[:, 1, 4 * f + jj + j:4 * f + jj + j + 1].to_broadcast([P, T])
                        m = V.tensor_tensor_scan(v[:, c, j], mag, v[:, c, j], 0.0, ALU.mult, ALU.add)
                link(m)
                V.tensor_tensor(m0, v[:, 1], sn, ALU.mult)
                link(V.tensor_tensor(m1, v[:, 0], sn, ALU.mult))
                V.tensor_tensor(v[:, 0], v[:, 0], cs, ALU.mult)
                V.tensor_tensor(v[:, 1], v[:, 1], cs, ALU.mult).then_inc(tab_free, 1)
                dve.wait_ge(tab_free, s + 1)
                V.tensor_tensor(v[:, 0], v[:, 0], m0, ALU.subtract)
                V.tensor_tensor(v[:, 1], v[:, 1], m1, ALU.add).then_inc(zz_done, 1)

            def y_tile(f):
                dve.wait_ge(y_done, 2 * f + 2)
                V.scalar_tensor_tensor(out=gel[:, f], in0=uT[:, f], scalar=vec("ssm_d", f),
                                       in1=nrm[:, (f % 2) * T:(f % 2 + 1) * T], op0=ALU.mult, op1=ALU.add).then_inc(yp_done, 1)

            for s in range(16):
                for nm, n in GATES[2 * s:2 * s + 2]:
                    ahead()
                    if nm == "glm":
                        wait_freed(dve, TILE["glm"] + n)
                        V.tensor_tensor(mrg[:, n], mrg[:, n], glm_t[:, n % 2], ALU.mult).then_inc(glm_used, 1)
                ssm_step(s)
                if s >= 2 and s % 2 == 0:
                    y_tile(s // 2 - 1)
                if s == 11:
                    for f in range(4):
                        a_part(f, gel[:, f], 20 + f + 1, al_done)
            y_tile(7)
            for f in range(4, 8):
                a_part(f, gel[:, f], 20 + f + 1, al_done)
            for n in range(KT):
                ahead(2)
                wait_tile(dve, TILE["glu"] + 2 * n)
                wait_freed(dve, TILE["glu"] + 2 * n + 1)
                V.scalar_tensor_tensor(out=gel[:, n], in0=tiles[:, (TILE["glu"] + 2 * n) % 2, 0:T], scalar=vec("b_glu", n), in1=sig_t[:, n % 2],
                                       op0=ALU.add, op1=ALU.mult).then_inc(freed["d"], 1)
                wait_freed(dve, TILE["glu"] + 2 * n)
                V.tensor_tensor(gel[:, n], gel[:, n], zs_t[:, n], ALU.mult).then_inc(gv_done, 1)
                if n:
                    dve.wait_ge(xh_done, KT * SPLITS[7] + n)
                    V.tensor_tensor(x_lo[:, n - 1], gel[:, n - 1], x_hi[:, n - 1].bitcast(F32),
                                    ALU.subtract).then_inc(xl_done, 1)
            dve.wait_ge(xh_done, KT * SPLITS[7] + KT)
            V.tensor_tensor(x_lo[:, 7], gel[:, 7], x_hi[:, 7].bitcast(F32), ALU.subtract).then_inc(xl_done, 1)
            for n in range(KT):
                ahead()
                wait_tile(dve, TILE["brs"] + n)
                V.tensor_tensor(gel[:, n], tiles[:, (TILE["brs"] + n) % 2, 0:T], gs_t[:, n], ALU.mult).then_inc(freed["d"], 1)
                wait_freed(dve, TILE["brs"] + n)
                V.tensor_tensor(mrg[:, n], mrg[:, n], gel[:, n], ALU.add).then_inc(af_done, 1)
                if n:
                    a_part(n - 1, mrg[:, n - 1], 28 + n, al_done)
            a_part(7, mrg[:, 7], 36, al_done)
            ahead(KT)
            dve.wait_ge(g_red, N_G)
            link(V.tensor_tensor(coef[:, 8, 24:32], mods[:, 176:184], vec("bias", 176, 8), ALU.add))
            link(V.tensor_tensor(coef[:, 8, 0:8], coef[:, 8, 24:32], vec("g_post", 0, 8), ALU.mult))
            root(7)
            for k in range(KT):
                link(V.scalar_tensor_tensor(out=t_buf[:, k], in0=o_raw[:, k], scalar=coef[:, 8, k:k + 1], in1=rx,
                                            op0=ALU.mult, op1=ALU.mult))
                V.tensor_tensor(x[:, k], x[:, k], t_buf[:, k], ALU.add).then_inc(fin_done, 1)

        @block.gpsimd
        def _(pool):
            chain = [0]
            G = nc.gpsimd

            def link(ins):
                chain[0] += 1
                ins.then_inc(pool_s, 1)
                pool.wait_ge(pool_s, chain[0])

            def cmul(out_, a, b, tmp, last=None):
                (ar, ai), (br, bi) = a, b
                link(G.tensor_tensor(out_[0], ar, br, ALU.mult))
                link(G.tensor_tensor(tmp, ai, bi, ALU.mult))
                link(G.tensor_tensor(out_[0], out_[0], tmp, ALU.subtract))
                link(G.tensor_tensor(out_[1], ar, bi, ALU.mult))
                link(G.tensor_tensor(tmp, ai, br, ALU.mult))
                m = G.tensor_tensor(out_[1], out_[1], tmp, ALU.add)
                if last is None:
                    link(m)
                else:
                    m.then_inc(last, 1)

            pool.wait_ge(sin_done, 1)
            p, spare = ssm_s[:, 5:7], [ssm_s[:, 16:18], ssm_s[:, 8:10]]
            tmp = region(40, [32, 16])
            step = 0
            for table, n in ((base_t, CH), (chunk_t, NCH)):
                link(G.memset(table[:, 0, :, 0:1], 1.0))
                link(G.memset(table[:, 1, :, 0:1], 0.0))
                w = 1
                while w < n:
                    cmul([table[:, c, :, w:2 * w] for c in range(2)], [table[:, c, :, 0:w] for c in range(2)],
                         [p[:, c].unsqueeze(2).to_broadcast([P, 32, w]) for c in range(2)], tmp[:, :, 0:w])
                    q = spare[step % 2]
                    cmul([q[:, 0], q[:, 1]], [p[:, 0], p[:, 1]], [p[:, 0], p[:, 1]], tmp[:, 0:2].rearrange("p a b -> p (a b)"))
                    p, w, step = q, 2 * w, step + 1
            G.memset(tmp[:, 0, 0:1], 0.0).then_inc(base_done, 1)
            pool.wait_ge(kr_done, 1)
            G.tensor_copy(k2[64:96], kr_buf[64:96, 1].unsqueeze(1).to_broadcast([32, HEADS_2, T])).then_inc(kb_done, 1)
            pool.wait_ge(c_in, 16)
            pool.wait_ge(f_done, 1)
            wait_tile(pool, TILE["att2"] + 7)
            fr, fi = (ssm_s[:, n].unsqueeze(2).to_broadcast([P, 32, 32]) for n in (13, 14))

            def table_step(s):
                j = 2 * s
                if s >= 2:
                    pool.wait_ge(tab_free, s - 1)
                a = [base_t[:, c, j:j + 2].unsqueeze(2).to_broadcast([P, 2, NCH, CH]) for c in range(2)]
                b = [chunk_t[:, c, j:j + 2].unsqueeze(3).to_broadcast([P, 2, NCH, CH]) for c in range(2)]
                o = [rot_t[s % 2][:, c].rearrange("p j (a b) -> p j a b", b=CH) for c in range(2)]
                cmul(o, a, b, rh[:].rearrange("p (j a b) -> p j a b", j=2, b=CH), tab_done)

            table_step(0)
            pool.wait_ge(tab_done, 1)
            link(G.tensor_tensor(cc[:, 0], c_raw[:, 0], fr, ALU.mult))
            link(G.tensor_tensor(cc_tmp[:, 0], c_raw[:, 1], fi, ALU.mult))
            link(G.tensor_tensor(cc[:, 0], cc[:, 0], cc_tmp[:, 0], ALU.subtract))
            link(G.tensor_tensor(cc[:, 1], c_raw[:, 0], fi, ALU.mult))
            link(G.tensor_tensor(cc_tmp[:, 1], c_raw[:, 1], fr, ALU.mult))
            link(G.tensor_tensor(cc[:, 1], cc[:, 1], cc_tmp[:, 1], ALU.add))
            G.tensor_scalar(cc[:, 1], cc[:, 1], -1.0, None, ALU.mult).then_inc(cc_done, 1)
            for s in range(1, 16):
                table_step(s)
                pool.wait_ge(tab_done, s + 1)


def columns(w):
    k, n = w.shape
    return w.reshape(k // P, P, n // P, P).transpose(2, 1, 0, 3).reshape(n // P, P, -1)


def padded(a):
    return np.pad(a, ((0, 0), (0, 0), (0, WIDTH - a.shape[2])))


def ffn_units(w_in, w_out):
    gate_up, rows = columns(w_in), w_out.reshape(FFN_TILES, P, D)
    out = np.empty((66, P, WIDTH), w_in.dtype)
    for j in range(FFN_TILES):
        out[g_unit(0, j)] = gate_up[j]
        out[g_unit(0, j) + 1] = gate_up[FFN_TILES + j]
        out[o_unit(0, j)] = rows[j]
    return out


def tiled(v):
    return np.asarray(v).reshape(-1, P).T


def constants():
    c = np.zeros((P, NC_), np.float32)
    put = lambda name, a: c.__setitem__((slice(0, a.shape[0]), slice(CON[name], CON[name] + a.shape[1])), a)
    put("ident", np.eye(P, dtype=np.float32))
    put("ones", np.ones((P, P), np.float32))
    for name, first, half in (("rot1", 0, 64), ("rot2", 64, 16)):
        m = np.zeros((P, P if name == "rot1" else QK_2), np.float32)
        for i in range(half):
            m[first + half + i, first + i] = -1.0
            m[first + i, first + half + i] = 1.0
        put(name, m[:m.shape[1]] if name == "rot2" else m)
    pos = np.arange(T, dtype=np.float32)
    inv = (10000.0 ** (-np.arange(0, HEAD_DIM, 2, dtype=np.float32) / HEAD_DIM)).astype(np.float32)
    ang = (inv[:, None] * pos[None, :]).astype(np.float32)
    put("cos1", np.tile(np.cos(ang), (2, 1)).astype(np.float32))
    put("sin1", np.tile(np.sin(ang), (2, 1)).astype(np.float32))
    q = np.arange(P)[:, None, None] + P * np.arange(2)[None, :, None]
    k = np.arange(T)[None, None, :]
    put("mask", np.where(k <= q, 0.0, -1e30).astype(np.float32).reshape(P, 2 * T))
    mask2 = np.where(k // 64 <= q // 64, 0.0, -1e30).astype(np.float32).reshape(P, 2 * T)
    t = np.arange(PAD)
    put("cnt", np.tile(np.concatenate([1.0 / np.minimum(t + 1, w) for w in POOL_W]).astype(np.float32), (P, 1)))
    inv2 = (10000.0 ** (-np.arange(0, 32, 2, dtype=np.float32) / 32)).astype(np.float32)
    c[64:96, CON["invf"]] = np.tile(inv2, 2)
    c[:, CON["eps"]] = EPS
    return c, mask2


def kernel(**inp):
    import concourse.bacc as bacc
    from concourse.bass_utils import run_bass_kernel_spmd

    a = {name: np.asarray(v) for name, v in inp.items()}
    w_in2 = a["w_in_2"][0]
    parts = [
        ffn_units(a["ffn_w_in"][0, 0], a["ffn_w_out"][0, 0]),
        a["pool_w"][0].reshape(2, 2, 2, P, 256).transpose(0, 3, 1, 2, 4).reshape(2, P, WIDTH),
        ffn_units(a["ffn_w_in"][0, 1], a["ffn_w_out"][0, 1]),
        columns(a["w_kv"]),
        ffn_units(a["ffn_w_in"][1, 0], a["ffn_w_out"][1, 0]),
        columns(a["w_q"][0]), columns(a["w_o"][0]),
        ffn_units(a["ffn_w_in"][1, 1], a["ffn_w_out"][1, 1]),
        columns(w_in2[:, 2048:2560]),
        padded(np.pad(w_in2[:, 2560:2592], ((0, 0), (64, 0))).reshape(KT, P, QK_2).transpose(1, 0, 2).reshape(1, P, -1)),
        columns(w_in2[:, 0:1024]),
        padded(a["w_q_up_2"][0].reshape(2, P, 4, 384).transpose(2, 1, 0, 3).reshape(4, P, -1)),
        a["w_kv_up_2"][0].reshape(2, P, 4, 512).transpose(2, 1, 0, 3).reshape(4, P, -1),
        columns(w_in2[:, 2592:3616]),
        columns(a["w_br_mla_2"][0]),
        columns(w_in2[:, 4640:5664]),
        columns(w_in2[:, 1024:2048]),
        columns(w_in2[:, 3616:4640]),
        columns(a["w_glu_2"][0]).reshape(2, KT, P, WIDTH).transpose(1, 0, 2, 3).reshape(16, P, WIDTH),
        columns(a["w_br_ssm_2"][0]),
        columns(a["w_out_2"][0]),
    ]
    stream = np.concatenate(parts)
    blocks = lambda w: w.reshape(8, P, -1, GW).transpose(2, 1, 0, 3)
    gstream = np.concatenate([blocks(a["ada_w"][0]), blocks(a["kv_ada_w"]), blocks(a["ada_w"][1]),
                              blocks(a["w_ada_2"][0])])
    bias = np.concatenate([a["ada_b"][0], a["kv_ada_b"], a["ada_b"][1], a["b_ada_2"][0]])
    states = lambda v: v.reshape(32, P).T
    vecs = np.concatenate([
        tiled(a["c"]), tiled(a["c_2"]), states(np.repeat(a["ssm_log_dt_2"][0], 64)), states(a["ssm_a_re_2"][0]),
        states(a["ssm_a_im_2"][0]), tiled(bias), tiled(a["norm_g"]), tiled(a["pool_scale"]), tiled(a["kv_norm"]),
        tiled(a["k_norm"]), tiled(a["q_norm"]), tiled(a["g_pre_2"]), tiled(a["ssm_d_2"]), tiled(a["b_glu_2"]),
        tiled(a["g_q_norm_2"]), tiled(a["g_kv_norm_2"]), tiled(a["g_post_2"])], axis=1)
    ssm_b = np.zeros((2, KT, 4, 2, 16, 2, 64), np.float32)
    ssm_c = np.zeros((2, 32, 2, 64, 2, 16), np.float32)
    for c, part in enumerate(("re", "im")):
        b = a[f"ssm_b_{part}_2"][0].reshape(KT, 4, 2, 64, 16)
        cc = a[f"ssm_c_{part}_2"][0].reshape(32, 2, 16, 64)
        for g in range(2):
            ssm_b[c, :, :, g, :, g, :] = b[:, :, g].transpose(0, 1, 3, 2)
            ssm_c[c, :, g, :, g, :] = cc[:, g].transpose(0, 2, 1)
    ssm_b = ssm_b.transpose(2, 3, 4, 0, 1, 5, 6).reshape(P, 2, KT, P)
    ssm_c = ssm_c.transpose(2, 3, 0, 1, 4, 5).reshape(P, 2, 32, 32)
    cons, mask2 = constants()
    arrays = {
        "stream": stream, "gstream": gstream, "vecs": vecs, "cons": cons, "mask2": mask2,
        "x_t": a["x"][0].T.reshape(KT, P, T).transpose(1, 0, 2),
        "pos": np.tile(a["positions_2"], (32, 1)).astype(np.int32), "ssm_b": ssm_b, "ssm_c": ssm_c,
    }
    arrays = {name: np.ascontiguousarray(v) for name, v in arrays.items()}
    nc = bacc.Bacc("TRN2", target_bir_lowering=False, num_devices=1)
    args = [nc.dram_tensor(f"in_{name}", v.shape, mybir.dt.from_np(v.dtype), kind="ExternalInput").ap()
            for name, v in arrays.items()]
    out = nc.dram_tensor("out_t", (P, KT, T), F32, kind="ExternalOutput").ap()
    build_program(nc, *args, out)
    r = run_bass_kernel_spmd(nc, [{f"in_{name}": v for name, v in arrays.items()}], core_ids=[0])
    return r.results[0]["out_t"].transpose(1, 0, 2).reshape(D, T).T.reshape(1, T, D)
```

```python
from contextlib import ExitStack

import numpy as np

import concourse.bass as bass
from concourse import mybir

F32 = mybir.dt.float32
F32R = mybir.dt.float32r
I32 = mybir.dt.int32
ALU = mybir.AluOpType
ACT = mybir.ActivationFunctionType
AX = mybir.AxisListType.X

P = 128
D = 1024
KT = D // P
T = 256
FFN_TILES = 22
WIDTH = 1024
EPS = 1e-6
HEADS_1, HEAD_DIM = 8, 128
HEADS_2, QK_2, V_2 = 16, 96, 64
TWO_PI = 6.283185307179586

PHASES = [("ffn0", 66), ("pool", 2), ("ffn1", 66), ("kv", 16), ("ffn2", 66), ("q", 8), ("o", 8), ("ffn3", 66),
          ("lat", 4), ("kr", 1), ("u", 8), ("qup", 4), ("kvup", 4), ("zm", 8), ("glm", 8), ("brm", 8),
          ("zs", 8), ("gls", 8), ("glu", 16), ("brs", 8), ("out", 8)]
UNIT, N_UNITS = {}, 0
for _name, _n in PHASES:
    UNIT[_name] = N_UNITS
    N_UNITS += _n
FFN_BASE = [UNIT[f"ffn{f}"] for f in range(4)]

RING, LAND = 4, 4
GW = 512
N_G = 46
G_PRE, G_POOL = 4, 1
G_FIRST = [1, 1, 1, 0]
SEGMENTS = [[(5, "silu")], [(5, "silu")], [(5, "silu")], [(1, "silu"), (3, "c2"), (1, None)]]
G_FFN = [4, 16, 27, 38]
M_LAYER = [0, 88]
M_KV, M_2 = 72, 160
N_MOD = 184

TILES = [("ffn0", 22, "d"), ("pool", 8, "d"), ("ffn1", 22, "d"), ("k", 8, "a"), ("ffn2", 22, "d"),
         ("q", 8, "a"), ("att1", 4, "d"), ("o", 8, "d"), ("ffn3", 22, "d"), ("lat", 4, "a"), ("kr", 1, "a"),
         ("u", 8, "a"), ("qup", 8, "a"), ("kvup", 12, "a"), ("att2+zm", 16, "x"), ("glm", 8, "a"),
         ("brm", 8, "d"), ("zs", 8, "a"), ("gls", 8, "a"), ("glu", 16, "y"), ("brs", 8, "d"), ("out", 8, "a")]
TILE, OWNER = {}, []
for _name, _n, _who in TILES:
    TILE[_name] = len(OWNER)
    OWNER += {"x": ["d", "a"], "y": ["a", "d"]}.get(_who, [_who] * 2) * (_n // 2) + [_who] * (_n % 2)
TILE_UNITS = {"pool": ("pool", 0, 4), "k": ("kv", 0, 1), "qup": ("qup", 0, 2), "kvup": ("kvup", 0, 3),
              "att1": None}
FINISHED, _parts = {}, 0
for _name, _n, _who in TILES:
    if _name.startswith("ffn"):
        continue
    _from = TILE_UNITS.get(_name, (_name, 0, 1))
    for _k in range(_n):
        if _name == "att2+zm":
            if _k % 2 == 0:
                _parts += 1
            FINISHED[TILE[_name] + _k] = ("used", UNIT["zm"] + _k // 2 + 1) if _k % 2 else ("part", _parts)
            continue
        if _from and _k % _from[2] == _from[2] - 1:
            FINISHED[TILE[_name] + _k] = ("used", UNIT[_from[0]] + _from[1] + _k // _from[2] + 1)
        else:
            _parts += 1
            FINISHED[TILE[_name] + _k] = ("part", _parts)


def freed_count(o):
    return OWNER[o], OWNER[:o + 1].count(OWNER[o])


VEC, NV = {}, 0
for _name, _n in [("c", 8), ("c2", 8), ("logdt", 32), ("lr", 32), ("li", 32), ("bias", N_MOD), ("norm_g", 48),
                  ("pool_scale", 8), ("kv_norm", 8), ("k_norm", 1), ("q_norm", 1), ("g_pre", 8), ("ssm_d", 8),
                  ("b_glu", 16), ("g_q", 2), ("g_kv", 2), ("g_post", 8)]:
    VEC[_name] = NV
    NV += _n
CON, NC_ = {}, 0
for _name, _n in [("ident", 128), ("ones", 128), ("rot1", 128), ("rot2", 96), ("cos1", T), ("sin1", T),
                  ("mask", 2 * T), ("cnt", 64), ("invf", 1), ("eps", 1), ("zero", 1)]:
    CON[_name] = NC_
    NC_ += _n
POOL_W = (2, 4, 8, 16)
PAD = 16
CH = 32
NCH = T // CH


GATES = [(_name, _n) for _name in ("glm", "brm", "zs", "gls") for _n in range(KT)]


def zm_tile(n):
    return TILE["att2+zm"] + 2 * n + 1


def att2_tile(g):
    return TILE["att2+zm"] + 2 * g


def g_unit(base, j):
    return base + (2 * j if j < 2 else 3 * j - 1)


def o_unit(base, j):
    return base + (65 if j == FFN_TILES - 1 else 3 * j + 4)


def build_program(nc, stream, gstream, vecs_d, cons_d, mask2_d, xin, pos_d, ssm_b, ssm_c, out):
    with ExitStack() as ctx:
        def sb(name, shape, dt=F32):
            return ctx.enter_context(nc.sbuf_tensor(name, shape, dt))

        def sem(name):
            return ctx.enter_context(nc.semaphore(name))

        land = sb("land", [P, LAND, WIDTH])
        w_hi = sb("w_hi", [P, RING, WIDTH], F32R)
        w_lo = sb("w_lo", [P, RING, WIDTH], F32R)
        x = sb("x", [P, KT, T])
        x_hi = sb("x_hi", [P, KT, T], F32R)
        x_lo = sb("x_lo", [P, KT, T], F32R)
        a_hi = sb("a_hi", [P, KT, T], F32R)
        a_lo = sb("a_lo", [P, KT, T], F32R)
        h_hi = sb("h_hi", [P, 2, T], F32R)
        h_lo = sb("h_lo", [P, 2, T], F32R)
        vecs = sb("vecs", [P, NV])
        cons = sb("cons", [P, NC_])
        rh = sb("rh", [P, 2 * T])
        base_t = sb("base_t", [P, 2, 32, CH])
        chunk_t = sb("chunk_t", [P, 2, 32, NCH])
        ssm_s = sb("ssm_s", [P, 20, 32])
        coef = sb("coef", [P, 9, 32])
        csil = sb("csil", [P, KT])
        att_s = sb("att_s", [P, 2, 16])
        ssm_m1 = sb("ssm_m1", [P, 2, 2, T])
        arena = sb("arena", [P, 20480])

        def region(kb, shape):
            n = int(np.prod(shape))
            v = arena[:, kb * 256:kb * 256 + n]
            names = "abcd"[:len(shape)]
            if len(shape) == 1:
                return v
            kw = {names[i]: shape[i] for i in range(1, len(shape))}
            return v.rearrange(f"p ({' '.join(names)}) -> p {' '.join(names)}", **kw)

        def region_at(col, shape):
            n = int(np.prod(shape))
            v = arena[:, col:col + n]
            names = "abcd"[:len(shape)]
            kw = {names[i]: shape[i] for i in range(1, len(shape))}
            return v.rearrange(f"p ({' '.join(names)}) -> p {' '.join(names)}", **kw)

        rx = region(79, [T])
        g_land = region(0, [2, 8, GW])
        g_acc = region(32, [2, GW])
        silu_b = region(36, [2, T])
        hid = region(38, [2, T])
        kT = region(40, [HEADS_1, T])
        v1 = region(48, [2, D])
        t_buf = region(56, [KT, T])
        qT = region(64, [HEADS_1, T])
        win_h = region(40, [KT, PAD + T])
        win_a = region_at(64 * 256, [KT, PAD + T])
        win_b = region_at(64 * 256 + KT * (PAD + T), [6, PAD + T])
        rope_sq, rope_kn, rope_t = region(56, [2, T]), region(58, [2, T]), region(60, [2, 2, T])
        ws1 = [(region(72, [4, T]), region(76, [2, 384])), (region(32, [4, T]), region(36, [2, 384]))]
        uT = region(0, [KT, T])
        q2 = region(8, [HEADS_2, T])
        k2 = region(24, [HEADS_2, T])
        v2 = region(40, [2, D])
        ym, zm = region(8, [KT, 2, T])[:, :, 0], region(8, [KT, 2, T])[:, :, 1]
        lat_raw, lat_sq, lat_n = region(64, [4, T]), region(68, [4, T]), region(72, [4, T])
        kr_buf = region(76, [3, T])
        pos_i = region(78, [T])
        rope2 = region(56, [2, T])[0:QK_2]
        ang = region(58, [6, T])
        ws2 = [(region(48, [4, T]), region(52, [2, 384])), (region(56, [4, T]), region(60, [2, 384]))]
        rot_t = [region(64, [2, 2, T]), region(68, [2, 2, T])]
        ssm_m = [(region(20, [2, T]), region(22, [2, T])), (ssm_m1[:, 0], ssm_m1[:, 1])]
        sig_t = region(26, [2, T])
        ssm_v = [region(16, [2, 2, T]), region(28, [2, 2, T])]
        gel = region(56, [KT, T])
        zs_t = region(32, [KT, T])
        b_sb = region(40, [2, KT, P])
        mrg = region(48, [KT, T])
        gs_t = region(8, [KT, T])
        cc = region(72, [2, 32, 32])
        c_raw = region(64, [2, 32, 32])
        o_raw = region(8, [KT, T])

        acc4 = ctx.enter_context(nc.psum_tensor("acc4", [P, 4, 512], F32))
        tiles = ctx.enter_context(nc.psum_tensor("tiles", [P, 2, 512], F32))
        nrm = ctx.enter_context(nc.psum_tensor("nrm", [P, 512], F32))
        mods = ctx.enter_context(nc.psum_tensor("mods", [P, 512], F32))
        yT = [acc4[:, n // 2, (n % 2) * T:(n % 2 + 1) * T] for n in range(KT)]

        landed = [sem(f"landed{i}") for i in range(LAND)]
        hi_done = sem("hi_done")
        lo_done = sem("lo_done")
        used = sem("used")
        g_landed = [sem(f"g_landed{i}") for i in range(2)]
        g_step = sem("g_step")
        g_done = sem("g_done")
        g_red = sem("g_red")
        vec_in, con_in, x_in, pos_in = sem("vec_in"), sem("con_in"), sem("x_in"), sem("pos_in")
        b_in, c_in, mask_in, out_st = sem("b_in"), sem("c_in"), sem("mask_in"), sem("out_st")
        freed = {"d": sem("freed_d"), "a": sem("freed_a")}
        part_done = sem("part_done")
        x_upd = sem("x_upd")
        sq_done, nrm_done, rt_done = sem("sq_done"), sem("nrm_done"), sem("rt_done")
        t_done, xh_done, xl_done = sem("t_done"), sem("xh_done"), sem("xl_done")
        silu_done, hh_done, h_done = sem("silu_done"), sem("hh_done"), sem("h_done")
        dve_s, act_s, pool_s = sem("dve_s"), sem("act_s"), sem("pool_s")
        csilu_done, ang_done, sin_done, f_done = sem("csilu_done"), sem("ang_done"), sem("sin_done"), sem("f_done")
        hread_done, v_done = sem("hread_done"), sem("v_done")
        hsq_done, hs_done, hrt_done = sem("hsq_done"), sem("hs_done"), sem("hrt_done")
        kn_done, hrot_done, rope_done = sem("kn_done"), sem("hrot_done"), sem("rope_done")
        s_done, sm_done, mx_done, ex_done = sem("s_done"), sem("sm_done"), sem("mx_done"), sem("ex_done")
        pn_done, pt_done, pe_done = sem("pn_done"), sem("pt_done"), sem("pe_done")
        af_done, ah_done, al_done = sem("af_done"), sem("ah_done"), sem("al_done")
        lsq_done, lsum_done, lrt_done = sem("lsq_done"), sem("lsum_done"), sem("lrt_done")
        krot_done, kr_done, kb_done = sem("krot_done"), sem("kr_done"), sem("kb_done")
        qrot_done, qrope_done = sem("qrot_done"), sem("qrope_done")
        base_done = sem("base_done")
        tab_done, cc_done = sem("tab_done"), sem("cc_done")
        bu_done, bu_free, zz_done, y_done = sem("bu_done"), sem("bu_free"), sem("zz_done"), sem("y_done")
        yp_done, gel_done, gv_done = sem("yp_done"), sem("gel_done"), sem("gv_done")
        zm_done = sem("zm_done")
        vs_done, zp_done = sem("vs_done"), sem("zp_done")
        fin_done = sem("fin_done")
        done_sem = {"used": used, "part": part_done}

        def wait_tile(eng, o):
            which, n = FINISHED[o]
            eng.wait_ge(done_sem[which], n)

        def wait_freed(eng, o):
            who, n = freed_count(o)
            eng.wait_ge(freed[who], n)

        def vec(name, a=0, n=1):
            return vecs[:, VEC[name] + a:VEC[name] + a + n]

        def con(name, n):
            return cons[:, CON[name]:CON[name] + n]

        ident, ones = con("ident", P), con("ones", P)
        cos1, sin1 = con("cos1", T), con("sin1", T)
        zero = con("zero", 1)

        STAGE = [(M_LAYER[0], 8 + M_LAYER[0], ("norm_g", 0)), (24, 32, ("norm_g", 8)), (48, 56, ("norm_g", 16)),
                 (M_KV, M_KV + 8, ("kv_norm", 0)), (88, 96, ("norm_g", 24)), (112, 120, ("norm_g", 32)),
                 (136, 144, ("norm_g", 40)), (M_2, M_2 + 8, ("g_pre", 0))]
        SPLITS = {0: 1, 1: 2, 2: 3, 3: 4, 4: 5, 5: 6, 6: 7, 7: 8}

        def wait_bank(eng, o):
            if o >= 2:
                who, n = freed_count(o - 2)
                eng.wait_ge(freed[who], n)

        def load_unit(sp, u, slot, i=0):
            if u >= LAND:
                sp.wait_ge(lo_done, i * 12 + (u - LAND + 1))
            sp.dma_start(land[:, slot], stream[i * 12 + u]).then_inc(landed[slot], 16)

        def split_hi(act, u, i=0):
            act.wait_ge(landed[u % LAND], i * (16 * 12 // LAND) + 16 * (u // LAND + 1))
            if u >= RING:
                act.wait_ge(used, i * 12 + (u - RING + 1))
            nc.scalar.copy(w_hi[:, u % RING], land[:, u % LAND]).then_inc(hi_done, 1)

        def split_lo(dve, u, i=0):
            dve.wait_ge(hi_done, i * 12 + (u + 1))
            nc.vector.tensor_tensor(w_lo[:, u % RING], land[:, u % LAND], w_hi[:, u % RING].bitcast(F32),
                                    ALU.subtract).then_inc(lo_done, 1)

        def products(pe, outs, pairs, start=True, stop=True, **kw):
            last = None
            for n, (lh, ll, rh, rl) in enumerate(pairs):
                first, end = start and n == 0, stop and n == len(pairs) - 1
                nc.tensor.matmul(outs, lh, rh, start=first, stop=False, **kw)
                nc.tensor.matmul(outs, lh, rl, start=False, stop=False, **kw)
                last = nc.tensor.matmul(outs, ll, rh, start=False, stop=end, **kw)
            return last

        def w_tile(u, a, n):
            return w_hi[:, u % RING, a:a + n], w_lo[:, u % RING, a:a + n]

        block = ctx.enter_context(nc.Block())

        @block.sync
        def _(sp):
            def g_load(b, i=0):
                if b >= 2:
                    sp.wait_ge(g_done, i * 2 + (b - 1))
                sp.dma_start(g_land[:, b % 2], gstream[i * 2 + b]).then_inc(g_landed[b % 2], 16)

            def units(name, n):
                for u in range(UNIT[name], UNIT[name] + n):
                    load_unit(sp, u, u % LAND)

            sp.dma_start(vecs[:], vecs_d).then_inc(vec_in, 16)
            g_load(0)
            g_load(1)
            sp.dma_start(x[:], xin).then_inc(x_in, 16)
            sp.dma_start(cons[:], cons_d).then_inc(con_in, 16)
            g_load(2)
            g_load(3)
            for k in range(LAND):
                load_unit(sp, k, k)
            for f in range(4):
                base, b = FFN_BASE[f], G_FFN[f]
                if G_FIRST[f]:
                    g_load(b)
                    b += 1
                for u in range(base, base + 5):
                    if not (f == 0 and u < LAND):
                        load_unit(sp, u, u % LAND)
                u = base + 5
                for reps, vector in SEGMENTS[f]:
                    with sp.Fori(0, reps) as i:
                        for m in range(4):
                            if vector and m % 2 == 0:
                                g_load(b + m // 2, i)
                            for s in range(3):
                                load_unit(sp, u + 3 * m + s, (u + 3 * m + s) % LAND, i)
                    u += 12 * reps
                    b += 2 * reps if vector else 0
                load_unit(sp, u, u % LAND)
                if f == 0:
                    g_load(G_PRE + 11)
                    units("pool", 2)
                elif f == 1:
                    units("kv", 16)
                elif f == 2:
                    units("q", 8)
                    units("o", 8)
            wait_freed(sp, TILE["att1"] + 3)
            sp.dma_start(con("mask", 2 * T), mask2_d).then_inc(mask_in, 16)
            sp.dma_start(pos_i[64:96].bitcast(I32), pos_d).then_inc(pos_in, 16)
            for name, n in PHASES[8:13]:
                units(name, n)
            sp.wait_ge(al_done, 4)
            sp.wait_ge(kb_done, 1)
            sp.dma_start(c_raw, ssm_c).then_inc(c_in, 16)
            units("zm", 8)
            units("glm", 6)
            wait_tile(sp, att2_tile(7))
            sp.dma_start(b_sb, ssm_b).then_inc(b_in, 16)
            for u in range(UNIT["glm"] + 6, N_UNITS):
                load_unit(sp, u, u % LAND)
            for k in range(KT):
                sp.wait_ge(fin_done, k + 1)
                sp.dma_start(out[:, k], x[:, k]).then_inc(out_st, 16)
            sp.wait_ge(out_st, 16 * KT)

        @block.tensor
        def _(pe):
            def reduce_block(b, i=0):
                pe.wait_ge(g_done, i * 2 + (b + 1))
                for q in range(4):
                    m = nc.tensor.matmul(mods[:, bass.ds(i * 8 + (4 * b + q), 1)],
                                         g_acc[:, b % 2, q * P:(q + 1) * P], ones[:, 0:1], start=True, stop=True)
                m.then_inc(g_red, 1)

            def sum_squares(n):
                if n:
                    pe.wait_ge(rt_done, n)
                for k in range(KT):
                    pe.wait_ge(sq_done, KT * n + k + 1)
                    m = nc.tensor.matmul(nrm[:, 0:T], ones, t_buf[:, k], start=(k == 0), stop=(k == KT - 1))
                m.then_inc(nrm_done, 1)

            def column_unit(u, o, hi, lo, split_sem=None, before=0, n_out=P):
                wait_bank(pe, o)
                pe.wait_ge(lo_done, u + 1)
                for k in range(KT):
                    if split_sem is not None:
                        pe.wait_ge(split_sem, before + k + 1)
                    m = products(pe, tiles[0:n_out, o % 2, 0:T],
                                 [(*w_tile(u, k * n_out, n_out), hi[:, k], lo[:, k])], start=(k == 0), stop=(k == KT - 1))
                m.then_inc(used, 1)

            def gate_unit(base, j, u, i, first=None):
                pe.wait_ge(lo_done, i * 12 + (u + 1))
                for k in range(KT):
                    if first is not None:
                        pe.wait_ge(xl_done, KT * (first - 1) + k + 1)
                    m = products(pe, tiles[:, j % 2, 0:T], [(*w_tile(u, k * P, P), x_hi[:, k], x_lo[:, k])],
                                 start=(k == 0), stop=(k == KT - 1))
                m.then_inc(used, 1)

            def up_unit(j, u, i):
                pe.wait_ge(lo_done, i * 12 + (u + 1))
                m = products(pe, tiles[:, j % 2, T:2 * T],
                             [(*w_tile(u, k * P, P), x_hi[:, k], x_lo[:, k]) for k in range(KT)])
                m.then_inc(used, 1)

            def out_unit(f, j, u, i, per):
                pe.wait_ge(lo_done, i * 12 + (u + 1))
                pe.wait_ge(h_done, i * per + (FFN_TILES * f + j + 1))
                for n in range(KT):
                    m = products(pe, yT[n], [(*w_tile(u, n * P, P), h_hi[:, j % 2], h_lo[:, j % 2])],
                                 start=(j == 0 and per == 0 and n % 2 == 0),
                                 stop=(j == FFN_TILES - 1 and per == 0), skip_group_check=True)
                m.then_inc(used, 1)

            def ffn(f, stage):
                base, o0, b = FFN_BASE[f], TILE[f"ffn{f}"], G_FFN[f]
                nd = OWNER[:o0].count("d")
                for j in range(2):
                    wait_bank(pe, o0 + j)
                    gate_unit(base, j, g_unit(base, j), 0, SPLITS[stage] if j == 0 else None)
                    up_unit(j, g_unit(base, j) + 1, 0)
                if f == 2:
                    pe.wait_ge(v_done, 2)
                out_unit(f, 0, o_unit(base, 0), 0, 0)
                if G_FIRST[f]:
                    reduce_block(b)
                    b += 1
                j0 = 2
                for reps, vector in SEGMENTS[f]:
                    with pe.Fori(0, reps) as i:
                        for m in range(4):
                            j = j0 + m
                            u = g_unit(base, j)
                            pe.wait_ge(freed["d"], i * 4 + (nd + j - 1))
                            gate_unit(base, j, u, i)
                            up_unit(j, u + 1, i)
                            out_unit(f, j - 1, u + 2, i, 4)
                            if vector and m % 2 == 1:
                                reduce_block(b + m // 2, i)
                    j0 += 4 * reps
                    b += 2 * reps if vector else 0
                out_unit(f, FFN_TILES - 1, o_unit(base, FFN_TILES - 1), 0, 0)

            def head_sum(n):
                if n % 4 == 1:
                    pe.wait_ge(hrt_done, n)
                elif n:
                    pe.wait_ge(hread_done, n - 1 if n % 4 else n)
                pe.wait_ge(hsq_done, n + 1)
                nc.tensor.matmul(nrm[:], ones, rope_sq, start=True, stop=True).then_inc(hs_done, 1)

            def head_rot(n):
                pe.wait_ge(hrt_done, min(n + 2, 4 * (n // 4) + 4))
                if n % 4 == 3:
                    pe.wait_ge(hread_done, n)
                pe.wait_ge(kn_done, n + 1)
                nc.tensor.matmul(nrm[:], con("rot1", P), rope_kn, start=True, stop=True).then_inc(hrot_done, 1)

            def head_steps(n0, h):
                if h in (5, 7, 9, 11):
                    head_rot(n0 + (h - 5) // 2)
                if h in (2, 4, 6, 8):
                    head_sum(n0 + h // 2 - 1)

            rot2 = cons[0:QK_2, CON["rot2"]:CON["rot2"] + QK_2]

            def attention(n0, groups, tile, qq, kk, vv, parts, vdim, ws, ready, beside=None):
                def scores(g):
                    ready(g)
                    if n0 + g:
                        pe.wait_ge(sm_done, n0 + g)
                    for h in range(2):
                        for qt in range(2):
                            m = nc.tensor.matmul(acc4[:, h, qt * T:(qt + 1) * T], qq[0:parts, 2 * g + h, qt * P:(qt + 1) * P],
                                                 kk[0:parts, 2 * g + h, :], start=True, stop=True)
                    m.then_inc(s_done, 1)

                scores(0)
                scores(1)
                for g in range(groups):
                    n = n0 + g
                    sm, pt = ws[g % 2]
                    pe.wait_ge(pn_done, 4 * (n + 1))
                    if n:
                        pe.wait_ge(pe_done, n)
                    for h in range(2):
                        for qt, kt in ((0, 0), (1, 0), (1, 1)):
                            col = T + 0 if kt else qt * P
                            m = nc.tensor.transpose(acc4[:, 2 + h, col:col + P], sm[:, 2 * h + qt, kt * P:(kt + 1) * P],
                                                    ident)
                    m.then_inc(pt_done, 1)
                    if g + 2 < groups:
                        scores(g + 2)
                    wait_bank(pe, tile(g))
                    pe.wait_ge(pe_done, n + 1)
                    for h in range(2):
                        head = 2 * g + h
                        if vdim == P:
                            dst = tiles[:, tile(g) % 2, h * T:(h + 1) * T]
                        else:
                            dst = tiles[h * vdim:(h + 1) * vdim, tile(g) % 2, 0:T]
                        nc.tensor.matmul(dst, vv[:, 0, head * vdim:(head + 1) * vdim], pt[:, h, 0:T],
                                         start=True, stop=False)
                        m = nc.tensor.matmul(dst[:, P:T], vv[:, 1, head * vdim:(head + 1) * vdim], pt[:, h, T:T + P],
                                             start=False, stop=True)
                    m.then_inc(part_done, 1)
                    if beside:
                        beside(g)

            pe.wait_ge(con_in, 16)
            for b in range(G_PRE):
                reduce_block(b)
            sum_squares(0)
            ffn(0, 0)
            sum_squares(1)
            reduce_block(G_PRE + 11)
            for q in range(2):
                u = UNIT["pool"] + q
                pe.wait_ge(lo_done, u + 1)
                for g in range(2):
                    for n in range(2):
                        o = TILE["pool"] + 4 * q + 2 * g + n
                        k0 = 4 * q + 2 * g
                        wait_bank(pe, o)
                        pe.wait_ge(xl_done, KT * (SPLITS[1] - 1) + k0 + 2)
                        m = products(pe, tiles[:, o % 2, 0:T],
                                     [(*w_tile(u, (2 * g + k) * 256 + n * P, P), x_hi[:, k0 + k], x_lo[:, k0 + k])
                                      for k in range(2)])
                        m.then_inc(used if (g, n) == (1, 1) else part_done, 1)
            sum_squares(2)
            ffn(1, 2)
            sum_squares(3)
            for h in range(HEADS_1):
                column_unit(UNIT["kv"] + h, TILE["k"] + h, x_hi, x_lo, xl_done if h == 0 else None,
                            KT * (SPLITS[3] - 1))
                head_steps(0, h)
            for k in range(KT):
                u = UNIT["kv"] + 8 + k
                pe.wait_ge(lo_done, u + 1)
                for tt in range(2):
                    rows = (x_hi[:, k, tt * P:(tt + 1) * P], x_lo[:, k, tt * P:(tt + 1) * P])
                    for c in range(2):
                        m = products(pe, acc4[:, 2 * tt + c], [(*rows, *w_tile(u, c * 512, 512))], start=(k == 0),
                                     stop=(k == KT - 1))
                m.then_inc(used, 1)
                head_steps(0, 8 + k)
            ffn(2, 4)
            sum_squares(4)
            for h in range(HEADS_1):
                column_unit(UNIT["q"] + h, TILE["q"] + h, x_hi, x_lo, xl_done if h == 0 else None, KT * (SPLITS[5] - 1))
                head_steps(4, h)
            head_steps(4, 8)
            head_steps(4, 9)
            head_steps(4, 11)
            attention(0, 4, lambda g: TILE["att1"] + g, qT, kT, v1, P, P, ws1, lambda g: pe.wait_ge(rope_done, 4 + g + 1))
            for n in range(KT):
                if n == 0:
                    wait_freed(pe, TILE["att1"] + 3)
                column_unit(UNIT["o"] + n, TILE["o"] + n, a_hi, a_lo)
            sum_squares(5)
            ffn(3, 6)
            sum_squares(6)
            for n in range(4):
                column_unit(UNIT["lat"] + n, TILE["lat"] + n, x_hi, x_lo, xl_done if n == 0 else None,
                            KT * (SPLITS[7] - 1))
            column_unit(UNIT["kr"], TILE["kr"], x_hi, x_lo, n_out=QK_2)
            for n in range(2):
                column_unit(UNIT["u"] + n, TILE["u"] + n, x_hi, x_lo)
            for q in range(2):
                for k in range(2):
                    pe.wait_ge(lsq_done, 2 * q + k + 1)
                    m = nc.tensor.matmul(nrm[:, q * T:(q + 1) * T], ones, lat_sq[:, 2 * q + k], start=(k == 0),
                                         stop=(k == 1))
            m.then_inc(lsum_done, 1)
            wait_freed(pe, TILE["kr"])
            nc.tensor.matmul(acc4[0:QK_2, 2, 0:T], rot2, kr_buf[0:QK_2, 0], start=True, stop=True).then_inc(krot_done, 1)
            for n in range(2, KT):
                column_unit(UNIT["u"] + n, TILE["u"] + n, x_hi, x_lo)
            for n in range(4):
                u = UNIT["qup"] + n
                pe.wait_ge(lo_done, u + 1)
                if n == 0:
                    pe.wait_ge(al_done, 4)
                for pair in range(2):
                    o = TILE["qup"] + 2 * n + pair
                    wait_bank(pe, o)
                    for h in range(2):
                        m = products(pe, tiles[0:QK_2, o % 2, h * T:(h + 1) * T],
                                     [(*w_tile(u, k * 384 + (2 * pair + h) * QK_2, QK_2), a_hi[:, k], a_lo[:, k])
                                      for k in range(2)])
                    m.then_inc(used if pair else part_done, 1)
            for n in range(4):
                u = UNIT["kvup"] + n
                pe.wait_ge(lo_done, u + 1)
                for pair in range(2):
                    o = TILE["kvup"] + 3 * n + pair
                    wait_bank(pe, o)
                    for h in range(2):
                        m = products(pe, tiles[:, o % 2, h * T:(h + 1) * T],
                                     [(*w_tile(u, k * 512 + (2 * pair + h) * P, P), a_hi[:, 2 + k], a_lo[:, 2 + k])
                                      for k in range(2)])
                    m.then_inc(part_done, 1)
                o = TILE["kvup"] + 3 * n + 2
                wait_bank(pe, o)
                for tt in range(2):
                    m = products(pe, tiles[:, o % 2, tt * T:(tt + 1) * T],
                                 [(a_hi[:, 2 + k, tt * P:(tt + 1) * P], a_lo[:, 2 + k, tt * P:(tt + 1) * P],
                                   *(w[:, u % RING, k * 512:(k + 1) * 512].rearrange("p (h c) -> p h c", c=P)[:, :, V_2:P]
                                     for w in (w_hi, w_lo))) for k in range(2)])
                m.then_inc(used, 1)
                for g in (2 * n, 2 * n + 1):
                    wait_freed(pe, TILE["qup"] + g)
                    if g >= 2:
                        pe.wait_ge(qrope_done, g - 1)
                    nc.tensor.matmul(acc4[0:QK_2, g % 2], rot2, q2[0:QK_2, 2 * g:2 * g + 2], start=True,
                                     stop=True).then_inc(qrot_done, 1)
            attention(4, 8, att2_tile, q2, k2, v2, QK_2, V_2, ws2, lambda g: (
                pe.wait_ge(qrope_done, 8), pe.wait_ge(kb_done, 1), wait_freed(pe, TILE["kvup"] + 11)),
                lambda g: column_unit(UNIT["zm"] + g, zm_tile(g), x_hi, x_lo))

            def ssm_b_step(s):
                if s == 0:
                    pe.wait_ge(b_in, 16)
                if s >= 2:
                    pe.wait_ge(bu_free, s - 1)
                f, jj = s // 2, 2 * (s % 2)
                for j in range(2):
                    r = 32 * (jj + j)
                    for c in range(2):
                        m = nc.tensor.matmul(acc4[:, jj + j, c * T:(c + 1) * T], b_sb[r:r + 32, c, f],
                                             uT[r:r + 32, f], start=True, stop=True)
                m.then_inc(bu_done, 1)

            def ssm_c_step(s):
                f, jj = s // 2, 2 * (s % 2)
                if s == 0:
                    pe.wait_ge(cc_done, 1)
                if s % 2 == 0 and f >= 1:
                    pe.wait_ge(yp_done, f)
                pe.wait_ge(zz_done, s + 1)
                pe.wait_ge(zp_done, s + 1)
                v, (m0, m1) = ssm_v[s % 2], ssm_m[s % 2]
                for j in range(2):
                    r = 32 * (jj + j)
                    terms = [(0, m0[:, j]), (1, v[:, 1, j]), (0, v[:, 0, j]), (1, m1[:, j])]
                    for n, (c, z) in enumerate(terms):
                        m = nc.tensor.matmul(nrm[r:r + 32, (f % 2) * T:(f % 2 + 1) * T], cc[:, c, 4 * f + jj + j],
                                             z, start=(n == 0), stop=(n == 3))
                m.then_inc(y_done, 1)

            for s in range(16):
                for nm, n in GATES[2 * s:2 * s + 2]:
                    if (nm, n) == GATES[1]:
                        ssm_b_step(0)
                    hi, lo = (a_hi, a_lo) if nm == "brm" else (x_hi, x_lo)
                    column_unit(UNIT[nm] + n, TILE[nm] + n, hi, lo, al_done if (nm, n) == ("brm", 0) else None, 4)
                if s + 1 < 16:
                    ssm_b_step(s + 1)
                ssm_c_step(s)
            for n in range(16):
                column_unit(UNIT["glu"] + n, TILE["glu"] + n, a_hi, a_lo, al_done if n == 0 else None, 12)
            for n in range(KT):
                column_unit(UNIT["brs"] + n, TILE["brs"] + n, x_hi, x_lo, xl_done if n == 0 else None, KT * SPLITS[7])
            for n in range(KT):
                column_unit(UNIT["out"] + n, TILE["out"] + n, a_hi, a_lo, al_done if n == 0 else None, 20)
            sum_squares(7)

        @block.scalar
        def _(act):
            chain = [0]

            def link(ins):
                chain[0] += 1
                ins.then_inc(act_s, 1)
                act.wait_ge(act_s, chain[0])

            def split(name, a, b):
                for n in range(a, b):
                    split_hi(act, UNIT[name] + n)

            def squares(n, ready):
                for k in range(KT):
                    ready(k)
                    nc.scalar.square(t_buf[:, k], x[:, k]).then_inc(sq_done, 1)
                act.wait_ge(nrm_done, n + 1)
                nc.scalar.activation(rx, nrm[:, 0:T], ACT.Sqrt, bias=con("eps", 1), scale=1.0 / D).then_inc(rt_done, 1)

            def norm_hi(stage):
                n = SPLITS[stage] - 1
                for k in range(KT):
                    act.wait_ge(t_done, KT * n + k + 1)
                    nc.scalar.activation(x_hi[:, k], t_buf[:, k], ACT.Identity,
                                         bias=coef[:, stage, 8 + k:9 + k]).then_inc(xh_done, 1)

            def silu_step(f, j, u, i, per):
                act.wait_ge(used, i * 12 + (u + 1))
                if j >= 2 or per:
                    nd = OWNER[:TILE[f"ffn{f}"]].count("d")
                    if nd + j - 1 > 0:
                        act.wait_ge(freed["d"], i * per + (nd + j - 1))
                nc.scalar.activation(silu_b[:, j % 2], tiles[:, j % 2, 0:T], ACT.Silu).then_inc(silu_done, 1)

            def ffn(f, pre):
                base = FFN_BASE[f]
                for s in range(pre, 4):
                    split_hi(act, base + s)
                split_hi(act, base + 4)
                silu_step(f, 0, base + 1, 0, 0)
                j0 = 2
                for reps, _ in SEGMENTS[f]:
                    with act.Fori(0, reps) as i:
                        for m in range(4):
                            u = g_unit(base, j0 + m)
                            for s in range(3):
                                split_hi(act, u + s, i)
                            silu_step(f, j0 + m - 1, g_unit(base, j0 + m - 1) + 1, i, 4)
                    j0 += 4 * reps
                split_hi(act, o_unit(base, 21))
                silu_step(f, 21, g_unit(base, 21) + 1, 0, 0)

            def head_square(n, src):
                if n:
                    act.wait_ge(hs_done, n)
                nc.scalar.square(rope_sq, src).then_inc(hsq_done, 1)

            def head_root(n):
                act.wait_ge(hs_done, n + 1)
                if n:
                    act.wait_ge(kn_done, n)
                nc.scalar.activation(rh[:], nrm[:], ACT.Sqrt, bias=con("eps", 1),
                                     scale=1.0 / HEAD_DIM).then_inc(hrt_done, 1)

            def head_steps(n0, h, o0, heads):
                if h < HEADS_1 and h % 2:
                    wait_freed(act, o0 + h)
                    head_square(n0 + h // 2, heads[:, h - 1:h + 1])
                if h in (2, 4, 6, 8):
                    head_root(n0 + h // 2 - 1)

            def evacuate(o, src, dst, func=ACT.Copy, **kw):
                wait_tile(act, o)
                nc.scalar.activation(dst, src, func, **kw).then_inc(freed["a"], 1)

            def tile_of(name, n):
                return tiles[:, (TILE[name] + n) % 2, 0:T]

            def exps(n, g, ws, scale):
                sm, pt = ws[g % 2]
                act.wait_ge(mx_done, n + 1)
                for r in range(4):
                    nc.scalar.activation(sm[:, r], sm[:, r], ACT.Exp, bias=att_s[:, g % 2, 4 + r:5 + r], scale=scale,
                                         accum_out=att_s[:, g % 2, 8 + r:9 + r]).then_inc(ex_done, 1)

            def probs_t(n, g, ws, tile):
                sm, pt = ws[g % 2]
                act.wait_ge(pt_done, n + 1)
                if g >= 2:
                    wait_tile(act, tile(g - 2))
                nc.scalar.copy(pt, acc4[:, 2:4, 0:384]).then_inc(pe_done, 1)

            act.wait_ge(vec_in, 16)
            nc.scalar.activation(csil[:], vec("c", 0, 8), ACT.Silu).then_inc(csilu_done, 1)
            link(nc.scalar.activation(ssm_s[:, 0], vec("logdt", 0, 32), ACT.Exp))
            act.wait_ge(ang_done, 1)
            link(nc.scalar.activation(ssm_s[:, 1], ssm_s[:, 2], ACT.Exp))
            act.wait_ge(ang_done, 2)
            nc.scalar.activation(ssm_s[:, 5:7], ssm_s[:, 3:5], ACT.Sin).then_inc(sin_done, 1)
            act.wait_ge(con_in, 16)
            squares(0, lambda k: act.wait_ge(x_in, 16))
            for k in range(3):
                split_hi(act, k)
            norm_hi(0)
            ffn(0, 3)
            split("pool", 0, 2)
            split_hi(act, UNIT["ffn1"])
            squares(1, lambda k: act.wait_ge(x_upd, k + 1))
            for k in range(KT):
                act.wait_ge(t_done, KT + k + 1)
                nc.scalar.copy(x_hi[:, k], t_buf[:, k]).then_inc(xh_done, 1)
            for s in range(1, 3):
                split_hi(act, UNIT["ffn1"] + s)
            squares(2, lambda k: wait_freed(act, TILE["pool"] + k))
            norm_hi(2)
            ffn(1, 3)
            split("kv", 0, 4)
            squares(3, lambda k: act.wait_ge(x_upd, KT + k + 1))
            norm_hi(3)
            for h in range(16):
                if h < HEADS_1:
                    evacuate(TILE["k"] + h, tile_of("k", h), kT[:, h])
                head_steps(0, h, TILE["k"], kT)
                split_hi(act, UNIT["kv"] + h + 4)
            act.wait_ge(used, UNIT["ffn2"])
            nc.scalar.copy(v1[:, 0], acc4[:, 0:2].rearrange("p a b -> p (a b)")).then_inc(v_done, 1)
            norm_hi(4)
            ffn(2, 4)
            split("q", 0, 4)
            squares(4, lambda k: act.wait_ge(x_upd, 2 * KT + k + 1))
            norm_hi(5)
            for h in range(HEADS_1):
                evacuate(TILE["q"] + h, tile_of("q", h), qT[:, h])
                head_steps(4, h, TILE["q"], qT)
                split_hi(act, UNIT["q"] + h + 4)
            head_root(7)

            def att_hi(g):
                wait_tile(act, TILE["att1"] + g)
                nc.scalar.copy(a_hi[:, 2 * g:2 * g + 2],
                               tiles[:, (TILE["att1"] + g) % 2].rearrange("p (h t) -> p h t", h=2)).then_inc(ah_done, 2)

            exps(0, 0, ws1, HEAD_DIM ** -0.5)
            exps(1, 1, ws1, HEAD_DIM ** -0.5)
            for g in range(4):
                probs_t(g, g, ws1, lambda g: TILE["att1"] + g)
                if g + 2 < 4:
                    exps(g + 2, g + 2, ws1, HEAD_DIM ** -0.5)
                att_hi(g)
            for n in range(4, 8):
                split_hi(act, UNIT["o"] + n)
            for s in range(4):
                split_hi(act, UNIT["ffn3"] + s)
            squares(5, lambda k: wait_freed(act, TILE["o"] + k))
            norm_hi(6)
            ffn(3, 4)
            split("lat", 0, 4)
            squares(6, lambda k: act.wait_ge(x_upd, 3 * KT + k + 1))
            norm_hi(7)
            next_unit = [UNIT["lat"] + 4]

            def ahead(n=1):
                for _ in range(n):
                    if next_unit[0] < N_UNITS:
                        split_hi(act, next_unit[0])
                        next_unit[0] += 1

            for n in range(4):
                evacuate(TILE["lat"] + n, tile_of("lat", n), lat_raw[:, n])
                ahead()
                wait_freed(act, TILE["lat"] + n)
                nc.scalar.square(lat_sq[:, n], lat_raw[:, n]).then_inc(lsq_done, 1)
            evacuate(TILE["kr"], tile_of("kr", 0)[0:QK_2], kr_buf[0:QK_2, 0])
            ahead()
            act.wait_ge(ang_done, 3)
            nc.scalar.activation(rope2[64:96], ang[64:96, 0:2], ACT.Sin).then_inc(sin_done, 1)
            for n in range(KT):
                evacuate(TILE["u"] + n, tile_of("u", n), uT[:, n])
                ahead()
                if n == 1:
                    act.wait_ge(lsum_done, 1)
                    nc.scalar.activation(rh[:], nrm[:], ACT.Sqrt, bias=con("eps", 1), scale=1.0 / 256).then_inc(lrt_done, 1)
                if n == 3:
                    for k in range(4):
                        act.wait_ge(af_done, k + 1)
                        nc.scalar.copy(a_hi[:, k], lat_n[:, k]).then_inc(ah_done, 1)
            for g in range(8):
                o = TILE["qup"] + g
                evacuate(o, tiles[0:QK_2, o % 2].rearrange("p (h t) -> p h t", h=2), q2[0:QK_2, 2 * g:2 * g + 2])
                if g % 2:
                    ahead()
            for n in range(4):
                for pair in range(2):
                    o = TILE["kvup"] + 3 * n + pair
                    h = 4 * n + 2 * pair
                    evacuate(o, tiles[0:64, o % 2].rearrange("p (h t) -> p h t", h=2), k2[0:64, h:h + 2])
                o = TILE["kvup"] + 3 * n + 2
                evacuate(o, tiles[:, o % 2].rearrange("p (t c) -> p t c", t=2), v2[:, :, 256 * n:256 * (n + 1)])
                ahead()
            exps(4, 0, ws2, QK_2 ** -0.5)
            exps(5, 1, ws2, QK_2 ** -0.5)
            for g in range(8):
                probs_t(4 + g, g, ws2, att2_tile)
                if g + 2 < 8:
                    exps(6 + g, g + 2, ws2, QK_2 ** -0.5)
                evacuate(zm_tile(g), tiles[:, zm_tile(g) % 2, 0:T], zm[:, g])
                ahead()
            wait_freed(act, zm_tile(7))
            nc.scalar.activation(zm, zm, ACT.Silu).then_inc(zm_done, 1)
            for n in range(KT):
                act.wait_ge(af_done, 4 + n + 1)
                nc.scalar.copy(a_hi[:, n], t_buf[:, n]).then_inc(ah_done, 1)

            def gelu_tile(f):
                act.wait_ge(yp_done, f + 1)
                nc.scalar.activation(gel[:, f], gel[:, f], ACT.Gelu_apprx_tanh).then_inc(gel_done, 1)

            def gelu_hi(f):
                act.wait_ge(gel_done, f + 1)
                nc.scalar.copy(a_hi[:, f], gel[:, f]).then_inc(ah_done, 1)

            for s in range(16):
                for nm, n in GATES[2 * s:2 * s + 2]:
                    o = TILE[nm] + n
                    if nm == "glm":
                        evacuate(o, tile_of(nm, n), mrg[:, n], ACT.Sigmoid)
                    elif nm == "zs":
                        evacuate(o, tile_of(nm, n), zs_t[:, n], ACT.Silu)
                    elif nm == "gls":
                        evacuate(o, tile_of(nm, n), gs_t[:, n], ACT.Sigmoid)
                    ahead()
                for f in {9: (0, 1, 2, 3), 15: (4, 5, 6)}.get(s, ()):
                    gelu_tile(f)
                for f in {9: (0, 1, 2, 3), 15: (4, 5, 6)}.get(s, ()):
                    gelu_hi(f)
            gelu_tile(7)
            gelu_hi(7)
            for n in range(KT):
                if n >= 2:
                    act.wait_ge(gv_done, n - 1)
                evacuate(TILE["glu"] + 2 * n, tile_of("glu", 2 * n), sig_t[:, n % 2], ACT.Sigmoid,
                         bias=vec("b_glu", 8 + n))
                ahead(2)
                if n >= 1:
                    act.wait_ge(gv_done, n)
                    nc.scalar.copy(x_hi[:, n - 1], gel[:, n - 1]).then_inc(xh_done, 1)
            act.wait_ge(gv_done, KT)
            nc.scalar.copy(x_hi[:, 7], gel[:, 7]).then_inc(xh_done, 1)
            for n in range(KT):
                ahead()
                act.wait_ge(af_done, 12 + n + 1)
                nc.scalar.copy(a_hi[:, n], mrg[:, n]).then_inc(ah_done, 1)
            for n in range(KT):
                evacuate(TILE["out"] + n, tile_of("out", n), o_raw[:, n])
                ahead()
                wait_freed(act, TILE["out"] + n)
                nc.scalar.square(t_buf[:, n], o_raw[:, n]).then_inc(sq_done, 1)
            act.wait_ge(nrm_done, 8)
            nc.scalar.activation(rx, nrm[:, 0:T], ACT.Sqrt, bias=con("eps", 1), scale=1.0 / D).then_inc(rt_done, 1)

        @block.vector
        def _(dve):
            chain = [0]
            blocks = [G_PRE]
            V = nc.vector

            def link(ins):
                chain[0] += 1
                ins.then_inc(dve_s, 1)
                dve.wait_ge(dve_s, chain[0])

            def g_part(b, k, vector, i=0):
                cv = csil[:, k:k + 1] if vector == "silu" else vec("c2", k)
                acc, rows = g_acc[:, b % 2], g_land[:, b % 2, k]
                if k == 0:
                    dve.wait_ge(g_landed[b % 2], i * 16 + 16 * (b // 2 + 1))
                    if b >= 2:
                        dve.wait_ge(g_red, i * 2 + (b - 1))
                    V.tensor_scalar(acc, rows, cv, None, ALU.mult).then_inc(g_step, 1)
                else:
                    dve.wait_ge(g_step, i * 14 + (7 * b + k))
                    V.scalar_tensor_tensor(out=acc, in0=rows, scalar=cv, in1=acc, op0=ALU.mult,
                                           op1=ALU.add).then_inc(g_done if k == 7 else g_step, 1)

            def g_block(b):
                for k in range(8):
                    g_part(b, k, "silu")

            def hidden(f, j, i, per):
                base, nd = FFN_BASE[f], OWNER[:TILE[f"ffn{f}"]].count("d")
                J = FFN_TILES * f + j
                dve.wait_ge(silu_done, i * per + (J + 1))
                V.tensor_tensor(hid[:, j % 2], silu_b[:, j % 2], tiles[:, j % 2, T:2 * T],
                                ALU.mult).then_inc(freed["d"], 1)
                dve.wait_ge(freed["d"], i * per + (nd + j + 1))
                if j >= 2 or per:
                    dve.wait_ge(used, i * 12 + (base + 3 * (j - 2) + 4 + 1))
                V.tensor_copy(h_hi[:, j % 2], hid[:, j % 2]).then_inc(hh_done, 1)
                dve.wait_ge(hh_done, i * per + (J + 1))
                V.tensor_tensor(h_lo[:, j % 2], hid[:, j % 2], h_hi[:, j % 2].bitcast(F32),
                                ALU.subtract).then_inc(h_done, 1)

            def gate_coef(stage, col, weight):
                dve.wait_ge(g_red, blocks[0])
                link(V.tensor_tensor(coef[:, stage, 24:32], mods[:, col:col + 8], vec("bias", col, 8), ALU.add))
                if isinstance(weight, float):
                    link(V.tensor_scalar(coef[:, stage, 16:24], coef[:, stage, 24:32], 1.0, weight, ALU.add, ALU.mult))
                else:
                    link(V.scalar_tensor_tensor(out=coef[:, stage, 16:24], in0=coef[:, stage, 24:32], scalar=1.0,
                                                in1=weight, op0=ALU.add, op1=ALU.mult))

            def norm_coef(stage):
                sh, sc, (gname, g0) = STAGE[stage]
                dve.wait_ge(g_red, blocks[0])
                link(V.tensor_tensor(coef[:, stage, 24:32], mods[:, sc:sc + 8], vec("bias", sc, 8), ALU.add))
                link(V.scalar_tensor_tensor(out=coef[:, stage, 0:8], in0=coef[:, stage, 24:32], scalar=1.0,
                                            in1=vec(gname, g0, 8), op0=ALU.add, op1=ALU.mult))
                link(V.tensor_tensor(coef[:, stage, 8:16], mods[:, sh:sh + 8], vec("bias", sh, 8), ALU.add))

            def root(n):
                dve.wait_ge(rt_done, n + 1)
                link(V.reciprocal(rx, rx))

            def norm_t(stage):
                for k in range(KT):
                    V.scalar_tensor_tensor(out=t_buf[:, k], in0=x[:, k], scalar=coef[:, stage, k:k + 1], in1=rx,
                                           op0=ALU.mult, op1=ALU.mult).then_inc(t_done, 1)
                    if k >= 1:
                        norm_lo(stage, k - 1)
                norm_lo(stage, KT - 1)

            def norm_lo(stage, k):
                n = SPLITS[stage] - 1
                dve.wait_ge(xh_done, KT * n + k + 1)
                dve.wait_ge(t_done, KT * n + k + 1)
                V.scalar_tensor_tensor(out=x_lo[:, k], in0=t_buf[:, k], scalar=coef[:, stage, 8 + k:9 + k],
                                       in1=x_hi[:, k].bitcast(F32), op0=ALU.add, op1=ALU.subtract).then_inc(xl_done, 1)

            def update(k, src, stage, signal):
                V.scalar_tensor_tensor(out=x[:, k], in0=src, scalar=coef[:, stage, 16 + k:17 + k], in1=x[:, k],
                                       op0=ALU.mult, op1=ALU.add).then_inc(signal, 1)

            def ffn(f, stage, pre, gate_col, ahead_units):
                base, b = FFN_BASE[f], G_FFN[f]
                for s in range(pre, 5):
                    split_lo(dve, base + s)
                hidden(f, 0, 0, 0)
                if G_FIRST[f]:
                    g_block(b)
                    b += 1
                j0 = 2
                for reps, vector in SEGMENTS[f]:
                    with dve.Fori(0, reps) as i:
                        for m in range(4):
                            j, u = j0 + m, g_unit(base, j0 + m)
                            for s in range(3):
                                split_lo(dve, u + s, i)
                                if vector:
                                    g_part(b + m // 2, 4 * (m % 2) + s, vector, i)
                            hidden(f, j - 1, i, 4)
                            if vector:
                                g_part(b + m // 2, 4 * (m % 2) + 3, vector, i)
                    j0 += 4 * reps
                    b += 2 * reps if vector else 0
                blocks[0] = b
                split_lo(dve, o_unit(base, 21))
                hidden(f, 21, 0, 0)
                for u in ahead_units:
                    split_lo(dve, u)
                gate_coef(stage, gate_col, 0.5)
                dve.wait_ge(used, base + 66)
                for k in range(KT):
                    update(k, yT[k], stage, x_upd)

            def reduce_angle(th, out_s, out_c, tmp, tmp2):
                for out_, quarter in ((out_s, 0.0), (out_c, 0.25)):
                    link(V.tensor_scalar(tmp, th, 1.0 / TWO_PI, quarter, ALU.mult, ALU.add))
                    link(V.tensor_scalar(tmp, tmp, 12582912.0, None, ALU.add))
                    link(V.tensor_scalar(tmp, tmp, -12582912.0, None, ALU.add))
                    link(V.scalar_tensor_tensor(out=tmp2, in0=tmp, scalar=-6.28125, in1=th, op0=ALU.mult, op1=ALU.add))
                    link(V.scalar_tensor_tensor(out=tmp2, in0=tmp, scalar=-0.0019350051879882812, in1=tmp2,
                                                op0=ALU.mult, op1=ALU.add))
                    link(V.scalar_tensor_tensor(out=tmp2, in0=tmp, scalar=-(TWO_PI - 6.28125 - 0.0019350051879882812),
                                                in1=tmp2, op0=ALU.mult, op1=ALU.add))
                    link(V.tensor_scalar(tmp2, tmp2, quarter * TWO_PI, 3.1415925, ALU.add, ALU.min))
                    link(V.tensor_scalar(out_, tmp2, -3.1415925, None, ALU.max))

            dve.wait_ge(act_s, 1)
            S = lambda n: ssm_s[:, n]
            lr, li = vec("lr", 0, 32), vec("li", 0, 32)
            V.tensor_tensor(S(2), lr, S(0), ALU.mult).then_inc(ang_done, 1)
            link(V.tensor_tensor(S(7), li, S(0), ALU.mult))
            reduce_angle(S(7), S(4), S(3), S(8), S(9))
            V.tensor_copy(S(19), S(8)).then_inc(ang_done, 1)
            dve.wait_ge(act_s, 2)
            dve.wait_ge(sin_done, 1)
            link(V.tensor_tensor(S(10), S(1), S(5), ALU.mult))
            link(V.tensor_scalar(S(10), S(10), -1.0, None, ALU.add))
            link(V.tensor_tensor(S(11), S(1), S(6), ALU.mult))
            link(V.tensor_tensor(S(12), lr, lr, ALU.mult))
            link(V.tensor_tensor(S(13), li, li, ALU.mult))
            link(V.tensor_tensor(S(12), S(12), S(13), ALU.add))
            link(V.reciprocal(S(12), S(12)))
            link(V.tensor_tensor(S(13), S(10), lr, ALU.mult))
            link(V.tensor_tensor(S(14), S(11), li, ALU.mult))
            link(V.tensor_tensor(S(13), S(13), S(14), ALU.add))
            link(V.tensor_tensor(S(13), S(13), S(12), ALU.mult))
            link(V.tensor_tensor(S(14), S(11), lr, ALU.mult))
            link(V.tensor_tensor(S(15), S(10), li, ALU.mult))
            link(V.tensor_tensor(S(14), S(14), S(15), ALU.subtract))
            V.tensor_tensor(S(14), S(14), S(12), ALU.mult).then_inc(f_done, 1)
            dve.wait_ge(csilu_done, 1)
            dve.wait_ge(vec_in, 16)
            for b in range(G_PRE):
                g_block(b)
            norm_coef(0)
            root(0)
            split_lo(dve, 0)
            norm_t(0)
            split_lo(dve, 1)
            split_lo(dve, 2)

            def rng(name, a, b):
                return range(UNIT[name] + a, UNIT[name] + b)

            def split(units):
                for u in units:
                    split_lo(dve, u)

            ffn(0, 0, 3, 16, [*rng("pool", 0, 2), UNIT["ffn1"]])

            g_block(G_PRE + 11)
            blocks[0] += 1
            norm_coef(1)
            gate_coef(1, 40, vec("pool_scale", 0, 8))
            dve.wait_ge(base_done, 1)
            link(V.memset(win_h[:, :, 0:PAD], 0.0))
            link(V.memset(win_a[:, :, 0:PAD], 0.0))
            link(V.memset(win_b[:, :, 0:PAD], 0.0))
            root(1)
            for k in range(KT):
                link(V.scalar_tensor_tensor(out=win_h[:, k, PAD:], in0=x[:, k], scalar=coef[:, 1, k:k + 1], in1=rx,
                                            op0=ALU.mult, op1=ALU.mult))
            for k in range(KT):
                link(V.tensor_scalar(win_h[:, k, PAD:], win_h[:, k, PAD:], coef[:, 1, 8 + k:9 + k], None, ALU.add))
            for g, w in enumerate(POOL_W):
                k0 = 2 * g
                src, dst = win_h[:, k0:k0 + 2], win_a[:, k0:k0 + 2]
                for level in range(g + 1):
                    sh = 1 << level
                    link(V.tensor_tensor(dst[:, :, PAD:], src[:, :, PAD:], src[:, :, PAD - sh:PAD + T - sh], ALU.add))
                    src, dst = dst, (win_b[:, k0 - 2:k0] if level % 2 == 0 and g else win_a[:, k0:k0 + 2])
                h2, t2 = win_h[:, k0:k0 + 2], t_buf[:, k0:k0 + 2]
                link(V.scalar_tensor_tensor(out=t2, in0=src[:, :, PAD:], scalar=1.0 / w, in1=h2[:, :, PAD:],
                                            op0=ALU.mult, op1=ALU.subtract))
                cnt = cons[:, CON["cnt"] + 16 * g:CON["cnt"] + 16 * (g + 1)].unsqueeze(1).to_broadcast([P, 2, 16])
                link(V.tensor_tensor(t2[:, :, 0:16], src[:, :, PAD:PAD + 16], cnt, ALU.mult))
                V.tensor_tensor(t2[:, :, 0:16], t2[:, :, 0:16], h2[:, :, PAD:PAD + 16], ALU.subtract).then_inc(t_done, 2)
                dve.wait_ge(t_done, KT + k0 + 2)
                dve.wait_ge(xh_done, KT + k0 + 2)
                V.tensor_tensor(x_lo[:, k0:k0 + 2], t2, x_hi[:, k0:k0 + 2].bitcast(F32), ALU.subtract).then_inc(xl_done, 2)
            for k in range(KT):
                wait_tile(dve, TILE["pool"] + k)
                update(k, tiles[:, k % 2, 0:T], 1, freed["d"])
                if k in (2, 5):
                    split_lo(dve, UNIT["ffn1"] + 1 + k // 5)
            norm_coef(2)
            root(2)
            norm_t(2)
            ffn(1, 2, 3, 64, rng("kv", 0, 4))

            def head_norm(n, raw, weight):
                dve.wait_ge(hrt_done, n + 1)
                link(V.reciprocal(rh[:], rh[:]))
                V.scalar_tensor_tensor(out=rope_kn, in0=raw, scalar=weight, in1=rh[:].rearrange("p (h t) -> p h t", h=2),
                                       op0=ALU.mult, op1=ALU.mult).then_inc(kn_done, 1)
                dve.wait_ge(kn_done, n + 1)
                V.tensor_tensor(rope_t[:, 0], rope_kn, cos1.unsqueeze(1).to_broadcast([P, 2, T]), ALU.mult)

            def head_rope(n, raw):
                dve.wait_ge(hrot_done, n + 1)
                m = V.tensor_tensor(rope_t[:, 1], nrm[:].rearrange("p (h t) -> p h t", h=2),
                                    sin1.unsqueeze(1).to_broadcast([P, 2, T]), ALU.mult)
                m.then_inc(hread_done, 1)
                dve.wait_ge(hread_done, n + 1)
                V.tensor_tensor(raw, rope_t[:, 0], rope_t[:, 1], ALU.add).then_inc(rope_done, 1)

            def head_steps(n0, h, heads, weight):
                if h in (5, 7, 9, 11):
                    n = (h - 5) // 2
                    head_rope(n0 + n, heads[:, 2 * n:2 * n + 2])
                if h in (3, 5, 7, 9):
                    n = (h - 3) // 2
                    head_norm(n0 + n, heads[:, 2 * n:2 * n + 2], weight)

            norm_coef(3)
            root(3)
            norm_t(3)
            for h in range(16):
                head_steps(0, h, kT, vec("k_norm"))
                split_lo(dve, UNIT["kv"] + h + 4)
            norm_coef(4)
            dve.wait_ge(used, UNIT["ffn2"])
            V.tensor_copy(v1[:, 1], acc4[:, 2:4].rearrange("p a b -> p (a b)")).then_inc(v_done, 1)
            norm_t(4)
            ffn(2, 4, 4, 104, rng("q", 0, 4))

            def scores_max(n, g, ws):
                sm, pt = ws[g % 2]
                scale = HEAD_DIM ** -0.5 if n < 4 else QK_2 ** -0.5
                dve.wait_ge(s_done, n + 1)
                if g >= 2:
                    dve.wait_ge(pt_done, n - 1)
                V.tensor_tensor(sm.rearrange("p (h q) t -> p h (q t)", h=2), acc4[:, 0:2],
                                con("mask", 2 * T).unsqueeze(1).to_broadcast([P, 2, 2 * T]), ALU.add).then_inc(sm_done, 1)
                dve.wait_ge(sm_done, n + 1)
                link(V.tensor_reduce(att_s[:, g % 2, 0:4], sm, AX, ALU.max))
                V.tensor_scalar(att_s[:, g % 2, 4:8], att_s[:, g % 2, 0:4], -scale, None, ALU.mult).then_inc(mx_done, 1)

            def normalise(n, g, ws):
                sm, pt = ws[g % 2]
                dve.wait_ge(ex_done, 4 * (n + 1))
                link(V.reciprocal(att_s[:, g % 2, 12:16], att_s[:, g % 2, 8:12]))
                for r in range(4):
                    V.tensor_scalar(sm[:, r], sm[:, r], att_s[:, g % 2, 12 + r:13 + r], None, ALU.mult).then_inc(pn_done, 1)

            def att_lo(g):
                dve.wait_ge(ah_done, 2 * g + 2)
                V.tensor_tensor(a_lo[:, 2 * g:2 * g + 2], tiles[:, (TILE["att1"] + g) % 2].rearrange("p (h t) -> p h t", h=2),
                                a_hi[:, 2 * g:2 * g + 2].bitcast(F32), ALU.subtract).then_inc(freed["d"], 1)

            norm_coef(5)
            root(4)
            norm_t(5)
            for h in range(HEADS_1):
                head_steps(4, h, qT, vec("q_norm"))
                split_lo(dve, UNIT["q"] + h + 4)
            head_steps(4, 9, qT, vec("q_norm"))
            head_steps(4, 11, qT, vec("q_norm"))
            scores_max(0, 0, ws1)
            scores_max(1, 1, ws1)
            normalise(0, 0, ws1)
            for g in range(4):
                if g + 1 < 4:
                    normalise(g + 1, g + 1, ws1)
                if g + 2 < 4:
                    scores_max(g + 2, g + 2, ws1)
                att_lo(g)
            gate_coef(5, 128, 1.0)
            for k in range(KT):
                split_lo(dve, UNIT["o"] + 4 + k)
                wait_tile(dve, TILE["o"] + k)
                update(k, tiles[:, k % 2, 0:T], 5, freed["d"])
            norm_coef(6)
            root(5)
            norm_t(6)
            ffn(3, 6, 4, 152, rng("lat", 0, 4))

            next_unit = [UNIT["lat"] + 4]

            def ahead(n=1):
                for _ in range(n):
                    if next_unit[0] < N_UNITS:
                        split_lo(dve, next_unit[0])
                        next_unit[0] += 1

            def a_part(k, src, ah, signal):
                dve.wait_ge(ah_done, ah)
                V.tensor_tensor(a_lo[:, k], src, a_hi[:, k].bitcast(F32), ALU.subtract).then_inc(signal, 1)

            norm_coef(7)
            root(6)
            norm_t(7)
            ahead(1)
            R = slice(64, 96)
            dve.wait_ge(xl_done, KT * SPLITS[7])
            dve.wait_ge(pos_in, 16)
            link(V.tensor_copy(ang[R, 2], pos_i[R].bitcast(I32)))
            link(V.tensor_scalar(ang[R, 3], ang[R, 2], con("invf", 1)[R], None, ALU.mult))
            reduce_angle(ang[R, 3], ang[R, 1], ang[R, 0], ang[R, 4], ang[R, 5])
            V.memset(rope2[0:64, 0], 1.0)
            V.memset(rope2[0:64, 1], 0.0)
            V.tensor_copy(ang[R, 5], ang[R, 4]).then_inc(ang_done, 1)
            ahead(4)
            for n in range(KT):
                ahead()
                if n == 2:
                    dve.wait_ge(lrt_done, 1)
                    link(V.reciprocal(rh[:], rh[:]))
                    for k in range(4):
                        V.scalar_tensor_tensor(out=lat_n[:, k], in0=lat_raw[:, k],
                                               scalar=vec("g_q", k) if k < 2 else vec("g_kv", k - 2),
                                               in1=rh[:, (k // 2) * T:(k // 2 + 1) * T], op0=ALU.mult,
                                               op1=ALU.mult).then_inc(af_done, 1)
                if n == 4:
                    dve.wait_ge(krot_done, 1)
                    dve.wait_ge(sin_done, 2)
                    V.tensor_tensor(kr_buf[R, 1], kr_buf[R, 0], rope2[R, 0], ALU.mult)
                    link(V.tensor_tensor(kr_buf[R, 2], acc4[R, 2, 0:T], rope2[R, 1], ALU.mult))
                    V.tensor_tensor(kr_buf[R, 1], kr_buf[R, 1], kr_buf[R, 2], ALU.add).then_inc(kr_done, 1)
                    dve.wait_ge(af_done, 4)
                    for k in range(4):
                        a_part(k, lat_n[:, k], 8 + k + 1, al_done)
            for n in range(4):
                ahead()

            def q_rope(g):
                pair = q2[0:QK_2, 2 * g:2 * g + 2]
                c2, s2 = (rope2[:, n].unsqueeze(1).to_broadcast([QK_2, 2, T]) for n in range(2))
                if g:
                    dve.wait_ge(qrope_done, g)
                dve.wait_ge(qrot_done, g + 1)
                V.tensor_tensor(rope_t[0:QK_2, 0], pair, c2, ALU.mult)
                link(V.tensor_tensor(rope_t[0:QK_2, 1], acc4[0:QK_2, g % 2].rearrange("p (h t) -> p h t", h=2), s2, ALU.mult))
                V.tensor_tensor(pair, rope_t[0:QK_2, 0], rope_t[0:QK_2, 1], ALU.add).then_inc(qrope_done, 1)

            for n in range(4):
                ahead()
                q_rope(2 * n)
                q_rope(2 * n + 1)

            def att2_out(g):
                wait_tile(dve, att2_tile(g))
                V.tensor_copy(ym[:, g], tiles[:, att2_tile(g) % 2, 0:T]).then_inc(freed["d"], 1)

            dve.wait_ge(mask_in, 16)
            scores_max(4, 0, ws2)
            scores_max(5, 1, ws2)
            normalise(4, 0, ws2)
            for g in range(8):
                if g + 1 < 8:
                    normalise(5 + g, g + 1, ws2)
                if g + 2 < 8:
                    scores_max(6 + g, g + 2, ws2)
                att2_out(g)
                ahead()
            wait_freed(dve, att2_tile(7))
            dve.wait_ge(zm_done, 1)
            for n in range(KT):
                V.tensor_tensor(t_buf[:, n], ym[:, n], zm[:, n], ALU.mult).then_inc(af_done, 1)
                if n:
                    dve.wait_ge(af_done, 4 + n)
                    a_part(n - 1, t_buf[:, n - 1], 12 + n, al_done)
            dve.wait_ge(af_done, 12)
            a_part(7, t_buf[:, 7], 20, al_done)

            def ssm_step(s):
                f, jj = s // 2, 2 * (s % 2)
                cs, sn = rot_t[s % 2][:, 0], rot_t[s % 2][:, 1]
                v, (m0, m1) = ssm_v[s % 2], ssm_m[s % 2]
                bur, bui = acc4[:, jj:jj + 2, 0:T], acc4[:, jj:jj + 2, T:2 * T]
                dve.wait_ge(tab_done, s + 1)
                dve.wait_ge(bu_done, s + 1)
                if s >= 2:
                    dve.wait_ge(y_done, s - 1)
                V.tensor_tensor(v[:, 0], bur, cs, ALU.mult)
                V.tensor_tensor(m0, bui, sn, ALU.mult)
                V.tensor_tensor(v[:, 1], bui, cs, ALU.mult)
                link(V.tensor_tensor(m1, bur, sn, ALU.mult))
                V.tensor_tensor(v[:, 0], v[:, 0], m0, ALU.add).then_inc(bu_free, 1)
                link(V.tensor_tensor(v[:, 1], v[:, 1], m1, ALU.subtract))
                for c in range(2):
                    for j in range(2):
                        mag = ssm_s[:, 1, 4 * f + jj + j:4 * f + jj + j + 1].to_broadcast([P, T])
                        m = V.tensor_tensor_scan(v[:, c, j], mag, v[:, c, j], 0.0, ALU.mult, ALU.add)
                    if c == 0:
                        m.then_inc(vs_done, 1)
                link(m)
                link(V.scalar_tensor_tensor(out=m0, in0=v[:, 1], scalar=-1.0, in1=sn, op0=ALU.mult, op1=ALU.mult))
                V.tensor_tensor(v[:, 1], v[:, 1], cs, ALU.mult).then_inc(zz_done, 1)

            def y_tile(f):
                dve.wait_ge(y_done, 2 * f + 2)
                V.scalar_tensor_tensor(out=gel[:, f], in0=uT[:, f], scalar=vec("ssm_d", f),
                                       in1=nrm[:, (f % 2) * T:(f % 2 + 1) * T], op0=ALU.mult, op1=ALU.add).then_inc(yp_done, 1)

            for s in range(16):
                ssm_step(s)
                if s >= 2 and s % 2 == 0:
                    y_tile(s // 2 - 1)
                for nm, n in GATES[2 * s:2 * s + 2]:
                    ahead()
                    if nm == "brm":
                        wait_tile(dve, TILE["brm"] + n)
                        wait_freed(dve, TILE["glm"] + n)
                        V.tensor_tensor(mrg[:, n], tiles[:, (TILE["brm"] + n) % 2, 0:T], mrg[:, n],
                                        ALU.mult).then_inc(freed["d"], 1)
                if s == 11:
                    for f in range(4):
                        a_part(f, gel[:, f], 20 + f + 1, al_done)
            y_tile(7)
            for f in range(4, 8):
                a_part(f, gel[:, f], 20 + f + 1, al_done)
            for n in range(KT):
                wait_tile(dve, TILE["glu"] + 2 * n + 1)
                wait_freed(dve, TILE["glu"] + 2 * n)
                V.scalar_tensor_tensor(out=gel[:, n], in0=tiles[:, (TILE["glu"] + 2 * n + 1) % 2, 0:T],
                                       scalar=vec("b_glu", n), in1=sig_t[:, n % 2],                      op0=ALU.add, op1=ALU.mult).then_inc(freed["d"], 1)
                wait_freed(dve, TILE["glu"] + 2 * n + 1)
                V.tensor_tensor(gel[:, n], gel[:, n], zs_t[:, n], ALU.mult).then_inc(gv_done, 1)
                ahead(2)
                if n:
                    dve.wait_ge(xh_done, KT * SPLITS[7] + n)
                    V.tensor_tensor(x_lo[:, n - 1], gel[:, n - 1], x_hi[:, n - 1].bitcast(F32),
                                    ALU.subtract).then_inc(xl_done, 1)
            dve.wait_ge(xh_done, KT * SPLITS[7] + KT)
            V.tensor_tensor(x_lo[:, 7], gel[:, 7], x_hi[:, 7].bitcast(F32), ALU.subtract).then_inc(xl_done, 1)
            for n in range(KT):
                wait_tile(dve, TILE["brs"] + n)
                V.tensor_tensor(gel[:, n], tiles[:, (TILE["brs"] + n) % 2, 0:T], gs_t[:, n], ALU.mult).then_inc(freed["d"], 1)
                wait_freed(dve, TILE["brs"] + n)
                V.tensor_tensor(mrg[:, n], mrg[:, n], gel[:, n], ALU.add).then_inc(af_done, 1)
                ahead()
                if n:
                    a_part(n - 1, mrg[:, n - 1], 28 + n, al_done)
            a_part(7, mrg[:, 7], 36, al_done)
            ahead(KT)
            dve.wait_ge(g_red, N_G)
            link(V.tensor_tensor(coef[:, 8, 24:32], mods[:, 176:184], vec("bias", 176, 8), ALU.add))
            link(V.tensor_tensor(coef[:, 8, 0:8], coef[:, 8, 24:32], vec("g_post", 0, 8), ALU.mult))
            root(7)
            for k in range(KT):
                link(V.scalar_tensor_tensor(out=t_buf[:, k], in0=o_raw[:, k], scalar=coef[:, 8, k:k + 1], in1=rx,
                                            op0=ALU.mult, op1=ALU.mult))
                V.tensor_tensor(x[:, k], x[:, k], t_buf[:, k], ALU.add).then_inc(fin_done, 1)

        @block.gpsimd
        def _(pool):
            chain = [0]
            G = nc.gpsimd

            def link(ins):
                chain[0] += 1
                ins.then_inc(pool_s, 1)
                pool.wait_ge(pool_s, chain[0])

            def cmul(out_, a, b, tmp, last=None):
                (ar, ai), (br, bi) = a, b
                link(G.tensor_tensor(out_[0], ar, br, ALU.mult))
                link(G.tensor_tensor(tmp, ai, bi, ALU.mult))
                link(G.tensor_tensor(out_[0], out_[0], tmp, ALU.subtract))
                link(G.tensor_tensor(out_[1], ar, bi, ALU.mult))
                link(G.tensor_tensor(tmp, ai, br, ALU.mult))
                m = G.tensor_tensor(out_[1], out_[1], tmp, ALU.add)
                if last is None:
                    link(m)
                else:
                    m.then_inc(last, 1)

            pool.wait_ge(sin_done, 1)
            p, spare = ssm_s[:, 5:7], [ssm_s[:, 16:18], ssm_s[:, 8:10]]
            tmp = region(40, [32, 16])
            step = 0
            for table, n in ((base_t, CH), (chunk_t, NCH)):
                link(G.memset(table[:, 0, :, 0:1], 1.0))
                link(G.memset(table[:, 1, :, 0:1], 0.0))
                w = 1
                while w < n:
                    cmul([table[:, c, :, w:2 * w] for c in range(2)], [table[:, c, :, 0:w] for c in range(2)],
                         [p[:, c].unsqueeze(2).to_broadcast([P, 32, w]) for c in range(2)], tmp[:, :, 0:w])
                    q = spare[step % 2]
                    cmul([q[:, 0], q[:, 1]], [p[:, 0], p[:, 1]], [p[:, 0], p[:, 1]], tmp[:, 0:2].rearrange("p a b -> p (a b)"))
                    p, w, step = q, 2 * w, step + 1
            G.memset(tmp[:, 0, 0:1], 0.0).then_inc(base_done, 1)
            pool.wait_ge(kr_done, 1)
            G.tensor_copy(k2[64:96], kr_buf[64:96, 1].unsqueeze(1).to_broadcast([32, HEADS_2, T])).then_inc(kb_done, 1)
            pool.wait_ge(c_in, 16)
            pool.wait_ge(f_done, 1)
            for half in (slice(0, 16), slice(16, 32)):
                fr, fi = (ssm_s[:, n, half].unsqueeze(2).to_broadcast([P, 16, 32]) for n in (13, 14))
                tmp = rh[:].rearrange("p (a b) -> p a b", b=32)
                re, im, cr, ci = c_raw[:, 0, half], c_raw[:, 1, half], cc[:, 0, half], cc[:, 1, half]
                link(G.tensor_tensor(cr, re, fr, ALU.mult))
                link(G.tensor_tensor(tmp, im, fi, ALU.mult))
                link(G.tensor_tensor(cr, cr, tmp, ALU.subtract))
                link(G.tensor_tensor(ci, re, fi, ALU.mult))
                link(G.tensor_tensor(tmp, im, fr, ALU.mult))
                link(G.tensor_tensor(ci, ci, tmp, ALU.add))
                m = G.tensor_scalar(ci, ci, -1.0, None, ALU.mult)
                if half.start:
                    m.then_inc(cc_done, 1)
                else:
                    link(m)
            pool.wait_ge(cc_done, 1)

            def table_step(s):
                j = 2 * s
                if s >= 2:
                    pool.wait_ge(zz_done, s - 1)
                a = [base_t[:, c, j:j + 2].unsqueeze(2).to_broadcast([P, 2, NCH, CH]) for c in range(2)]
                b = [chunk_t[:, c, j:j + 2].unsqueeze(3).to_broadcast([P, 2, NCH, CH]) for c in range(2)]
                o = [rot_t[s % 2][:, c].rearrange("p j (a b) -> p j a b", b=CH) for c in range(2)]
                cmul(o, a, b, rh[:].rearrange("p (j a b) -> p j a b", j=2, b=CH), tab_done)

            table_step(0)
            pool.wait_ge(tab_done, 1)
            table_step(1)
            for s in range(16):
                v, m1 = ssm_v[s % 2], ssm_m[s % 2][1]
                pool.wait_ge(vs_done, s + 1)
                link(G.tensor_tensor(m1, v[:, 0], rot_t[s % 2][:, 1], ALU.mult))
                G.tensor_tensor(v[:, 0], v[:, 0], rot_t[s % 2][:, 0], ALU.mult).then_inc(zp_done, 1)
                if s + 2 < 16:
                    pool.wait_ge(zp_done, s + 1)
                    table_step(s + 2)
                    pool.wait_ge(tab_done, s + 3)


def columns(w):
    k, n = w.shape
    return w.reshape(k // P, P, n // P, P).transpose(2, 1, 0, 3).reshape(n // P, P, -1)


def padded(a):
    return np.pad(a, ((0, 0), (0, 0), (0, WIDTH - a.shape[2])))


def ffn_units(w_in, w_out):
    gate_up, rows = columns(w_in), w_out.reshape(FFN_TILES, P, D)
    out = np.empty((66, P, WIDTH), w_in.dtype)
    for j in range(FFN_TILES):
        out[g_unit(0, j)] = gate_up[j]
        out[g_unit(0, j) + 1] = gate_up[FFN_TILES + j]
        out[o_unit(0, j)] = rows[j]
    return out


def tiled(v):
    return np.asarray(v).reshape(-1, P).T


def constants():
    c = np.zeros((P, NC_), np.float32)
    put = lambda name, a: c.__setitem__((slice(0, a.shape[0]), slice(CON[name], CON[name] + a.shape[1])), a)
    put("ident", np.eye(P, dtype=np.float32))
    put("ones", np.ones((P, P), np.float32))
    for name, first, half in (("rot1", 0, 64), ("rot2", 64, 16)):
        m = np.zeros((P, P if name == "rot1" else QK_2), np.float32)
        for i in range(half):
            m[first + half + i, first + i] = -1.0
            m[first + i, first + half + i] = 1.0
        put(name, m[:m.shape[1]] if name == "rot2" else m)
    pos = np.arange(T, dtype=np.float32)
    inv = (10000.0 ** (-np.arange(0, HEAD_DIM, 2, dtype=np.float32) / HEAD_DIM)).astype(np.float32)
    ang = (inv[:, None] * pos[None, :]).astype(np.float32)
    put("cos1", np.tile(np.cos(ang), (2, 1)).astype(np.float32))
    put("sin1", np.tile(np.sin(ang), (2, 1)).astype(np.float32))
    q = np.arange(P)[:, None, None] + P * np.arange(2)[None, :, None]
    k = np.arange(T)[None, None, :]
    put("mask", np.where(k <= q, 0.0, -1e30).astype(np.float32).reshape(P, 2 * T))
    mask2 = np.where(k // 64 <= q // 64, 0.0, -1e30).astype(np.float32).reshape(P, 2 * T)
    t = np.arange(PAD)
    put("cnt", np.tile(np.concatenate([1.0 / np.minimum(t + 1, w) for w in POOL_W]).astype(np.float32), (P, 1)))
    inv2 = (10000.0 ** (-np.arange(0, 32, 2, dtype=np.float32) / 32)).astype(np.float32)
    c[64:96, CON["invf"]] = np.tile(inv2, 2)
    c[:, CON["eps"]] = EPS
    return c, mask2


def kernel(**inp):
    import concourse.bacc as bacc
    from concourse.bass_utils import run_bass_kernel_spmd

    a = {name: np.asarray(v) for name, v in inp.items()}
    w_in2 = a["w_in_2"][0]
    parts = [
        ffn_units(a["ffn_w_in"][0, 0], a["ffn_w_out"][0, 0]),
        a["pool_w"][0].reshape(2, 2, 2, P, 256).transpose(0, 3, 1, 2, 4).reshape(2, P, WIDTH),
        ffn_units(a["ffn_w_in"][0, 1], a["ffn_w_out"][0, 1]),
        columns(a["w_kv"][:, :D]), a["w_kv"][:, D:].reshape(KT, P, D),
        ffn_units(a["ffn_w_in"][1, 0], a["ffn_w_out"][1, 0]),
        columns(a["w_q"][0]), columns(a["w_o"][0]),
        ffn_units(a["ffn_w_in"][1, 1], a["ffn_w_out"][1, 1]),
        columns(w_in2[:, 2048:2560]),
        padded(np.pad(w_in2[:, 2560:2592], ((0, 0), (64, 0))).reshape(KT, P, QK_2).transpose(1, 0, 2).reshape(1, P, -1)),
        columns(w_in2[:, 0:1024]),
        padded(a["w_q_up_2"][0].reshape(2, P, 4, 384).transpose(2, 1, 0, 3).reshape(4, P, -1)),
        a["w_kv_up_2"][0].reshape(2, P, 4, 512).transpose(2, 1, 0, 3).reshape(4, P, -1),
        columns(w_in2[:, 2592:3616]),
        columns(w_in2[:, 4640:5664]),
        columns(a["w_br_mla_2"][0]),
        columns(w_in2[:, 1024:2048]),
        columns(w_in2[:, 3616:4640]),
        columns(a["w_glu_2"][0]).reshape(2, KT, P, WIDTH)[::-1].transpose(1, 0, 2, 3).reshape(16, P, WIDTH),
        columns(a["w_br_ssm_2"][0]),
        columns(a["w_out_2"][0]),
    ]
    stream = np.concatenate(parts)
    blocks = lambda w: w.reshape(8, P, -1, GW).transpose(2, 1, 0, 3)
    gstream = np.concatenate([blocks(a["ada_w"][0]), blocks(a["kv_ada_w"]), blocks(a["ada_w"][1]),
                              blocks(a["w_ada_2"][0])])
    bias = np.concatenate([a["ada_b"][0], a["kv_ada_b"], a["ada_b"][1], a["b_ada_2"][0]])
    states = lambda v: v.reshape(32, P).T
    vecs = np.concatenate([
        tiled(a["c"]), tiled(a["c_2"]), states(np.repeat(a["ssm_log_dt_2"][0], 64)), states(a["ssm_a_re_2"][0]),
        states(a["ssm_a_im_2"][0]), tiled(bias), tiled(a["norm_g"]), tiled(a["pool_scale"]), tiled(a["kv_norm"]),
        tiled(a["k_norm"]), tiled(a["q_norm"]), tiled(a["g_pre_2"]), tiled(a["ssm_d_2"]), tiled(a["b_glu_2"]),
        tiled(a["g_q_norm_2"]), tiled(a["g_kv_norm_2"]), tiled(a["g_post_2"])], axis=1)
    ssm_b = np.zeros((2, KT, 4, 2, 16, 2, 64), np.float32)
    ssm_c = np.zeros((2, 32, 2, 64, 2, 16), np.float32)
    for c, part in enumerate(("re", "im")):
        b = a[f"ssm_b_{part}_2"][0].reshape(KT, 4, 2, 64, 16)
        cc = a[f"ssm_c_{part}_2"][0].reshape(32, 2, 16, 64)
        for g in range(2):
            ssm_b[c, :, :, g, :, g, :] = b[:, :, g].transpose(0, 1, 3, 2)
            ssm_c[c, :, g, :, g, :] = cc[:, g].transpose(0, 2, 1)
    ssm_b = ssm_b.transpose(2, 3, 4, 0, 1, 5, 6).reshape(P, 2, KT, P)
    ssm_c = ssm_c.transpose(2, 3, 0, 1, 4, 5).reshape(P, 2, 32, 32)
    cons, mask2 = constants()
    arrays = {
        "stream": stream, "gstream": gstream, "vecs": vecs, "cons": cons, "mask2": mask2,
        "x_t": a["x"][0].T.reshape(KT, P, T).transpose(1, 0, 2),
        "pos": np.tile(a["positions_2"], (32, 1)).astype(np.int32), "ssm_b": ssm_b, "ssm_c": ssm_c,
    }
    arrays = {name: np.ascontiguousarray(v) for name, v in arrays.items()}
    nc = bacc.Bacc("TRN2", target_bir_lowering=False, num_devices=1)
    args = [nc.dram_tensor(f"in_{name}", v.shape, mybir.dt.from_np(v.dtype), kind="ExternalInput").ap()
            for name, v in arrays.items()]
    out = nc.dram_tensor("out_t", (P, KT, T), F32, kind="ExternalOutput").ap()
    build_program(nc, *args, out)
    r = run_bass_kernel_spmd(nc, [{f"in_{name}": v for name, v in arrays.items()}], core_ids=[0])
    return r.results[0]["out_t"].transpose(1, 0, 2).reshape(D, T).T.reshape(1, T, D)
```

```python
from contextlib import ExitStack

import numpy as np

import concourse.bass as bass
from concourse import mybir

F32 = mybir.dt.float32
F32R = mybir.dt.float32r
I32 = mybir.dt.int32
ALU = mybir.AluOpType
ACT = mybir.ActivationFunctionType
AX = mybir.AxisListType.X

P = 128
D = 1024
KT = D // P
T = 256
FFN_TILES = 22
WIDTH = 1024
EPS = 1e-6
HEADS_1, HEAD_DIM = 8, 128
HEADS_2, QK_2, V_2 = 16, 96, 64
TWO_PI = 6.283185307179586

PHASES = [("ffn0", 66), ("pool", 2), ("ffn1", 66), ("kv", 16), ("ffn2", 66), ("q", 8), ("o", 8), ("ffn3", 66),
          ("lat", 4), ("kr", 1), ("u", 8), ("qup", 4), ("kvup", 4), ("zm", 8), ("glm", 8), ("brm", 8),
          ("zs", 8), ("gls", 8), ("glu", 16), ("brs", 8), ("out", 8)]
UNIT, N_UNITS = {}, 0
for _name, _n in PHASES:
    UNIT[_name] = N_UNITS
    N_UNITS += _n
FFN_BASE = [UNIT[f"ffn{f}"] for f in range(4)]

RING, LAND = 4, 4
GW = 512
N_G = 46
G_PRE, G_POOL = 4, 15
G_FIRST = [1, 1, 1, 0]
SEGMENTS = [[(5, "silu")], [(5, "silu")], [(5, "silu")], [(1, "silu"), (3, "c2"), (1, None)]]
G_FFN = [4, 16, 27, 38]
M_LAYER = [0, 88]
M_KV, M_2 = 72, 160
N_MOD = 184

TILES = [("ffn0", 22, "d"), ("pool", 8, "d"), ("ffn1", 22, "d"), ("k", 8, "a"), ("ffn2", 22, "d"),
         ("q", 8, "a"), ("att1", 4, "d"), ("o", 8, "d"), ("ffn3", 22, "d"), ("lat", 4, "a"), ("kr", 1, "a"),
         ("u", 8, "a"), ("qup", 8, "a"), ("kvup", 12, "a"), ("att2+zm", 16, "x"), ("glm", 8, "a"),
         ("brm", 8, "d"), ("zs", 8, "a"), ("gls", 8, "a"), ("glu", 16, "y"), ("brs", 8, "d"), ("out", 8, "a")]
TILE, OWNER = {}, []
for _name, _n, _who in TILES:
    TILE[_name] = len(OWNER)
    OWNER += {"x": ["d", "a"], "y": ["a", "d"]}.get(_who, [_who] * 2) * (_n // 2) + [_who] * (_n % 2)
TILE_UNITS = {"pool": ("pool", 0, 4), "k": ("kv", 0, 1), "qup": ("qup", 0, 2), "kvup": ("kvup", 0, 3),
              "att1": None}
FINISHED, _parts = {}, 0
for _name, _n, _who in TILES:
    if _name.startswith("ffn"):
        continue
    _from = TILE_UNITS.get(_name, (_name, 0, 1))
    for _k in range(_n):
        if _name == "att2+zm":
            if _k % 2 == 0:
                _parts += 1
            FINISHED[TILE[_name] + _k] = ("used", UNIT["zm"] + _k // 2 + 1) if _k % 2 else ("part", _parts)
            continue
        if _from and _k % _from[2] == _from[2] - 1:
            FINISHED[TILE[_name] + _k] = ("used", UNIT[_from[0]] + _from[1] + _k // _from[2] + 1)
        else:
            _parts += 1
            FINISHED[TILE[_name] + _k] = ("part", _parts)


def freed_count(o):
    return OWNER[o], OWNER[:o + 1].count(OWNER[o])


VEC, NV = {}, 0
for _name, _n in [("c", 8), ("c2", 8), ("logdt", 32), ("lr", 32), ("li", 32), ("bias", N_MOD), ("norm_g", 48),
                  ("pool_scale", 8), ("kv_norm", 8), ("k_norm", 1), ("q_norm", 1), ("g_pre", 8), ("ssm_d", 8),
                  ("b_glu", 16), ("g_q", 2), ("g_kv", 2), ("g_post", 8)]:
    VEC[_name] = NV
    NV += _n
CON, NC_ = {}, 0
for _name, _n in [("eps", 1), ("ident", 128), ("ones", 128), ("rot1", 128), ("rot2", 96), ("cos1", T), ("sin1", T),
                  ("mask", 2 * T), ("cnt", 64), ("invf", 1)]:
    CON[_name] = NC_
    NC_ += _n
POOL_W = (2, 4, 8, 16)
PAD = 16
CH = 32
NCH = T // CH


GATES = [(_name, _n) for _name in ("glm", "brm", "zs", "gls") for _n in range(KT)]


def zm_tile(n):
    return TILE["att2+zm"] + 2 * n + 1


def att2_tile(g):
    return TILE["att2+zm"] + 2 * g


def g_unit(base, j):
    return base + (2 * j if j < 2 else 3 * j - 1)


def o_unit(base, j):
    return base + (65 if j == FFN_TILES - 1 else 3 * j + 4)


def build_program(nc, stream, gstream, vecs_d, cons_d, mask2_d, xin, pos_d, ssm_b, ssm_c, out):
    with ExitStack() as ctx:
        def sb(name, shape, dt=F32):
            return ctx.enter_context(nc.sbuf_tensor(name, shape, dt))

        def sem(name):
            return ctx.enter_context(nc.semaphore(name))

        land = sb("land", [P, LAND, WIDTH])
        w_hi = sb("w_hi", [P, RING, WIDTH], F32R)
        w_lo = sb("w_lo", [P, RING, WIDTH], F32R)
        x = sb("x", [P, KT, T])
        x_hi = sb("x_hi", [P, KT, T], F32R)
        x_lo = sb("x_lo", [P, KT, T], F32R)
        a_hi = sb("a_hi", [P, KT, T], F32R)
        a_lo = sb("a_lo", [P, KT, T], F32R)
        h_hi = sb("h_hi", [P, 2, T], F32R)
        h_lo = sb("h_lo", [P, 2, T], F32R)
        vecs = sb("vecs", [P, NV])
        cons = sb("cons", [P, NC_])
        rh = sb("rh", [P, 2 * T])
        base_t = sb("base_t", [P, 2, 32, CH])
        chunk_t = sb("chunk_t", [P, 2, 32, NCH])
        ssm_s = sb("ssm_s", [P, 20, 32])
        coef = sb("coef", [P, 9, 32])
        csil = sb("csil", [P, KT])
        eps_root = sb("eps_root", [P, 1])[:]
        att_s = sb("att_s", [P, 2, 16])
        ssm_m1 = sb("ssm_m1", [P, 4, T])
        rope_tab = sb("rope_tab", [P, 4, T])
        arena = sb("arena", [P, 20480])

        def region_at(col, shape):
            v = arena[:, col:col + int(np.prod(shape))]
            names = "abcd"[:len(shape)]
            kw = {names[i]: shape[i] for i in range(1, len(shape))}
            return v.rearrange(f"p ({' '.join(names)}) -> p {' '.join(names)}", **kw) if kw else v

        def region(kb, shape):
            return region_at(kb * 256, shape)

        rx = region(79, [T])
        g_land = region(0, [2, 8, GW])
        g_acc = region(32, [2, GW])
        silu_b = region(36, [2, T])
        hid = region(38, [2, T])
        kT = region(40, [HEADS_1, T])
        v1 = region(48, [2, D])
        t_buf = region(56, [KT, T])
        qT = region(64, [HEADS_1, T])
        win_h = region(40, [KT, PAD + T])
        win_a = region_at(64 * 256, [KT, PAD + T])
        win_b = region_at(64 * 256 + KT * (PAD + T), [6, PAD + T])
        rope_sq, rope_kn, rope_t = region(56, [2, T]), region(58, [2, T]), region(60, [2, 2, T])
        ws1 = [(region(72, [4, T]), region(76, [2, 384])), (region(32, [4, T]), region(36, [2, 384]))]
        uT = region(0, [KT, T])
        q2 = region(8, [HEADS_2, T])
        k2 = region(24, [HEADS_2, T])
        v2 = region(40, [2, D])
        ym, zm = region(8, [KT, 2, T])[:, :, 0], region(8, [KT, 2, T])[:, :, 1]
        lat_raw, lat_sq, lat_n = region(64, [4, T]), region(68, [4, T]), region(72, [4, T])
        kr_buf = region(76, [3, T])
        rope2 = rope_tab[0:QK_2, 0:2]
        ang = rope_tab[:, 2:4]
        pos_i, theta, tmp_a, tmp_b = (ssm_m1[:, n] for n in range(4))
        ws2 = [(region(48, [4, T]), region(52, [2, 384])), (region(56, [4, T]), region(60, [2, 384]))]
        rot_t = [region(64, [2, 2, T]), region(68, [2, 2, T])]
        ssm_m = [(region(20, [2, T]), region(22, [2, T])), (ssm_m1[:, 0:2], ssm_m1[:, 2:4])]
        sig_t = region(26, [2, T])
        ssm_v = [region(16, [2, 2, T]), region(28, [2, 2, T])]
        gel = region(56, [KT, T])
        zs_t = region(32, [KT, T])
        b_sb = region(40, [2, KT, P])
        mrg = region(48, [KT, T])
        gs_t = region(8, [KT, T])
        cc = region(72, [2, 32, 32])
        c_raw = region(64, [2, 32, 32])
        o_raw = region(8, [KT, T])

        acc4 = ctx.enter_context(nc.psum_tensor("acc4", [P, 4, 512], F32))
        tiles = ctx.enter_context(nc.psum_tensor("tiles", [P, 2, 512], F32))
        nrm = ctx.enter_context(nc.psum_tensor("nrm", [P, 512], F32))
        mods = ctx.enter_context(nc.psum_tensor("mods", [P, 512], F32))
        yT = [acc4[:, n // 2, (n % 2) * T:(n % 2 + 1) * T] for n in range(KT)]

        landed = [sem(f"landed{i}") for i in range(LAND)]
        hi_done = sem("hi_done")
        lo_done = sem("lo_done")
        used = sem("used")
        g_landed = [sem(f"g_landed{i}") for i in range(2)]
        g_step = sem("g_step")
        g_done = sem("g_done")
        g_red = sem("g_red")
        vec_in, con_in, x_in, pos_in = sem("vec_in"), sem("con_in"), sem("x_in"), sem("pos_in")
        y_bank = sem("y_bank")
        pw_done, ph_done = sem("pw_done"), sem("ph_done")
        one_in, den_done = sem("one_in"), sem("den_done")
        b_in, c_in, mask_in, out_st = sem("b_in"), sem("c_in"), sem("mask_in"), sem("out_st")
        freed = {"d": sem("freed_d"), "a": sem("freed_a")}
        part_done = sem("part_done")
        x_upd = sem("x_upd")
        sq_done, nrm_done, rt_done = sem("sq_done"), sem("nrm_done"), sem("rt_done")
        t_done, xh_done, xl_done = sem("t_done"), sem("xh_done"), sem("xl_done")
        silu_done, hh_done, h_done = sem("silu_done"), sem("hh_done"), sem("h_done")
        dve_s, act_s, pool_s = sem("dve_s"), sem("act_s"), sem("pool_s")
        csilu_done, ang_done, sin_done = sem("csilu_done"), sem("ang_done"), sem("sin_done")
        hcos_done = sem("hcos_done")
        hread_done, v_done = sem("hread_done"), sem("v_done")
        hsq_done, hs_done, hrt_done = sem("hsq_done"), sem("hs_done"), sem("hrt_done")
        kn_done, hrot_done, rope_done = sem("kn_done"), sem("hrot_done"), sem("rope_done")
        s_done, sm_done, mx_done, ex_done = sem("s_done"), sem("sm_done"), sem("mx_done"), sem("ex_done")
        pn_done, pt_done, pe_done = sem("pn_done"), sem("pt_done"), sem("pe_done")
        af_done, ah_done, al_done = sem("af_done"), sem("ah_done"), sem("al_done")
        lsq_done, lsum_done, lrt_done = sem("lsq_done"), sem("lsum_done"), sem("lrt_done")
        krot_done, kr_done, kb_done = sem("krot_done"), sem("kr_done"), sem("kb_done")
        qrot_done, qrope_done = sem("qrot_done"), sem("qrope_done")
        base_done = sem("base_done")
        tab_done, cc_done = sem("tab_done"), sem("cc_done")
        bu_done, bu_free, zz_done, y_done = sem("bu_done"), sem("bu_free"), sem("zz_done"), sem("y_done")
        yp_done, gel_done, gv_done = sem("yp_done"), sem("gel_done"), sem("gv_done")
        zm_done = sem("zm_done")
        vs_done, zp_done = sem("vs_done"), sem("zp_done")
        fin_done = sem("fin_done")
        done_sem = {"used": used, "part": part_done}

        def wait_tile(eng, o):
            which, n = FINISHED[o]
            eng.wait_ge(done_sem[which], n)

        def wait_freed(eng, o):
            who, n = freed_count(o)
            eng.wait_ge(freed[who], n)

        def vec(name, a=0, n=1):
            return vecs[:, VEC[name] + a:VEC[name] + a + n]

        def con(name, n):
            return cons[:, CON[name]:CON[name] + n]

        ident, ones = con("ident", P), con("ones", P)
        cos1, sin1 = con("cos1", T), con("sin1", T)

        STAGE = [(M_LAYER[0], 8 + M_LAYER[0], ("norm_g", 0)), (24, 32, ("norm_g", 8)), (48, 56, ("norm_g", 16)),
                 (M_KV, M_KV + 8, ("kv_norm", 0)), (88, 96, ("norm_g", 24)), (112, 120, ("norm_g", 32)),
                 (136, 144, ("norm_g", 40)), (M_2, M_2 + 8, ("g_pre", 0))]
        N_STAGES = len(STAGE)

        def wait_bank(eng, o):
            if o >= 2:
                who, n = freed_count(o - 2)
                eng.wait_ge(freed[who], n)

        def load_unit(sp, u, slot, i=0):
            if u >= LAND:
                sp.wait_ge(lo_done, i * 12 + (u - LAND + 1))
            sp.dma_start(land[:, slot], stream[i * 12 + u]).then_inc(landed[slot], 16)

        def split_hi(act, u, i=0):
            act.wait_ge(landed[u % LAND], i * (16 * 12 // LAND) + 16 * (u // LAND + 1))
            if u >= RING:
                act.wait_ge(used, i * 12 + (u - RING + 1))
            nc.scalar.copy(w_hi[:, u % RING], land[:, u % LAND]).then_inc(hi_done, 1)

        def split_lo(dve, u, i=0):
            dve.wait_ge(hi_done, i * 12 + (u + 1))
            nc.vector.tensor_tensor(w_lo[:, u % RING], land[:, u % LAND], w_hi[:, u % RING].bitcast(F32),
                                    ALU.subtract).then_inc(lo_done, 1)

        def products(pe, outs, pairs, start=True, stop=True, **kw):
            last = None
            for n, (lh, ll, rh, rl) in enumerate(pairs):
                first, end = start and n == 0, stop and n == len(pairs) - 1
                nc.tensor.matmul(outs, lh, rh, start=first, stop=False, **kw)
                nc.tensor.matmul(outs, lh, rl, start=False, stop=False, **kw)
                last = nc.tensor.matmul(outs, ll, rh, start=False, stop=end, **kw)
            return last

        def w_tile(u, a, n):
            return w_hi[:, u % RING, a:a + n], w_lo[:, u % RING, a:a + n]

        block = ctx.enter_context(nc.Block())

        @block.sync
        def _(sp):
            def g_load(b, i=0):
                if b >= 2:
                    sp.wait_ge(g_done, i * 2 + (b - 1))
                sp.dma_start(g_land[:, b % 2], gstream[i * 2 + b]).then_inc(g_landed[b % 2], 16)

            def units(name, n):
                for u in range(UNIT[name], UNIT[name] + n):
                    load_unit(sp, u, u % LAND)

            n_first = CON["ones"] + P
            sp.dma_start(vecs[:], vecs_d).then_inc(vec_in, 16)
            g_load(0)
            sp.dma_start(cons[:, 0:n_first], cons_d[:, 0:n_first]).then_inc(one_in, 16)
            g_load(1)
            sp.dma_start(x[:], xin).then_inc(x_in, 16)
            g_load(2)
            g_load(3)
            sp.dma_start(cons[:, n_first:], cons_d[:, n_first:]).then_inc(con_in, 16)
            for k in range(LAND):
                load_unit(sp, k, k)
            sp.dma_start(pos_i[64:96].bitcast(I32), pos_d).then_inc(pos_in, 16)
            for f in range(4):
                base, b = FFN_BASE[f], G_FFN[f]
                if G_FIRST[f]:
                    g_load(b)
                    b += 1
                for u in range(base, base + 5):
                    if not (f == 0 and u < LAND):
                        load_unit(sp, u, u % LAND)
                u = base + 5
                for reps, vector in SEGMENTS[f]:
                    with sp.Fori(0, reps) as i:
                        for m in range(4):
                            if vector and m % 2 == 0:
                                g_load(b + m // 2, i)
                            for s in range(3):
                                load_unit(sp, u + 3 * m + s, (u + 3 * m + s) % LAND, i)
                    u += 12 * reps
                    b += 2 * reps if vector else 0
                load_unit(sp, u, u % LAND)
                if f == 0:
                    g_load(G_POOL)
                    units("pool", 2)
                elif f == 1:
                    units("kv", 16)
                elif f == 2:
                    units("q", 8)
                    units("o", 8)
            wait_freed(sp, TILE["att1"] + 3)
            sp.dma_start(con("mask", 2 * T), mask2_d).then_inc(mask_in, 16)
            for name, n in PHASES[8:13]:
                units(name, n)
            sp.wait_ge(al_done, 4)
            sp.wait_ge(kb_done, 1)
            sp.dma_start(c_raw, ssm_c).then_inc(c_in, 16)
            units("zm", 8)
            units("glm", 6)
            wait_tile(sp, att2_tile(7))
            sp.dma_start(b_sb, ssm_b).then_inc(b_in, 16)
            for u in range(UNIT["glm"] + 6, N_UNITS):
                load_unit(sp, u, u % LAND)
            for k in range(KT):
                sp.wait_ge(fin_done, k + 1)
                sp.dma_start(out[:, k], x[:, k]).then_inc(out_st, 16)
            sp.wait_ge(out_st, 16 * KT)

        @block.tensor
        def _(pe):
            def reduce_block(b, i=0):
                pe.wait_ge(g_done, i * 2 + (b + 1))
                for q in range(4):
                    m = nc.tensor.matmul(mods[:, bass.ds(i * 8 + (4 * b + q), 1)],
                                         g_acc[:, b % 2, q * P:(q + 1) * P], ones[:, 0:1], start=True, stop=True)
                m.then_inc(g_red, 1)

            def sum_squares(n):
                if n:
                    pe.wait_ge(rt_done, n)
                for k in range(KT):
                    pe.wait_ge(sq_done, KT * n + k + 1)
                    m = nc.tensor.matmul(nrm[:, 0:T], ones, t_buf[:, k], start=(k == 0), stop=(k == KT - 1))
                m.then_inc(nrm_done, 1)

            def column_unit(u, o, hi, lo, split_sem=None, before=0, n_out=P):
                wait_bank(pe, o)
                pe.wait_ge(lo_done, u + 1)
                for k in range(KT):
                    if split_sem is not None:
                        pe.wait_ge(split_sem, before + k + 1)
                    pair = (*w_tile(u, k * n_out, n_out), hi[:, k], lo[:, k])
                    m = products(pe, tiles[0:n_out, o % 2, 0:T], [pair], start=(k == 0), stop=(k == KT - 1))
                m.then_inc(used, 1)

            def gate_unit(base, j, u, i, first=None):
                pe.wait_ge(lo_done, i * 12 + (u + 1))
                for k in range(KT):
                    if first is not None:
                        pe.wait_ge(xl_done, KT * first + k + 1)
                    m = products(pe, tiles[:, j % 2, 0:T], [(*w_tile(u, k * P, P), x_hi[:, k], x_lo[:, k])],
                                 start=(k == 0), stop=(k == KT - 1))
                m.then_inc(used, 1)

            def up_unit(j, u, i):
                pe.wait_ge(lo_done, i * 12 + (u + 1))
                m = products(pe, tiles[:, j % 2, T:2 * T],
                             [(*w_tile(u, k * P, P), x_hi[:, k], x_lo[:, k]) for k in range(KT)])
                m.then_inc(used, 1)

            def out_unit(f, j, u, i, per):
                pe.wait_ge(lo_done, i * 12 + (u + 1))
                pe.wait_ge(h_done, i * per + (FFN_TILES * f + j + 1))
                for n in range(KT):
                    m = products(pe, yT[n], [(*w_tile(u, n * P, P), h_hi[:, j % 2], h_lo[:, j % 2])],
                                 start=(j == 0 and per == 0 and n % 2 == 0),
                                 stop=(j == FFN_TILES - 1 and per == 0), skip_group_check=True)
                    if j == FFN_TILES - 1 and n % 2 and n < KT - 1:
                        m.then_inc(y_bank, 1)
                m.then_inc(used, 1)

            def ffn(f, stage):
                base, o0, b = FFN_BASE[f], TILE[f"ffn{f}"], G_FFN[f]
                nd = OWNER[:o0].count("d")
                for j in range(2):
                    wait_bank(pe, o0 + j)
                    gate_unit(base, j, g_unit(base, j), 0, stage if j == 0 else None)
                    up_unit(j, g_unit(base, j) + 1, 0)
                if f == 2:
                    pe.wait_ge(v_done, 2)
                out_unit(f, 0, o_unit(base, 0), 0, 0)
                if G_FIRST[f]:
                    reduce_block(b)
                    b += 1
                j0 = 2
                for reps, vector in SEGMENTS[f]:
                    with pe.Fori(0, reps) as i:
                        for m in range(4):
                            j = j0 + m
                            u = g_unit(base, j)
                            pe.wait_ge(freed["d"], i * 4 + (nd + j - 1))
                            gate_unit(base, j, u, i)
                            up_unit(j, u + 1, i)
                            out_unit(f, j - 1, u + 2, i, 4)
                            if vector and m % 2 == 1:
                                reduce_block(b + m // 2, i)
                    j0 += 4 * reps
                    b += 2 * reps if vector else 0
                out_unit(f, FFN_TILES - 1, o_unit(base, FFN_TILES - 1), 0, 0)

            def head_sum(n):
                if n % 4 == 1:
                    pe.wait_ge(hrt_done, n)
                elif n:
                    pe.wait_ge(hread_done, n - 1 if n % 4 else n)
                pe.wait_ge(hsq_done, n + 1)
                nc.tensor.matmul(nrm[:], ones, rope_sq, start=True, stop=True).then_inc(hs_done, 1)

            def head_rot(n):
                pe.wait_ge(hrt_done, min(n + 2, 4 * (n // 4) + 4))
                if n % 4 == 3:
                    pe.wait_ge(hread_done, n)
                pe.wait_ge(kn_done, n + 1)
                nc.tensor.matmul(nrm[:], con("rot1", P), rope_kn, start=True, stop=True).then_inc(hrot_done, 1)

            def head_steps(n0, h):
                if h in (5, 7, 9, 11):
                    head_rot(n0 + (h - 5) // 2)
                if h in (2, 4, 6, 8):
                    head_sum(n0 + h // 2 - 1)

            rot2 = cons[0:QK_2, CON["rot2"]:CON["rot2"] + QK_2]

            def attention(n0, groups, tile, qq, kk, vv, parts, vdim, ws, ready, beside=None):
                def scores(g):
                    ready(g)
                    if n0 + g:
                        pe.wait_ge(sm_done, n0 + g)
                    for h in range(2):
                        for qt in range(2):
                            m = nc.tensor.matmul(acc4[:, h, qt * T:(qt + 1) * T],
                                                 qq[0:parts, 2 * g + h, qt * P:(qt + 1) * P],
                                                 kk[0:parts, 2 * g + h, :], start=True, stop=True)
                    m.then_inc(s_done, 1)

                scores(0)
                scores(1)
                for g in range(groups):
                    n = n0 + g
                    sm, pt = ws[g % 2]
                    pe.wait_ge(pn_done, 4 * (n + 1))
                    if n:
                        pe.wait_ge(pe_done, n)
                    for h in range(2):
                        for qt, kt in ((0, 0), (1, 0), (1, 1)):
                            col = T + 0 if kt else qt * P
                            m = nc.tensor.transpose(acc4[:, 2 + h, col:col + P], sm[:, 2 * h + qt, kt * P:(kt + 1) * P],
                                                    ident)
                    m.then_inc(pt_done, 1)
                    if g + 2 < groups:
                        scores(g + 2)
                    wait_bank(pe, tile(g))
                    pe.wait_ge(pe_done, n + 1)
                    for h in range(2):
                        head = 2 * g + h
                        if vdim == P:
                            dst = tiles[:, tile(g) % 2, h * T:(h + 1) * T]
                        else:
                            dst = tiles[h * vdim:(h + 1) * vdim, tile(g) % 2, 0:T]
                        nc.tensor.matmul(dst, vv[:, 0, head * vdim:(head + 1) * vdim], pt[:, h, 0:T],
                                         start=True, stop=False)
                        m = nc.tensor.matmul(dst[:, P:T], vv[:, 1, head * vdim:(head + 1) * vdim], pt[:, h, T:T + P],
                                             start=False, stop=True)
                    m.then_inc(part_done, 1)
                    if beside:
                        beside(g)

            pe.wait_ge(one_in, 16)
            reduce_block(0)
            reduce_block(1)
            sum_squares(0)
            for b in range(2, G_PRE):
                reduce_block(b)
            ffn(0, 0)
            sum_squares(1)
            for q in range(2):
                u = UNIT["pool"] + q
                pe.wait_ge(lo_done, u + 1)
                for g in range(2):
                    for n in range(2):
                        o = TILE["pool"] + 4 * q + 2 * g + n
                        k0 = 4 * q + 2 * g
                        wait_bank(pe, o)
                        pe.wait_ge(xl_done, KT * 1 + k0 + 2)
                        m = products(pe, tiles[:, o % 2, 0:T],
                                     [(*w_tile(u, (2 * g + k) * 256 + n * P, P), x_hi[:, k0 + k], x_lo[:, k0 + k])
                                      for k in range(2)])
                        m.then_inc(used if (g, n) == (1, 1) else part_done, 1)
            sum_squares(2)
            reduce_block(G_POOL)
            ffn(1, 2)
            sum_squares(3)
            for h in range(HEADS_1):
                column_unit(UNIT["kv"] + h, TILE["k"] + h, x_hi, x_lo, xl_done if h == 0 else None,
                            KT * 3)
                head_steps(0, h)
            for k in range(KT):
                u = UNIT["kv"] + 8 + k
                pe.wait_ge(lo_done, u + 1)
                for tt in range(2):
                    rows = (x_hi[:, k, tt * P:(tt + 1) * P], x_lo[:, k, tt * P:(tt + 1) * P])
                    for c in range(2):
                        m = products(pe, acc4[:, 2 * tt + c], [(*rows, *w_tile(u, c * 512, 512))], start=(k == 0),
                                     stop=(k == KT - 1))
                m.then_inc(used, 1)
                head_steps(0, 8 + k)
            ffn(2, 4)
            sum_squares(4)
            for h in range(HEADS_1):
                column_unit(UNIT["q"] + h, TILE["q"] + h, x_hi, x_lo, xl_done if h == 0 else None, KT * 5)
                head_steps(4, h)
            head_steps(4, 8)
            head_steps(4, 9)
            head_steps(4, 11)
            attention(0, 4, lambda g: TILE["att1"] + g, qT, kT, v1, P, P, ws1,
                      lambda g: pe.wait_ge(rope_done, 4 + g + 1))
            for n in range(KT):
                if n == 0:
                    wait_freed(pe, TILE["att1"] + 3)
                column_unit(UNIT["o"] + n, TILE["o"] + n, a_hi, a_lo)
            sum_squares(5)
            ffn(3, 6)
            sum_squares(6)
            for n in range(4):
                column_unit(UNIT["lat"] + n, TILE["lat"] + n, x_hi, x_lo, xl_done if n == 0 else None,
                            KT * 7)
            column_unit(UNIT["kr"], TILE["kr"], x_hi, x_lo, n_out=QK_2)
            for n in range(2):
                column_unit(UNIT["u"] + n, TILE["u"] + n, x_hi, x_lo)
            for q in range(2):
                for k in range(2):
                    pe.wait_ge(lsq_done, 2 * q + k + 1)
                    m = nc.tensor.matmul(nrm[:, q * T:(q + 1) * T], ones, lat_sq[:, 2 * q + k], start=(k == 0),
                                         stop=(k == 1))
            m.then_inc(lsum_done, 1)
            wait_freed(pe, TILE["kr"])
            nc.tensor.matmul(acc4[0:QK_2, 2, 0:T], rot2, kr_buf[0:QK_2, 0], start=True,
                             stop=True).then_inc(krot_done, 1)
            for n in range(2, KT):
                column_unit(UNIT["u"] + n, TILE["u"] + n, x_hi, x_lo)
            for n in range(4):
                u = UNIT["qup"] + n
                pe.wait_ge(lo_done, u + 1)
                if n == 0:
                    pe.wait_ge(al_done, 4)
                for pair in range(2):
                    o = TILE["qup"] + 2 * n + pair
                    wait_bank(pe, o)
                    for h in range(2):
                        m = products(pe, tiles[0:QK_2, o % 2, h * T:(h + 1) * T],
                                     [(*w_tile(u, k * 384 + (2 * pair + h) * QK_2, QK_2), a_hi[:, k], a_lo[:, k])
                                      for k in range(2)])
                    m.then_inc(used if pair else part_done, 1)
            for n in range(4):
                u = UNIT["kvup"] + n
                pe.wait_ge(lo_done, u + 1)
                for pair in range(2):
                    o = TILE["kvup"] + 3 * n + pair
                    wait_bank(pe, o)
                    for h in range(2):
                        m = products(pe, tiles[:, o % 2, h * T:(h + 1) * T],
                                     [(*w_tile(u, k * 512 + (2 * pair + h) * P, P), a_hi[:, 2 + k], a_lo[:, 2 + k])
                                      for k in range(2)])
                    m.then_inc(part_done, 1)
                o = TILE["kvup"] + 3 * n + 2
                wait_bank(pe, o)
                for tt in range(2):
                    m = products(pe, tiles[:, o % 2, tt * T:(tt + 1) * T],
                                 [(a_hi[:, 2 + k, tt * P:(tt + 1) * P], a_lo[:, 2 + k, tt * P:(tt + 1) * P],
                                   *(w[:, u % RING, k * 512:(k + 1) * 512].rearrange("p (h c) -> p h c", c=P)[:, :, V_2:P]
                                     for w in (w_hi, w_lo))) for k in range(2)])
                m.then_inc(used, 1)
                for g in (2 * n, 2 * n + 1):
                    wait_freed(pe, TILE["qup"] + g)
                    if g >= 2:
                        pe.wait_ge(qrope_done, g - 1)
                    nc.tensor.matmul(acc4[0:QK_2, 2 + g % 2], rot2, q2[0:QK_2, 2 * g:2 * g + 2], start=True,
                                     stop=True).then_inc(qrot_done, 1)
            attention(4, 8, att2_tile, q2, k2, v2, QK_2, V_2, ws2, lambda g: (
                pe.wait_ge(qrope_done, g + 1), pe.wait_ge(kb_done, 1), wait_freed(pe, TILE["kvup"] + 11)),
                lambda g: column_unit(UNIT["zm"] + g, zm_tile(g), x_hi, x_lo))

            def ssm_b_step(s):
                if s == 0:
                    pe.wait_ge(b_in, 16)
                if s >= 2:
                    pe.wait_ge(bu_free, s - 1)
                f, jj = s // 2, 2 * (s % 2)
                for j in range(2):
                    r = 32 * (jj + j)
                    for c in range(2):
                        m = nc.tensor.matmul(acc4[:, jj + j, c * T:(c + 1) * T], b_sb[r:r + 32, c, f],
                                             uT[r:r + 32, f], start=True, stop=True)
                m.then_inc(bu_done, 1)

            def ssm_c_step(s):
                f, jj = s // 2, 2 * (s % 2)
                if s == 0:
                    pe.wait_ge(cc_done, 1)
                if s % 2 == 0 and f >= 1:
                    pe.wait_ge(yp_done, f)
                pe.wait_ge(zz_done, s + 1)
                pe.wait_ge(zp_done, s + 1)
                v, (m0, m1) = ssm_v[s % 2], ssm_m[s % 2]
                for j in range(2):
                    r = 32 * (jj + j)
                    terms = [(0, m0[:, j]), (1, v[:, 1, j]), (0, v[:, 0, j]), (1, m1[:, j])]
                    for n, (c, z) in enumerate(terms):
                        m = nc.tensor.matmul(nrm[r:r + 32, (f % 2) * T:(f % 2 + 1) * T], cc[:, c, 4 * f + jj + j],
                                             z, start=(n == 0), stop=(n == 3))
                m.then_inc(y_done, 1)

            for s in range(16):
                for nm, n in GATES[2 * s:2 * s + 2]:
                    if (nm, n) == GATES[1]:
                        ssm_b_step(0)
                    hi, lo = (a_hi, a_lo) if nm == "brm" else (x_hi, x_lo)
                    column_unit(UNIT[nm] + n, TILE[nm] + n, hi, lo, al_done if (nm, n) == ("brm", 0) else None, 4)
                if s + 1 < 16:
                    ssm_b_step(s + 1)
                if s:
                    ssm_c_step(s - 1)
            ssm_c_step(15)
            for n in range(16):
                column_unit(UNIT["glu"] + n, TILE["glu"] + n, a_hi, a_lo, al_done if n == 0 else None, 12)
            for n in range(KT):
                column_unit(UNIT["brs"] + n, TILE["brs"] + n, x_hi, x_lo, xl_done if n == 0 else None, KT * N_STAGES)
            for n in range(KT):
                column_unit(UNIT["out"] + n, TILE["out"] + n, a_hi, a_lo, al_done if n == 0 else None, 20)
            sum_squares(7)

        @block.scalar
        def _(act):
            chain = [0]

            def link(ins):
                chain[0] += 1
                ins.then_inc(act_s, 1)
                act.wait_ge(act_s, chain[0])

            def split(name, a, b):
                for n in range(a, b):
                    split_hi(act, UNIT[name] + n)

            def squares(n, ready, last_unit=None):
                nc.scalar.activation(eps_root, con("eps", 1), ACT.Sqrt)
                for k in range(KT):
                    ready(k)
                    nc.scalar.square(t_buf[:, k], x[:, k]).then_inc(sq_done, 1)
                if last_unit is not None:
                    split_hi(act, last_unit)
                act.wait_ge(nrm_done, n + 1)
                nc.scalar.activation(rx, nrm[:, 0:T], ACT.Sqrt, bias=con("eps", 1), scale=1.0 / D).then_inc(rt_done, 1)

            def norm_hi(stage):
                n = stage
                for k in range(KT):
                    act.wait_ge(t_done, KT * n + k + 1)
                    nc.scalar.activation(x_hi[:, k], t_buf[:, k], ACT.Identity,
                                         bias=coef[:, stage, 8 + k:9 + k]).then_inc(xh_done, 1)

            def silu_step(f, j, u, i, per):
                act.wait_ge(used, i * 12 + (u + 1))
                if j >= 2 or per:
                    nd = OWNER[:TILE[f"ffn{f}"]].count("d")
                    if nd + j - 1 > 0:
                        act.wait_ge(freed["d"], i * per + (nd + j - 1))
                nc.scalar.activation(silu_b[:, j % 2], tiles[:, j % 2, 0:T], ACT.Silu).then_inc(silu_done, 1)

            def ffn(f, pre):
                base = FFN_BASE[f]
                for s in range(pre, 4):
                    split_hi(act, base + s)
                split_hi(act, base + 4)
                silu_step(f, 0, base + 1, 0, 0)
                j0 = 2
                for reps, _ in SEGMENTS[f]:
                    with act.Fori(0, reps) as i:
                        for m in range(4):
                            u = g_unit(base, j0 + m)
                            for s in range(3):
                                split_hi(act, u + s, i)
                            silu_step(f, j0 + m - 1, g_unit(base, j0 + m - 1) + 1, i, 4)
                    j0 += 4 * reps
                split_hi(act, o_unit(base, 21))
                silu_step(f, 21, g_unit(base, 21) + 1, 0, 0)

            def head_square(n, src):
                if n:
                    act.wait_ge(hs_done, n)
                nc.scalar.square(rope_sq, src).then_inc(hsq_done, 1)

            def head_root(n):
                act.wait_ge(hs_done, n + 1)
                if n:
                    act.wait_ge(kn_done, n)
                nc.scalar.activation(rh[:], nrm[:], ACT.Sqrt, bias=con("eps", 1),
                                     scale=1.0 / HEAD_DIM).then_inc(hrt_done, 1)

            def head_steps(n0, h, o0, heads):
                if h < HEADS_1 and h % 2:
                    wait_freed(act, o0 + h)
                    head_square(n0 + h // 2, heads[:, h - 1:h + 1])
                if h in (2, 4, 6, 8):
                    head_root(n0 + h // 2 - 1)

            def evacuate(o, src, dst, func=ACT.Copy, **kw):
                wait_tile(act, o)
                nc.scalar.activation(dst, src, func, **kw).then_inc(freed["a"], 1)

            def tile_of(name, n):
                return tiles[:, (TILE[name] + n) % 2, 0:T]

            def exps(n, g, ws, scale):
                sm, pt = ws[g % 2]
                act.wait_ge(mx_done, n + 1)
                for r in range(4):
                    nc.scalar.activation(sm[:, r], sm[:, r], ACT.Exp, bias=att_s[:, g % 2, 4 + r:5 + r], scale=scale,
                                         accum_out=att_s[:, g % 2, 8 + r:9 + r]).then_inc(ex_done, 1)

            def probs_t(n, g, ws, tile):
                sm, pt = ws[g % 2]
                act.wait_ge(pt_done, n + 1)
                if g >= 2:
                    wait_tile(act, tile(g - 2))
                nc.scalar.copy(pt, acc4[:, 2:4, 0:384]).then_inc(pe_done, 1)

            act.wait_ge(vec_in, 16)
            nc.scalar.activation(csil[:], vec("c", 0, 8), ACT.Silu).then_inc(csilu_done, 1)
            link(nc.scalar.activation(ssm_s[:, 0], vec("logdt", 0, 32), ACT.Exp))
            act.wait_ge(ang_done, 1)
            link(nc.scalar.activation(ssm_s[:, 1], ssm_s[:, 2], ACT.Exp))
            act.wait_ge(ang_done, 2)
            nc.scalar.activation(ssm_s[:, 5:7], ssm_s[:, 3:5], ACT.Sin).then_inc(sin_done, 1)
            act.wait_ge(one_in, 16)
            squares(0, lambda k: act.wait_ge(x_in, 16))
            for k in range(3):
                split_hi(act, k)
            norm_hi(0)
            ffn(0, 3)
            split("pool", 0, 2)
            split_hi(act, UNIT["ffn1"])
            squares(1, lambda k: act.wait_ge(x_upd, k + 1))
            for i, k in enumerate((6, 7, 0, 1, 2, 3, 4, 5)):
                act.wait_ge(pw_done, i + 1)
                nc.scalar.activation(win_h[:, k, PAD:], win_h[:, k, PAD:], ACT.Identity,
                                     bias=coef[:, 1, 8 + k:9 + k]).then_inc(ph_done, 1)
            for k in range(0, KT, 2):
                act.wait_ge(t_done, KT + k + 2)
                nc.scalar.copy(x_hi[:, k:k + 2], t_buf[:, k:k + 2]).then_inc(xh_done, 2)
            for s in range(1, 3):
                split_hi(act, UNIT["ffn1"] + s)
            squares(2, lambda k: wait_freed(act, TILE["pool"] + k))
            norm_hi(2)
            ffn(1, 3)
            split("kv", 0, 3)
            squares(3, lambda k: act.wait_ge(x_upd, KT + k + 1), UNIT["kv"] + 3)
            norm_hi(3)
            for h in range(16):
                if h < HEADS_1:
                    evacuate(TILE["k"] + h, tile_of("k", h), kT[:, h])
                head_steps(0, h, TILE["k"], kT)
                split_hi(act, UNIT["kv"] + h + 4)
            act.wait_ge(used, UNIT["ffn2"])
            nc.scalar.copy(v1[:, 0], acc4[:, 0:2].rearrange("p a b -> p (a b)")).then_inc(v_done, 1)
            norm_hi(4)
            ffn(2, 4)
            split("q", 0, 3)
            squares(4, lambda k: act.wait_ge(x_upd, 2 * KT + k + 1), UNIT["q"] + 3)
            norm_hi(5)
            for h in range(HEADS_1):
                evacuate(TILE["q"] + h, tile_of("q", h), qT[:, h])
                head_steps(4, h, TILE["q"], qT)
                split_hi(act, UNIT["q"] + h + 4)
            head_root(7)

            def att_hi(g):
                wait_tile(act, TILE["att1"] + g)
                nc.scalar.copy(a_hi[:, 2 * g:2 * g + 2],
                               tiles[:, (TILE["att1"] + g) % 2].rearrange("p (h t) -> p h t", h=2)).then_inc(ah_done, 2)

            exps(0, 0, ws1, HEAD_DIM ** -0.5)
            exps(1, 1, ws1, HEAD_DIM ** -0.5)
            for g in range(4):
                probs_t(g, g, ws1, lambda g: TILE["att1"] + g)
                att_hi(g)
                if g + 2 < 4:
                    exps(g + 2, g + 2, ws1, HEAD_DIM ** -0.5)
            squares(5, lambda k: (split_hi(act, UNIT["o"] + 4 + k), wait_freed(act, TILE["o"] + k)))
            norm_hi(6)
            ffn(3, 4)
            split("lat", 0, 3)
            squares(6, lambda k: act.wait_ge(x_upd, 3 * KT + k + 1), UNIT["lat"] + 3)
            norm_hi(7)
            next_unit = [UNIT["lat"] + 4]

            def ahead(n=1):
                for _ in range(n):
                    if next_unit[0] < N_UNITS:
                        split_hi(act, next_unit[0])
                        next_unit[0] += 1

            for n in range(4):
                evacuate(TILE["lat"] + n, tile_of("lat", n), lat_raw[:, n])
                ahead()
                wait_freed(act, TILE["lat"] + n)
                nc.scalar.square(lat_sq[:, n], lat_raw[:, n]).then_inc(lsq_done, 1)
            evacuate(TILE["kr"], tile_of("kr", 0)[0:QK_2], kr_buf[0:QK_2, 0])
            ahead()
            act.wait_ge(ang_done, 3)
            nc.scalar.activation(rope2[64:96], ang[64:96, 0:2], ACT.Sin).then_inc(sin_done, 1)
            for n in range(KT):
                evacuate(TILE["u"] + n, tile_of("u", n), uT[:, n])
                ahead()
                if n == 1:
                    act.wait_ge(lsum_done, 1)
                    nc.scalar.activation(rh[:], nrm[:], ACT.Sqrt, bias=con("eps", 1),
                                         scale=1.0 / 256).then_inc(lrt_done, 1)
                if n == 3:
                    for k in range(4):
                        act.wait_ge(af_done, k + 1)
                        nc.scalar.copy(a_hi[:, k], lat_n[:, k]).then_inc(ah_done, 1)
            for g in range(8):
                o = TILE["qup"] + g
                evacuate(o, tiles[0:QK_2, o % 2].rearrange("p (h t) -> p h t", h=2), q2[0:QK_2, 2 * g:2 * g + 2])
                if g % 2:
                    ahead()
            for n in range(4):
                for pair in range(2):
                    o = TILE["kvup"] + 3 * n + pair
                    h = 4 * n + 2 * pair
                    evacuate(o, tiles[0:64, o % 2].rearrange("p (h t) -> p h t", h=2), k2[0:64, h:h + 2])
                o = TILE["kvup"] + 3 * n + 2
                evacuate(o, tiles[:, o % 2].rearrange("p (t c) -> p t c", t=2), v2[:, :, 256 * n:256 * (n + 1)])
                ahead()
            exps(4, 0, ws2, QK_2 ** -0.5)
            exps(5, 1, ws2, QK_2 ** -0.5)
            for g in range(8):
                probs_t(4 + g, g, ws2, att2_tile)
                if g:
                    evacuate(zm_tile(g - 1), tiles[:, zm_tile(g - 1) % 2, 0:T], zm[:, g - 1])
                    ahead()
                if g + 2 < 8:
                    exps(6 + g, g + 2, ws2, QK_2 ** -0.5)
            evacuate(zm_tile(7), tiles[:, zm_tile(7) % 2, 0:T], zm[:, 7])
            ahead()
            wait_freed(act, zm_tile(7))
            nc.scalar.activation(zm, zm, ACT.Silu).then_inc(zm_done, 1)
            for n in range(KT):
                act.wait_ge(af_done, 4 + n + 1)
                nc.scalar.copy(a_hi[:, n], t_buf[:, n]).then_inc(ah_done, 1)

            def gelu_tile(f):
                act.wait_ge(yp_done, f + 1)
                nc.scalar.activation(gel[:, f], gel[:, f], ACT.Gelu_apprx_tanh).then_inc(gel_done, 1)

            def gelu_hi(f):
                act.wait_ge(gel_done, f + 1)
                nc.scalar.copy(a_hi[:, f], gel[:, f]).then_inc(ah_done, 1)

            for s in range(16):
                for nm, n in GATES[2 * s:2 * s + 2]:
                    o = TILE[nm] + n
                    if nm == "glm":
                        evacuate(o, tile_of(nm, n), mrg[:, n], ACT.Sigmoid)
                    elif nm == "zs":
                        evacuate(o, tile_of(nm, n), zs_t[:, n], ACT.Silu)
                    elif nm == "gls":
                        evacuate(o, tile_of(nm, n), gs_t[:, n], ACT.Sigmoid)
                    ahead()
                for f in {10: (0, 1, 2, 3), 15: (4, 5, 6)}.get(s, ()):
                    gelu_tile(f)
                for f in {10: (0, 1, 2, 3), 15: (4, 5, 6)}.get(s, ()):
                    gelu_hi(f)
            gelu_tile(7)
            gelu_hi(7)
            for n in range(KT):
                if n >= 2:
                    act.wait_ge(gv_done, n - 1)
                evacuate(TILE["glu"] + 2 * n, tile_of("glu", 2 * n), sig_t[:, n % 2], ACT.Sigmoid,
                         bias=vec("b_glu", 8 + n))
                ahead(2)
                if n >= 1:
                    act.wait_ge(gv_done, n)
                    nc.scalar.copy(x_hi[:, n - 1], gel[:, n - 1]).then_inc(xh_done, 1)
            act.wait_ge(gv_done, KT)
            nc.scalar.copy(x_hi[:, 7], gel[:, 7]).then_inc(xh_done, 1)
            for n in range(KT):
                ahead()
                act.wait_ge(af_done, 12 + n + 1)
                nc.scalar.copy(a_hi[:, n], mrg[:, n]).then_inc(ah_done, 1)
            for n in range(KT):
                evacuate(TILE["out"] + n, tile_of("out", n), o_raw[:, n])
                ahead()
                wait_freed(act, TILE["out"] + n)
                nc.scalar.square(t_buf[:, n], o_raw[:, n]).then_inc(sq_done, 1)
            act.wait_ge(nrm_done, 8)
            nc.scalar.activation(rx, nrm[:, 0:T], ACT.Sqrt, bias=con("eps", 1), scale=1.0 / D).then_inc(rt_done, 1)

        @block.vector
        def _(dve):
            chain = [0]
            blocks = [G_PRE]
            V = nc.vector

            def link(ins):
                chain[0] += 1
                ins.then_inc(dve_s, 1)
                dve.wait_ge(dve_s, chain[0])

            def g_part(b, k, vector, i=0):
                cv = csil[:, k:k + 1] if vector == "silu" else vec("c2", k)
                acc, rows = g_acc[:, b % 2], g_land[:, b % 2, k]
                if k == 0:
                    dve.wait_ge(g_landed[b % 2], i * 16 + 16 * (b // 2 + 1))
                    if b >= 2:
                        dve.wait_ge(g_red, i * 2 + (b - 1))
                    V.tensor_scalar(acc, rows, cv, None, ALU.mult).then_inc(g_step, 1)
                else:
                    dve.wait_ge(g_step, i * 14 + (7 * b + k))
                    V.scalar_tensor_tensor(out=acc, in0=rows, scalar=cv, in1=acc, op0=ALU.mult,
                                           op1=ALU.add).then_inc(g_done if k == 7 else g_step, 1)

            def g_block(b):
                for k in range(8):
                    g_part(b, k, "silu")

            def hidden(f, j, i, per):
                base, nd = FFN_BASE[f], OWNER[:TILE[f"ffn{f}"]].count("d")
                J = FFN_TILES * f + j
                dve.wait_ge(silu_done, i * per + (J + 1))
                V.tensor_tensor(hid[:, j % 2], silu_b[:, j % 2], tiles[:, j % 2, T:2 * T],
                                ALU.mult).then_inc(freed["d"], 1)
                dve.wait_ge(freed["d"], i * per + (nd + j + 1))
                if j >= 2 or per:
                    dve.wait_ge(used, i * 12 + (base + 3 * (j - 2) + 4 + 1))
                V.tensor_copy(h_hi[:, j % 2], hid[:, j % 2]).then_inc(hh_done, 1)
                dve.wait_ge(hh_done, i * per + (J + 1))
                V.tensor_tensor(h_lo[:, j % 2], hid[:, j % 2], h_hi[:, j % 2].bitcast(F32),
                                ALU.subtract).then_inc(h_done, 1)

            def gate_coef(stage, col, weight):
                dve.wait_ge(g_red, blocks[0])
                link(V.tensor_tensor(coef[:, stage, 24:32], mods[:, col:col + 8], vec("bias", col, 8), ALU.add))
                if isinstance(weight, float):
                    link(V.tensor_scalar(coef[:, stage, 16:24], coef[:, stage, 24:32], 1.0, weight, ALU.add, ALU.mult))
                else:
                    link(V.scalar_tensor_tensor(out=coef[:, stage, 16:24], in0=coef[:, stage, 24:32], scalar=1.0,
                                                in1=weight, op0=ALU.add, op1=ALU.mult))

            def norm_coef(stage):
                sh, sc, (gname, g0) = STAGE[stage]
                dve.wait_ge(g_red, blocks[0])
                link(V.tensor_tensor(coef[:, stage, 24:32], mods[:, sc:sc + 8], vec("bias", sc, 8), ALU.add))
                link(V.scalar_tensor_tensor(out=coef[:, stage, 0:8], in0=coef[:, stage, 24:32], scalar=1.0,
                                            in1=vec(gname, g0, 8), op0=ALU.add, op1=ALU.mult))
                link(V.tensor_tensor(coef[:, stage, 8:16], mods[:, sh:sh + 8], vec("bias", sh, 8), ALU.add))

            def root(n):
                dve.wait_ge(rt_done, n + 1)
                link(V.reciprocal(rx, rx))

            def norm_t(stage):
                for k in range(KT):
                    V.scalar_tensor_tensor(out=t_buf[:, k], in0=x[:, k], scalar=coef[:, stage, k:k + 1], in1=rx,
                                           op0=ALU.mult, op1=ALU.mult).then_inc(t_done, 1)
                    if k >= 1:
                        norm_lo(stage, k - 1)
                norm_lo(stage, KT - 1)

            def norm_lo(stage, k):
                n = stage
                dve.wait_ge(xh_done, KT * n + k + 1)
                dve.wait_ge(t_done, KT * n + k + 1)
                V.scalar_tensor_tensor(out=x_lo[:, k], in0=t_buf[:, k], scalar=coef[:, stage, 8 + k:9 + k],
                                       in1=x_hi[:, k].bitcast(F32), op0=ALU.add, op1=ALU.subtract).then_inc(xl_done, 1)

            def update(k, src, stage, signal):
                V.scalar_tensor_tensor(out=x[:, k], in0=src, scalar=coef[:, stage, 16 + k:17 + k], in1=x[:, k],
                                       op0=ALU.mult, op1=ALU.add).then_inc(signal, 1)

            def ffn(f, stage, pre, gate_col, ahead_units):
                base, b = FFN_BASE[f], G_FFN[f]
                for s in range(pre, 5):
                    split_lo(dve, base + s)
                hidden(f, 0, 0, 0)
                if G_FIRST[f]:
                    g_block(b)
                    b += 1
                j0 = 2
                for reps, vector in SEGMENTS[f]:
                    with dve.Fori(0, reps) as i:
                        for m in range(4):
                            j, u = j0 + m, g_unit(base, j0 + m)
                            for s in range(3):
                                split_lo(dve, u + s, i)
                                if vector:
                                    g_part(b + m // 2, 4 * (m % 2) + s, vector, i)
                            hidden(f, j - 1, i, 4)
                            if vector:
                                g_part(b + m // 2, 4 * (m % 2) + 3, vector, i)
                    j0 += 4 * reps
                    b += 2 * reps if vector else 0
                blocks[0] = b
                split_lo(dve, o_unit(base, 21))
                hidden(f, 21, 0, 0)
                gate_coef(stage, gate_col, 0.5)
                for u in ahead_units[:3]:
                    split_lo(dve, u)
                for k in range(KT):
                    if k < KT - 2:
                        dve.wait_ge(y_bank, 3 * f + k // 2 + 1)
                    else:
                        dve.wait_ge(used, base + 66)
                    update(k, yT[k], stage, x_upd)
                for u in ahead_units[3:]:
                    split_lo(dve, u)

            dve.wait_ge(csilu_done, 1)
            dve.wait_ge(vec_in, 16)
            for b in range(G_PRE):
                g_block(b)
                if b == 1:
                    dve.wait_ge(den_done, 1)
                    V.reciprocal(ssm_s[:, 12], ssm_s[:, 12]).then_inc(den_done, 1)
            root(0)
            norm_coef(0)
            split_lo(dve, 0)
            norm_t(0)
            split_lo(dve, 1)
            split_lo(dve, 2)

            def rng(name, a, b):
                return range(UNIT[name] + a, UNIT[name] + b)

            def split(units):
                for u in units:
                    split_lo(dve, u)

            ffn(0, 0, 3, 16, [*rng("pool", 0, 2), UNIT["ffn1"]])

            def pooled_lo(g):
                dve.wait_ge(t_done, KT + 2 * g + 2)
                dve.wait_ge(xh_done, KT + 2 * g + 2)
                V.tensor_tensor(x_lo[:, 2 * g:2 * g + 2], t_buf[:, 2 * g:2 * g + 2],
                                x_hi[:, 2 * g:2 * g + 2].bitcast(F32), ALU.subtract).then_inc(xl_done, 2)

            norm_coef(1)
            gate_coef(1, 40, vec("pool_scale", 0, 8))
            dve.wait_ge(base_done, 1)
            for k in range(4):
                g_part(G_POOL, k, "silu")
            root(1)
            for k in (6, 7, 0, 1, 2, 3, 4, 5):
                V.scalar_tensor_tensor(out=win_h[:, k, PAD:], in0=x[:, k], scalar=coef[:, 1, k:k + 1], in1=rx,
                                       op0=ALU.mult, op1=ALU.mult).then_inc(pw_done, 1)
            window = [win_h[:, 2 * g:2 * g + 2] for g in range(3)]
            for level in range(3):
                for g in range(level, 3):
                    src, sh = window[g], 1 << level
                    dst = win_b[:, 2 * g - 2:2 * g] if level == 1 else win_a[:, 2 * g:2 * g + 2]
                    if level == 0:
                        dve.wait_ge(ph_done, 2 * g + 4)
                    m = V.tensor_tensor(dst[:, :, PAD:], src[:, :, PAD:], src[:, :, PAD - sh:PAD + T - sh], ALU.add)
                    window[g] = dst
                link(m)
            for g in range(3):
                h2, t2, src = win_h[:, 2 * g:2 * g + 2], t_buf[:, 2 * g:2 * g + 2], window[g]
                link(V.scalar_tensor_tensor(out=t2, in0=src[:, :, PAD:], scalar=1.0 / POOL_W[g], in1=h2[:, :, PAD:],
                                            op0=ALU.mult, op1=ALU.subtract))
                cnt = cons[:, CON["cnt"] + 16 * g:CON["cnt"] + 16 * (g + 1)].unsqueeze(1).to_broadcast([P, 2, 16])
                link(V.tensor_tensor(t2[:, :, 0:16], src[:, :, PAD:PAD + 16], cnt, ALU.mult))
                V.tensor_tensor(t2[:, :, 0:16], t2[:, :, 0:16], h2[:, :, PAD:PAD + 16],
                                ALU.subtract).then_inc(t_done, 2)
                if g:
                    pooled_lo(g - 1)
            pooled_lo(2)
            pooled_lo(3)
            for k in range(KT):
                wait_tile(dve, TILE["pool"] + k)
                update(k, tiles[:, k % 2, 0:T], 1, freed["d"])
                if k in (2, 5):
                    split_lo(dve, UNIT["ffn1"] + 1 + k // 5)
            for k in range(4, 8):
                g_part(G_POOL, k, "silu")
            blocks[0] += 1
            norm_coef(2)
            root(2)
            norm_t(2)
            ffn(1, 2, 3, 64, rng("kv", 0, 4))

            def head_norm(n, raw, weight):
                if n:
                    dve.wait_ge(hcos_done, n)
                dve.wait_ge(hrt_done, n + 1)
                link(V.reciprocal(rh[:], rh[:]))
                V.scalar_tensor_tensor(out=rope_kn, in0=raw, scalar=weight,
                                       in1=rh[:].rearrange("p (h t) -> p h t", h=2), op0=ALU.mult,
                                       op1=ALU.mult).then_inc(kn_done, 1)

            def head_rope(n, raw):
                dve.wait_ge(hrot_done, n + 1)
                m = V.tensor_tensor(rope_t[:, 1], nrm[:].rearrange("p (h t) -> p h t", h=2),
                                    sin1.unsqueeze(1).to_broadcast([P, 2, T]), ALU.mult)
                m.then_inc(hread_done, 1)
                dve.wait_ge(hread_done, n + 1)
                dve.wait_ge(hcos_done, n + 1)
                V.tensor_tensor(raw, rope_t[:, 0], rope_t[:, 1], ALU.add).then_inc(rope_done, 1)

            def head_steps(n0, h, heads, weight):
                if h in (5, 7, 9, 11):
                    n = (h - 5) // 2
                    head_rope(n0 + n, heads[:, 2 * n:2 * n + 2])
                if h in (3, 5, 7, 9):
                    n = (h - 3) // 2
                    head_norm(n0 + n, heads[:, 2 * n:2 * n + 2], weight)

            norm_coef(3)
            root(3)
            norm_t(3)
            for h in range(16):
                head_steps(0, h, kT, vec("k_norm"))
                split_lo(dve, UNIT["kv"] + h + 4)
            norm_coef(4)
            dve.wait_ge(used, UNIT["ffn2"])
            V.tensor_copy(v1[:, 1], acc4[:, 2:4].rearrange("p a b -> p (a b)")).then_inc(v_done, 1)
            norm_t(4)
            ffn(2, 4, 4, 104, rng("q", 0, 4))

            def scores_max(n, g, ws):
                sm, pt = ws[g % 2]
                scale = HEAD_DIM ** -0.5 if n < 4 else QK_2 ** -0.5
                dve.wait_ge(s_done, n + 1)
                if g >= 2:
                    dve.wait_ge(pt_done, n - 1)
                V.tensor_tensor(sm.rearrange("p (h q) t -> p h (q t)", h=2), acc4[:, 0:2],
                                con("mask", 2 * T).unsqueeze(1).to_broadcast([P, 2, 2 * T]),
                                ALU.add).then_inc(sm_done, 1)
                dve.wait_ge(sm_done, n + 1)
                link(V.tensor_reduce(att_s[:, g % 2, 0:4], sm, AX, ALU.max))
                V.tensor_scalar(att_s[:, g % 2, 4:8], att_s[:, g % 2, 0:4], -scale, None, ALU.mult).then_inc(mx_done, 1)

            def normalise(n, g, ws):
                sm, pt = ws[g % 2]
                dve.wait_ge(ex_done, 4 * (n + 1))
                link(V.reciprocal(att_s[:, g % 2, 12:16], att_s[:, g % 2, 8:12]))
                for r in range(4):
                    V.tensor_scalar(sm[:, r], sm[:, r], att_s[:, g % 2, 12 + r:13 + r], None,
                                    ALU.mult).then_inc(pn_done, 1)

            def att_lo(g):
                dve.wait_ge(ah_done, 2 * g + 2)
                heads = tiles[:, (TILE["att1"] + g) % 2].rearrange("p (h t) -> p h t", h=2)
                V.tensor_tensor(a_lo[:, 2 * g:2 * g + 2], heads,
                                a_hi[:, 2 * g:2 * g + 2].bitcast(F32), ALU.subtract).then_inc(freed["d"], 1)

            norm_coef(5)
            root(4)
            norm_t(5)
            for h in range(HEADS_1):
                head_steps(4, h, qT, vec("q_norm"))
                if h < 4:
                    split_lo(dve, UNIT["q"] + h + 4)
            head_steps(4, 9, qT, vec("q_norm"))
            head_steps(4, 11, qT, vec("q_norm"))
            scores_max(0, 0, ws1)
            scores_max(1, 1, ws1)
            normalise(0, 0, ws1)
            for g in range(4):
                if g + 1 < 4:
                    normalise(g + 1, g + 1, ws1)
                if g + 2 < 4:
                    scores_max(g + 2, g + 2, ws1)
                att_lo(g)
                split_lo(dve, UNIT["o"] + g)
            gate_coef(5, 128, 1.0)
            for k in range(KT):
                wait_tile(dve, TILE["o"] + k)
                update(k, tiles[:, k % 2, 0:T], 5, freed["d"])
                split_lo(dve, UNIT["o"] + 4 + k)
            norm_coef(6)
            root(5)
            norm_t(6)
            ffn(3, 6, 4, 152, rng("lat", 0, 4))

            next_unit = [UNIT["lat"] + 4]

            def ahead(n=1):
                for _ in range(n):
                    if next_unit[0] < N_UNITS:
                        split_lo(dve, next_unit[0])
                        next_unit[0] += 1

            def a_part(k, src, ah, signal):
                dve.wait_ge(ah_done, ah)
                V.tensor_tensor(a_lo[:, k], src, a_hi[:, k].bitcast(F32), ALU.subtract).then_inc(signal, 1)

            norm_coef(7)
            root(6)
            norm_t(7)
            ahead(5)
            R = slice(64, 96)
            for n in range(KT):
                ahead()
                if n == 2:
                    dve.wait_ge(lrt_done, 1)
                    link(V.reciprocal(rh[:], rh[:]))
                    for k in range(4):
                        V.scalar_tensor_tensor(out=lat_n[:, k], in0=lat_raw[:, k],
                                               scalar=vec("g_q", k) if k < 2 else vec("g_kv", k - 2),
                                               in1=rh[:, (k // 2) * T:(k // 2 + 1) * T], op0=ALU.mult,
                                               op1=ALU.mult).then_inc(af_done, 1)
                if n == 4:
                    dve.wait_ge(krot_done, 1)
                    dve.wait_ge(sin_done, 2)
                    V.tensor_tensor(kr_buf[R, 1], kr_buf[R, 0], rope2[R, 0], ALU.mult)
                    link(V.tensor_tensor(kr_buf[R, 2], acc4[R, 2, 0:T], rope2[R, 1], ALU.mult))
                    V.tensor_tensor(kr_buf[R, 1], kr_buf[R, 1], kr_buf[R, 2], ALU.add).then_inc(kr_done, 1)
                    dve.wait_ge(af_done, 4)
                    for k in range(4):
                        a_part(k, lat_n[:, k], 8 + k + 1, al_done)
            for n in range(4):
                ahead()

            def q_rope(g):
                pair = q2[0:QK_2, 2 * g:2 * g + 2]
                c2, s2 = (rope2[:, n].unsqueeze(1).to_broadcast([QK_2, 2, T]) for n in range(2))
                if g:
                    dve.wait_ge(qrope_done, g)
                dve.wait_ge(qrot_done, g + 1)
                V.tensor_tensor(rope_t[0:QK_2, 0], pair, c2, ALU.mult)
                rotated = acc4[0:QK_2, 2 + g % 2].rearrange("p (h t) -> p h t", h=2)
                link(V.tensor_tensor(rope_t[0:QK_2, 1], rotated, s2, ALU.mult))
                V.tensor_tensor(pair, rope_t[0:QK_2, 0], rope_t[0:QK_2, 1], ALU.add).then_inc(qrope_done, 1)

            for n in range(4):
                ahead()
                q_rope(2 * n)
                q_rope(2 * n + 1)

            def att2_out(g):
                wait_tile(dve, att2_tile(g))
                V.tensor_copy(ym[:, g], tiles[:, att2_tile(g) % 2, 0:T]).then_inc(freed["d"], 1)

            dve.wait_ge(mask_in, 16)
            scores_max(4, 0, ws2)
            scores_max(5, 1, ws2)
            normalise(4, 0, ws2)
            for g in range(8):
                if g + 1 < 8:
                    normalise(5 + g, g + 1, ws2)
                if g + 2 < 8:
                    scores_max(6 + g, g + 2, ws2)
                att2_out(g)
                if g:
                    ahead()
            wait_freed(dve, att2_tile(7))
            dve.wait_ge(zm_done, 1)
            for n in range(KT):
                V.tensor_tensor(t_buf[:, n], ym[:, n], zm[:, n], ALU.mult).then_inc(af_done, 1)

            dve.wait_ge(af_done, 4 + KT)
            def ssm_step(s):
                f, jj = s // 2, 2 * (s % 2)
                cs, sn = rot_t[s % 2][:, 0], rot_t[s % 2][:, 1]
                v, (m0, m1) = ssm_v[s % 2], ssm_m[s % 2]
                bur, bui = acc4[:, jj:jj + 2, 0:T], acc4[:, jj:jj + 2, T:2 * T]
                dve.wait_ge(tab_done, s + 1)
                dve.wait_ge(bu_done, s + 1)
                if s >= 2:
                    dve.wait_ge(y_done, s - 1)
                V.tensor_tensor(v[:, 0], bur, cs, ALU.mult)
                V.tensor_tensor(m0, bui, sn, ALU.mult)
                V.tensor_tensor(v[:, 1], bui, cs, ALU.mult)
                link(V.tensor_tensor(m1, bur, sn, ALU.mult))
                V.tensor_tensor(v[:, 0], v[:, 0], m0, ALU.add).then_inc(bu_free, 1)
                link(V.tensor_tensor(v[:, 1], v[:, 1], m1, ALU.subtract))
                for c in range(2):
                    for j in range(2):
                        mag = ssm_s[:, 1, 4 * f + jj + j:4 * f + jj + j + 1].to_broadcast([P, T])
                        m = V.tensor_tensor_scan(v[:, c, j], mag, v[:, c, j], 0.0, ALU.mult, ALU.add)
                    if c == 0:
                        m.then_inc(vs_done, 1)
                link(m)
                link(V.scalar_tensor_tensor(out=m0, in0=v[:, 1], scalar=-1.0, in1=sn, op0=ALU.mult, op1=ALU.mult))
                V.tensor_tensor(v[:, 1], v[:, 1], cs, ALU.mult).then_inc(zz_done, 1)

            def y_tile(f):
                dve.wait_ge(y_done, 2 * f + 2)
                V.scalar_tensor_tensor(out=gel[:, f], in0=uT[:, f], scalar=vec("ssm_d", f),
                                       in1=nrm[:, (f % 2) * T:(f % 2 + 1) * T], op0=ALU.mult,
                                       op1=ALU.add).then_inc(yp_done, 1)

            for s in range(16):
                ssm_step(s)
                if s == 0:
                    ahead()
                    for n in range(KT):
                        a_part(n, t_buf[:, n], 13 + n, al_done)
                for nm, n in GATES[2 * s:2 * s + 2]:
                    ahead()
                    if nm == "brm":
                        wait_tile(dve, TILE["brm"] + n)
                        wait_freed(dve, TILE["glm"] + n)
                        V.tensor_tensor(mrg[:, n], tiles[:, (TILE["brm"] + n) % 2, 0:T], mrg[:, n],
                                        ALU.mult).then_inc(freed["d"], 1)
                if s >= 2 and s % 2 == 0:
                    y_tile(s // 2 - 1)
                if s == 11:
                    for f in range(4):
                        a_part(f, gel[:, f], 20 + f + 1, al_done)
            y_tile(7)
            for f in range(4, 8):
                a_part(f, gel[:, f], 20 + f + 1, al_done)
            for n in range(KT):
                wait_tile(dve, TILE["glu"] + 2 * n + 1)
                wait_freed(dve, TILE["glu"] + 2 * n)
                V.scalar_tensor_tensor(out=gel[:, n], in0=tiles[:, (TILE["glu"] + 2 * n + 1) % 2, 0:T],
                                       scalar=vec("b_glu", n), in1=sig_t[:, n % 2], op0=ALU.add,
                                       op1=ALU.mult).then_inc(freed["d"], 1)
                wait_freed(dve, TILE["glu"] + 2 * n + 1)
                V.tensor_tensor(gel[:, n], gel[:, n], zs_t[:, n], ALU.mult).then_inc(gv_done, 1)
                ahead(2)
                if n:
                    dve.wait_ge(xh_done, KT * N_STAGES + n)
                    V.tensor_tensor(x_lo[:, n - 1], gel[:, n - 1], x_hi[:, n - 1].bitcast(F32),
                                    ALU.subtract).then_inc(xl_done, 1)
            dve.wait_ge(xh_done, KT * N_STAGES + KT)
            V.tensor_tensor(x_lo[:, 7], gel[:, 7], x_hi[:, 7].bitcast(F32), ALU.subtract).then_inc(xl_done, 1)
            for n in range(KT):
                wait_tile(dve, TILE["brs"] + n)
                V.tensor_tensor(gel[:, n], tiles[:, (TILE["brs"] + n) % 2, 0:T], gs_t[:, n],
                                ALU.mult).then_inc(freed["d"], 1)
                wait_freed(dve, TILE["brs"] + n)
                V.tensor_tensor(mrg[:, n], mrg[:, n], gel[:, n], ALU.add).then_inc(af_done, 1)
                ahead()
                if n:
                    a_part(n - 1, mrg[:, n - 1], 28 + n, al_done)
            a_part(7, mrg[:, 7], 36, al_done)
            ahead(KT)
            dve.wait_ge(g_red, N_G)
            link(V.tensor_tensor(coef[:, 8, 24:32], mods[:, 176:184], vec("bias", 176, 8), ALU.add))
            link(V.tensor_tensor(coef[:, 8, 0:8], coef[:, 8, 24:32], vec("g_post", 0, 8), ALU.mult))
            root(7)
            for k in range(KT):
                V.scalar_tensor_tensor(out=t_buf[:, k], in0=o_raw[:, k], scalar=coef[:, 8, k:k + 1], in1=rx,
                                       op0=ALU.mult, op1=ALU.mult).then_inc(t_done, 1)
                if k:
                    dve.wait_ge(t_done, KT * N_STAGES + k)
                    V.tensor_tensor(x[:, k - 1], x[:, k - 1], t_buf[:, k - 1], ALU.add).then_inc(fin_done, 1)
            dve.wait_ge(t_done, KT * N_STAGES + KT)
            V.tensor_tensor(x[:, 7], x[:, 7], t_buf[:, 7], ALU.add).then_inc(fin_done, 1)

        @block.gpsimd
        def _(pool):
            chain = [0]
            G = nc.gpsimd

            def link(ins):
                chain[0] += 1
                ins.then_inc(pool_s, 1)
                pool.wait_ge(pool_s, chain[0])

            def cmul(out_, a, b, tmp, last=None):
                (ar, ai), (br, bi) = a, b
                link(G.tensor_tensor(out_[0], ar, br, ALU.mult))
                link(G.tensor_tensor(tmp, ai, bi, ALU.mult))
                link(G.tensor_tensor(out_[0], out_[0], tmp, ALU.subtract))
                link(G.tensor_tensor(out_[1], ar, bi, ALU.mult))
                link(G.tensor_tensor(tmp, ai, br, ALU.mult))
                m = G.tensor_tensor(out_[1], out_[1], tmp, ALU.add)
                if last is None:
                    link(m)
                else:
                    m.then_inc(last, 1)

            def reduce_angle(th, out_s, out_c, tmp, tmp2, tmp3):
                for out_, quarter in ((out_s, 0.0), (out_c, 0.25)):
                    link(G.tensor_scalar(tmp, th, 1.0 / TWO_PI, quarter, ALU.mult, ALU.add))
                    link(G.tensor_scalar(tmp, tmp, 12582912.0, None, ALU.add))
                    link(G.tensor_scalar(tmp, tmp, -12582912.0, None, ALU.add))
                    a = th
                    for part in (-6.28125, -0.0019350051879882812, -(TWO_PI - 6.28125 - 0.0019350051879882812)):
                        link(G.tensor_scalar(tmp3, tmp, part, None, ALU.mult))
                        link(G.tensor_tensor(tmp2, a, tmp3, ALU.add))
                        a = tmp2
                    link(G.tensor_scalar(tmp2, tmp2, quarter * TWO_PI, 3.1415925, ALU.add, ALU.min))
                    link(G.tensor_scalar(out_, tmp2, -3.1415925, None, ALU.max))

            S = lambda n: ssm_s[:, n]
            lr, li = vec("lr", 0, 32), vec("li", 0, 32)
            pool.wait_ge(vec_in, 16)
            pool.wait_ge(act_s, 1)
            G.tensor_tensor(S(2), lr, S(0), ALU.mult).then_inc(ang_done, 1)
            link(G.tensor_tensor(S(7), li, S(0), ALU.mult))
            reduce_angle(S(7), S(4), S(3), S(8), S(9), S(15))
            G.tensor_copy(S(19), S(8)).then_inc(ang_done, 1)
            pool.wait_ge(act_s, 2)
            pool.wait_ge(sin_done, 1)
            link(G.tensor_tensor(S(10), S(1), S(5), ALU.mult))
            link(G.tensor_scalar(S(10), S(10), -1.0, None, ALU.add))
            link(G.tensor_tensor(S(11), S(1), S(6), ALU.mult))
            link(G.tensor_tensor(S(12), lr, lr, ALU.mult))
            link(G.tensor_tensor(S(13), li, li, ALU.mult))
            G.tensor_tensor(S(12), S(12), S(13), ALU.add).then_inc(den_done, 1)
            pool.wait_ge(den_done, 2)
            link(G.tensor_tensor(S(13), S(10), lr, ALU.mult))
            link(G.tensor_tensor(S(14), S(11), li, ALU.mult))
            link(G.tensor_tensor(S(13), S(13), S(14), ALU.add))
            link(G.tensor_tensor(S(13), S(13), S(12), ALU.mult))
            link(G.tensor_tensor(S(14), S(11), lr, ALU.mult))
            link(G.tensor_tensor(S(15), S(10), li, ALU.mult))
            link(G.tensor_tensor(S(14), S(14), S(15), ALU.subtract))
            link(G.tensor_tensor(S(14), S(14), S(12), ALU.mult))
            p, spare = ssm_s[:, 5:7], [ssm_s[:, 16:18], ssm_s[:, 8:10]]
            tmp = region(40, [32, 16])
            step = 0
            for table, n in ((base_t, CH), (chunk_t, NCH)):
                link(G.memset(table[:, 0, :, 0:1], 1.0))
                link(G.memset(table[:, 1, :, 0:1], 0.0))
                w = 1
                while w < n:
                    cmul([table[:, c, :, w:2 * w] for c in range(2)], [table[:, c, :, 0:w] for c in range(2)],
                         [p[:, c].unsqueeze(2).to_broadcast([P, 32, w]) for c in range(2)], tmp[:, :, 0:w])
                    q = spare[step % 2]
                    power = [p[:, 0], p[:, 1]]
                    cmul([q[:, 0], q[:, 1]], power, power, tmp[:, 0:2].rearrange("p a b -> p (a b)"))
                    p, w, step = q, 2 * w, step + 1
            link(G.memset(win_h[:, :, 0:PAD], 0.0))
            link(G.memset(win_a[:, :, 0:PAD], 0.0))
            G.memset(win_b[:, :, 0:PAD], 0.0).then_inc(base_done, 1)
            pool.wait_ge(base_done, 1)
            R = slice(64, 96)
            pool.wait_ge(pos_in, 16)
            pool.wait_ge(con_in, 16)
            link(G.tensor_copy(tmp_a[R], pos_i[R].bitcast(I32)))
            link(G.tensor_scalar(theta[R], tmp_a[R], con("invf", 1)[R], None, ALU.mult))
            reduce_angle(theta[R], ang[R, 1], ang[R, 0], tmp_a[R], tmp_b[R], pos_i[R])
            link(G.memset(rope2[0:64, 0], 1.0))
            link(G.memset(rope2[0:64, 1], 0.0))
            G.tensor_copy(tmp_b[R], tmp_a[R]).then_inc(ang_done, 1)
            pool.wait_ge(ang_done, 3)
            src, dst = win_h[:, 6:8], win_a[:, 6:8]
            pool.wait_ge(ph_done, 2)
            for level in range(4):
                sh = 1 << level
                link(G.tensor_tensor(dst[:, :, PAD:], src[:, :, PAD:], src[:, :, PAD - sh:PAD + T - sh], ALU.add))
                src, dst = dst, (win_b[:, 4:6] if level % 2 == 0 else win_a[:, 6:8])
            h2, t2 = win_h[:, 6:8], t_buf[:, 6:8]
            link(G.tensor_scalar(t2, src[:, :, PAD:], 1.0 / 16, None, ALU.mult))
            cnt = cons[:, CON["cnt"] + 48:CON["cnt"] + 64].unsqueeze(1).to_broadcast([P, 2, 16])
            link(G.tensor_tensor(t2[:, :, 0:16], src[:, :, PAD:PAD + 16], cnt, ALU.mult))
            link(G.tensor_tensor(t2[:, :, 16:], t2[:, :, 16:], h2[:, :, PAD + 16:], ALU.subtract))
            pool.wait_ge(t_done, KT + 6)
            G.tensor_tensor(t2[:, :, 0:16], t2[:, :, 0:16], h2[:, :, PAD:PAD + 16],
                                ALU.subtract).then_inc(t_done, 2)
            for n in range(8):
                pool.wait_ge(kn_done, n + 1)
                if n:
                    pool.wait_ge(rope_done, n)
                G.tensor_tensor(rope_t[:, 0], rope_kn, cos1.unsqueeze(1).to_broadcast([P, 2, T]),
                                ALU.mult).then_inc(hcos_done, 1)
            pool.wait_ge(hcos_done, 8)
            pool.wait_ge(kr_done, 1)
            G.tensor_copy(k2[64:96], kr_buf[64:96, 1].unsqueeze(1).to_broadcast([32, HEADS_2, T])).then_inc(kb_done, 1)
            pool.wait_ge(c_in, 16)
            for half in (slice(0, 16), slice(16, 32)):
                fr, fi = (ssm_s[:, n, half].unsqueeze(2).to_broadcast([P, 16, 32]) for n in (13, 14))
                tmp = rh[:].rearrange("p (a b) -> p a b", b=32)
                re, im, cr, ci = c_raw[:, 0, half], c_raw[:, 1, half], cc[:, 0, half], cc[:, 1, half]
                link(G.tensor_tensor(cr, re, fr, ALU.mult))
                link(G.tensor_tensor(tmp, im, fi, ALU.mult))
                link(G.tensor_tensor(cr, cr, tmp, ALU.subtract))
                link(G.tensor_tensor(ci, re, fi, ALU.mult))
                link(G.tensor_tensor(tmp, im, fr, ALU.mult))
                link(G.tensor_tensor(ci, ci, tmp, ALU.add))
                m = G.tensor_scalar(ci, ci, -1.0, None, ALU.mult)
                if half.start:
                    m.then_inc(cc_done, 1)
                else:
                    link(m)
            pool.wait_ge(cc_done, 1)

            def table_step(s):
                j = 2 * s
                if s >= 2:
                    pool.wait_ge(zz_done, s - 1)
                a = [base_t[:, c, j:j + 2].unsqueeze(2).to_broadcast([P, 2, NCH, CH]) for c in range(2)]
                b = [chunk_t[:, c, j:j + 2].unsqueeze(3).to_broadcast([P, 2, NCH, CH]) for c in range(2)]
                o = [rot_t[s % 2][:, c].rearrange("p j (a b) -> p j a b", b=CH) for c in range(2)]
                cmul(o, a, b, rh[:].rearrange("p (j a b) -> p j a b", j=2, b=CH), tab_done)

            table_step(0)
            pool.wait_ge(tab_done, 1)
            table_step(1)
            for s in range(16):
                v, m1 = ssm_v[s % 2], ssm_m[s % 2][1]
                pool.wait_ge(vs_done, s + 1)
                link(G.tensor_tensor(m1, v[:, 0], rot_t[s % 2][:, 1], ALU.mult))
                G.tensor_tensor(v[:, 0], v[:, 0], rot_t[s % 2][:, 0], ALU.mult).then_inc(zp_done, 1)
                if s + 2 < 16:
                    pool.wait_ge(zp_done, s + 1)
                    table_step(s + 2)
                    pool.wait_ge(tab_done, s + 3)


def columns(w):
    k, n = w.shape
    return w.reshape(k // P, P, n // P, P).transpose(2, 1, 0, 3).reshape(n // P, P, -1)


def padded(a):
    return np.pad(a, ((0, 0), (0, 0), (0, WIDTH - a.shape[2])))


def ffn_units(w_in, w_out):
    gate_up, rows = columns(w_in), w_out.reshape(FFN_TILES, P, D)
    out = np.empty((66, P, WIDTH), w_in.dtype)
    for j in range(FFN_TILES):
        out[g_unit(0, j)] = gate_up[j]
        out[g_unit(0, j) + 1] = gate_up[FFN_TILES + j]
        out[o_unit(0, j)] = rows[j]
    return out


def tiled(v):
    return np.asarray(v).reshape(-1, P).T


def constants():
    c = np.zeros((P, NC_), np.float32)
    put = lambda name, a: c.__setitem__((slice(0, a.shape[0]), slice(CON[name], CON[name] + a.shape[1])), a)
    put("ident", np.eye(P, dtype=np.float32))
    put("ones", np.ones((P, P), np.float32))
    for name, first, half in (("rot1", 0, 64), ("rot2", 64, 16)):
        m = np.zeros((P, P if name == "rot1" else QK_2), np.float32)
        for i in range(half):
            m[first + half + i, first + i] = -1.0
            m[first + i, first + half + i] = 1.0
        put(name, m[:m.shape[1]] if name == "rot2" else m)
    pos = np.arange(T, dtype=np.float32)
    inv = (10000.0 ** (-np.arange(0, HEAD_DIM, 2, dtype=np.float32) / HEAD_DIM)).astype(np.float32)
    ang = (inv[:, None] * pos[None, :]).astype(np.float32)
    put("cos1", np.tile(np.cos(ang), (2, 1)).astype(np.float32))
    put("sin1", np.tile(np.sin(ang), (2, 1)).astype(np.float32))
    q = np.arange(P)[:, None, None] + P * np.arange(2)[None, :, None]
    k = np.arange(T)[None, None, :]
    put("mask", np.where(k <= q, 0.0, -1e30).astype(np.float32).reshape(P, 2 * T))
    mask2 = np.where(k // 64 <= q // 64, 0.0, -1e30).astype(np.float32).reshape(P, 2 * T)
    t = np.arange(PAD)
    put("cnt", np.tile(np.concatenate([1.0 / np.minimum(t + 1, w) for w in POOL_W]).astype(np.float32), (P, 1)))
    inv2 = (10000.0 ** (-np.arange(0, 32, 2, dtype=np.float32) / 32)).astype(np.float32)
    c[64:96, CON["invf"]] = np.tile(inv2, 2)
    c[:, CON["eps"]] = EPS
    return c, mask2


def kernel(**inp):
    import concourse.bacc as bacc
    from concourse.bass_utils import run_bass_kernel_spmd

    a = {name: np.asarray(v) for name, v in inp.items()}
    w_in2 = a["w_in_2"][0]
    parts = [
        ffn_units(a["ffn_w_in"][0, 0], a["ffn_w_out"][0, 0]),
        a["pool_w"][0].reshape(2, 2, 2, P, 256).transpose(0, 3, 1, 2, 4).reshape(2, P, WIDTH),
        ffn_units(a["ffn_w_in"][0, 1], a["ffn_w_out"][0, 1]),
        columns(a["w_kv"][:, :D]), a["w_kv"][:, D:].reshape(KT, P, D),
        ffn_units(a["ffn_w_in"][1, 0], a["ffn_w_out"][1, 0]),
        columns(a["w_q"][0]), columns(a["w_o"][0]),
        ffn_units(a["ffn_w_in"][1, 1], a["ffn_w_out"][1, 1]),
        columns(w_in2[:, 2048:2560]),
        padded(np.pad(w_in2[:, 2560:2592], ((0, 0), (64, 0))).reshape(KT, P, QK_2).transpose(1, 0, 2).reshape(1, P, -1)),
        columns(w_in2[:, 0:1024]),
        padded(a["w_q_up_2"][0].reshape(2, P, 4, 384).transpose(2, 1, 0, 3).reshape(4, P, -1)),
        a["w_kv_up_2"][0].reshape(2, P, 4, 512).transpose(2, 1, 0, 3).reshape(4, P, -1),
        columns(w_in2[:, 2592:3616]),
        columns(w_in2[:, 4640:5664]),
        columns(a["w_br_mla_2"][0]),
        columns(w_in2[:, 1024:2048]),
        columns(w_in2[:, 3616:4640]),
        columns(a["w_glu_2"][0]).reshape(2, KT, P, WIDTH)[::-1].transpose(1, 0, 2, 3).reshape(16, P, WIDTH),
        columns(a["w_br_ssm_2"][0]),
        columns(a["w_out_2"][0]),
    ]
    stream = np.concatenate(parts)
    blocks = lambda w: w.reshape(8, P, -1, GW).transpose(2, 1, 0, 3)
    gstream = np.concatenate([blocks(a["ada_w"][0]), blocks(a["kv_ada_w"]), blocks(a["ada_w"][1]),
                              blocks(a["w_ada_2"][0])])
    bias = np.concatenate([a["ada_b"][0], a["kv_ada_b"], a["ada_b"][1], a["b_ada_2"][0]])
    states = lambda v: v.reshape(32, P).T
    vecs = np.concatenate([
        tiled(a["c"]), tiled(a["c_2"]), states(np.repeat(a["ssm_log_dt_2"][0], 64)), states(a["ssm_a_re_2"][0]),
        states(a["ssm_a_im_2"][0]), tiled(bias), tiled(a["norm_g"]), tiled(a["pool_scale"]), tiled(a["kv_norm"]),
        tiled(a["k_norm"]), tiled(a["q_norm"]), tiled(a["g_pre_2"]), tiled(a["ssm_d_2"]), tiled(a["b_glu_2"]),
        tiled(a["g_q_norm_2"]), tiled(a["g_kv_norm_2"]), tiled(a["g_post_2"])], axis=1)
    ssm_b = np.zeros((2, KT, 4, 2, 16, 2, 64), np.float32)
    ssm_c = np.zeros((2, 32, 2, 64, 2, 16), np.float32)
    for c, part in enumerate(("re", "im")):
        b = a[f"ssm_b_{part}_2"][0].reshape(KT, 4, 2, 64, 16)
        cc = a[f"ssm_c_{part}_2"][0].reshape(32, 2, 16, 64)
        for g in range(2):
            ssm_b[c, :, :, g, :, g, :] = b[:, :, g].transpose(0, 1, 3, 2)
            ssm_c[c, :, g, :, g, :] = cc[:, g].transpose(0, 2, 1)
    ssm_b = ssm_b.transpose(2, 3, 4, 0, 1, 5, 6).reshape(P, 2, KT, P)
    ssm_c = ssm_c.transpose(2, 3, 0, 1, 4, 5).reshape(P, 2, 32, 32)
    cons, mask2 = constants()
    arrays = {
        "stream": stream, "gstream": gstream, "vecs": vecs, "cons": cons, "mask2": mask2,
        "x_t": a["x"][0].T.reshape(KT, P, T).transpose(1, 0, 2),
        "pos": np.tile(a["positions_2"], (32, 1)).astype(np.int32), "ssm_b": ssm_b, "ssm_c": ssm_c,
    }
    arrays = {name: np.ascontiguousarray(v) for name, v in arrays.items()}
    nc = bacc.Bacc("TRN2", target_bir_lowering=False, num_devices=1)
    args = [nc.dram_tensor(f"in_{name}", v.shape, mybir.dt.from_np(v.dtype), kind="ExternalInput").ap()
            for name, v in arrays.items()]
    out = nc.dram_tensor("out_t", (P, KT, T), F32, kind="ExternalOutput").ap()
    build_program(nc, *args, out)
    r = run_bass_kernel_spmd(nc, [{f"in_{name}": v for name, v in arrays.items()}], core_ids=[0])
    return r.results[0]["out_t"].transpose(1, 0, 2).reshape(D, T).T.reshape(1, T, D)
```
